# Optimizing a Trainium2 kernel written in Bass

```python
import jax, jax.numpy as jnp
from jax import lax
import numpy as np

D_MODEL = 1024
BATCH = 1
SEQ = 1024
DEPTH = 1
DEC_BATCH = 8
DEC_SEQ = 16
PAST_LEN = 512

CHUNK = 64
H_M = 4
DH_M = 256
W_M = H_M * DH_M
H_F = 16
DH_F = 64
W_F = H_F * DH_F
Q_BLOCK = 128
D_PLE = 256
PEER_HEADS = 8
PEER_KEYS = 128
PEER_N = PEER_KEYS * PEER_KEYS
PEER_DQ = 256
PEER_TOPK = 16
PEER_BLOCK = 128
EPS = 1e-6
_IN_SIZES = (W_M, W_M, W_M, W_M, H_M, H_M, W_F, W_F, W_F, H_F, D_MODEL, D_MODEL)
IN_COLS = sum(_IN_SIZES)

kernel_name = 'hybrid_mlstm_fox_peer_stream_step'

def rmsnorm(x, g):
    xf = x.astype(jnp.float32)
    y = xf * lax.rsqrt(jnp.mean(xf * xf, axis=-1, keepdims=True) + EPS)
    return (y * g.astype(jnp.float32)).astype(x.dtype)

def split_cols(z):
    offs = []
    acc = 0
    for s in _IN_SIZES[:-1]:
        acc += s
        offs.append(acc)
    return jnp.split(z, offs, axis=-1)

def mlstm_chunkwise(q, k, v, i_pre, log_f, C0, n0, m0):
    f32 = jnp.float32
    B, T = q.shape[0], q.shape[1]
    L = min(CHUNK, T)
    nc = T // L

    def to_chunks(z):
        return jnp.moveaxis(z.reshape((B, nc, L) + z.shape[2:]), 1, 0)

    xs = (to_chunks(q.astype(f32)), to_chunks(k.astype(f32) * DH_M ** -0.5), to_chunks(v.astype(f32)),
          to_chunks(i_pre.astype(f32)), to_chunks(log_f.astype(f32)))
    tril = jnp.tril(jnp.ones((L, L), dtype=bool))

    def step(carry, inp):
        C, n, m = carry
        qc, kc, vc, ic, fc = inp
        ic = jnp.swapaxes(ic, 1, 2)
        b = jnp.cumsum(jnp.swapaxes(fc, 1, 2), axis=-1)
        D = jnp.where(tril, b[..., :, None] - b[..., None, :] + ic[..., None, :], -jnp.inf)
        g = b + m[..., None]
        mt = jnp.maximum(g, jnp.max(D, axis=-1))
        wD = jnp.exp(D - mt[..., None])
        wg = jnp.exp(g - mt)
        qk = jnp.einsum('blhd,bshd->bhls', qc, kc) * wD
        num = wg[..., None] * jnp.einsum('blhd,bhde->bhle', qc, C) + jnp.einsum('bhls,bshe->bhle', qk, vc)
        dot = wg * jnp.einsum('blhd,bhd->bhl', qc, n) + jnp.sum(qk, axis=-1)
        h = num / jnp.maximum(jnp.abs(dot), jnp.exp(-mt))[..., None]
        m_new = mt[..., -1]
        wC = jnp.exp(b[..., -1] + m - m_new)
        ws = jnp.exp(b[..., -1:] - b + ic - m_new[..., None])
        C_new = wC[..., None, None] * C + jnp.einsum('bhs,bshd,bshe->bhde', ws, kc, vc)
        n_new = wC[..., None] * n + jnp.einsum('bhs,bshd->bhd', ws, kc)
        return (C_new, n_new, m_new), jnp.swapaxes(h, 1, 2)

    (C, n, m), hs = lax.scan(step, (C0.astype(f32), n0.astype(f32), m0.astype(f32)), xs)
    h = jnp.moveaxis(hs, 0, 1).reshape(B, T, H_M, DH_M)
    return h.astype(q.dtype), C.astype(C0.dtype), n.astype(n0.dtype), m.astype(m0.dtype)

def fox_block(qb, cq, q_pos, k, v, ck, k_pos):
    s = jnp.einsum('bqhd,bshd->bhqs', qb.astype(jnp.float32), k) * DH_F ** -0.5
    s = s + jnp.swapaxes(cq, 1, 2)[..., :, None] - jnp.swapaxes(ck, 1, 2)[..., None, :]
    s = jnp.where(k_pos[None, :] <= q_pos[:, None], s, -jnp.inf)
    p = jax.nn.softmax(s, axis=-1)
    return jnp.einsum('bhqs,bshd->bqhd', p, v).astype(qb.dtype)

def peer(x, w_q, keys1, keys2, u_tab, v_tab):
    shp = x.shape
    xt = x.reshape(-1, D_MODEL)
    n = xt.shape[0]
    pad = (-n) % PEER_BLOCK
    blocks = jnp.pad(xt, ((0, pad), (0, 0))).reshape(-1, PEER_BLOCK, D_MODEL)
    half = PEER_DQ // 2
    k1 = keys1.astype(jnp.float32)
    k2 = keys2.astype(jnp.float32)

    def one(xb):
        q = (xb @ w_q).reshape(PEER_BLOCK, PEER_HEADS, PEER_DQ).astype(jnp.float32)
        s1 = jnp.einsum('thd,hkd->thk', q[..., :half], k1)
        s2 = jnp.einsum('thd,hkd->thk', q[..., half:], k2)
        v1, i1 = lax.top_k(s1, PEER_TOPK)
        v2, i2 = lax.top_k(s2, PEER_TOPK)
        cand = (v1[..., :, None] + v2[..., None, :]).reshape(PEER_BLOCK, PEER_HEADS, PEER_TOPK * PEER_TOPK)
        sc, j = lax.top_k(cand, PEER_TOPK)
        idx = (jnp.take_along_axis(i1, j // PEER_TOPK, axis=-1) * PEER_KEYS
               + jnp.take_along_axis(i2, j % PEER_TOPK, axis=-1))
        g = jax.nn.softmax(sc, axis=-1)
        act = jax.nn.gelu(jnp.einsum('thkd,td->thk', u_tab[idx], xb).astype(jnp.float32), approximate=False)
        return jnp.einsum('thk,thkd->td', (g * act).astype(xb.dtype), v_tab[idx])

    out = lax.map(one, blocks).reshape(-1, D_MODEL)[:n]
    return out.reshape(shp).astype(x.dtype)

def trunk_layer(h, p, lw, mstate, fox_cache):
    f32 = jnp.float32
    B, T = h.shape[0], h.shape[1]
    a = rmsnorm(h, lw['norm_mix'])
    z = a @ lw['w_in']
    qm, km, vm, om, im, fm, qf, kf, vf, ff, gm, gf = split_cols(z)
    i_pre = im.astype(f32) + lw['mlstm_b_i'].astype(f32)
    log_fm = jax.nn.log_sigmoid(fm.astype(f32) + lw['mlstm_b_f'].astype(f32))
    y_m, C, n, m = mlstm_chunkwise(qm.reshape(B, T, H_M, DH_M), km.reshape(B, T, H_M, DH_M),
                                   vm.reshape(B, T, H_M, DH_M), i_pre, log_fm, mstate[0], mstate[1], mstate[2])
    y_m = jax.nn.sigmoid(om) * y_m.reshape(B, T, W_M)
    log_ff = jax.nn.log_sigmoid(ff.astype(f32) + lw['fox_b_f'].astype(f32))
    q = qf.reshape(B, T, H_F, DH_F)
    k = kf.reshape(B, T, H_F, DH_F)
    v = vf.reshape(B, T, H_F, DH_F)
    if fox_cache is None:
        c = jnp.cumsum(log_ff, axis=1)
        k32, v32 = k.astype(f32), v.astype(f32)
        kpos = jnp.arange(T)
        nb = T // Q_BLOCK
        qs = jnp.moveaxis(q.reshape(B, nb, Q_BLOCK, H_F, DH_F), 1, 0)
        cs = jnp.moveaxis(c.reshape(B, nb, Q_BLOCK, H_F), 1, 0)
        ps = kpos.reshape(nb, Q_BLOCK)
        yb = lax.map(lambda t: fox_block(t[0], t[1], t[2], k32, v32, c, kpos), (qs, cs, ps))
        y_f = jnp.moveaxis(yb, 0, 1).reshape(B, T, W_F)
    else:
        ck, cv, clf = fox_cache
        P = ck.shape[1]
        k_all = jnp.concatenate([ck.astype(f32), k.astype(f32)], axis=1)
        v_all = jnp.concatenate([cv.astype(f32), v.astype(f32)], axis=1)
        c_all = jnp.cumsum(jnp.concatenate([clf.astype(f32), log_ff], axis=1), axis=1)
        y_f = fox_block(q, c_all[:, P:], P + jnp.arange(T), k_all, v_all, c_all, jnp.arange(P + T))
        y_f = y_f.reshape(B, T, W_F)
    merge = jax.nn.sigmoid(gm) * (y_m @ lw['w_br_m']) + jax.nn.sigmoid(gf) * (y_f @ lw['w_br_f'])
    h = h + merge @ lw['w_out']
    h = h + peer(rmsnorm(h, lw['norm_ffn']), lw['peer_w_q'], lw['peer_keys1'], lw['peer_keys2'],
                 lw['peer_u'], lw['peer_v'])
    e = rmsnorm(h, lw['norm_ple'])
    h = h + jax.nn.sigmoid(e @ lw['w_ple_gate']) * (p @ lw['w_ple_proj'])
    return h, (k, v, log_ff.astype(h.dtype), C, n, m)

def setup_inputs(seed: int = 0) -> dict:
    key = jax.random.key(seed)
    ks = jax.random.split(key, 32)
    nrm = lambda i, shape, s: jax.random.normal(ks[i], shape, jnp.float32) * s
    D = D_MODEL
    return {
        'x_prompt': nrm(0, (BATCH, SEQ, D), 1.0),
        'x_sample': nrm(1, (DEC_BATCH, DEC_SEQ, D), 1.0),
        'p_prompt': nrm(2, (DEPTH, BATCH, SEQ, D_PLE), 1.0),
        'p_sample': nrm(3, (DEPTH, DEC_BATCH, DEC_SEQ, D_PLE), 1.0),
        'cache_fox_k': nrm(4, (DEPTH, DEC_BATCH, PAST_LEN, H_F, DH_F), 1.0),
        'cache_fox_v': nrm(5, (DEPTH, DEC_BATCH, PAST_LEN, H_F, DH_F), 1.0),
        'cache_fox_logf': jax.nn.log_sigmoid(3.0 + nrm(6, (DEPTH, DEC_BATCH, PAST_LEN, H_F), 0.5)),
        'state_mlstm_C': nrm(7, (DEPTH, DEC_BATCH, H_M, DH_M, DH_M), 0.1),
        'state_mlstm_n': nrm(8, (DEPTH, DEC_BATCH, H_M, DH_M), 0.1),
        'state_mlstm_m': nrm(9, (DEPTH, DEC_BATCH, H_M), 1.0),
        'norm_mix': 1.0 + nrm(10, (DEPTH, D), 0.02),
        'w_in': nrm(11, (DEPTH, D, IN_COLS), D ** -0.5),
        'mlstm_b_i': nrm(12, (DEPTH, H_M), 0.1),
        'mlstm_b_f': 3.0 + nrm(13, (DEPTH, H_M), 0.5),
        'fox_b_f': 3.0 + nrm(14, (DEPTH, H_F), 0.5),
        'w_br_m': nrm(15, (DEPTH, W_M, D), W_M ** -0.5),
        'w_br_f': nrm(16, (DEPTH, W_F, D), W_F ** -0.5),
        'w_out': nrm(17, (DEPTH, D, D), D ** -0.5),
        'norm_ffn': 1.0 + nrm(18, (DEPTH, D), 0.02),
        'peer_w_q': nrm(19, (DEPTH, D, PEER_HEADS * PEER_DQ), D ** -0.5),
        'peer_keys1': nrm(20, (DEPTH, PEER_HEADS, PEER_KEYS, PEER_DQ // 2), (PEER_DQ // 2) ** -0.5),
        'peer_keys2': nrm(21, (DEPTH, PEER_HEADS, PEER_KEYS, PEER_DQ // 2), (PEER_DQ // 2) ** -0.5),
        'peer_u': nrm(22, (DEPTH, PEER_N, D), D ** -0.5),
        'peer_v': nrm(23, (DEPTH, PEER_N, D), PEER_HEADS ** -0.5),
        'norm_ple': 1.0 + nrm(24, (DEPTH, D), 0.02),
        'w_ple_gate': nrm(25, (DEPTH, D, D), D ** -0.5),
        'w_ple_proj': nrm(26, (DEPTH, D_PLE, D), D_PLE ** -0.5),
        'norm_final': 1.0 + nrm(27, (D,), 0.02),
    }

def reference(x_prompt, x_sample, p_prompt, p_sample, cache_fox_k, cache_fox_v, cache_fox_logf,
              state_mlstm_C, state_mlstm_n, state_mlstm_m, norm_mix, w_in, mlstm_b_i, mlstm_b_f, fox_b_f,
              w_br_m, w_br_f, w_out, norm_ffn, peer_w_q, peer_keys1, peer_keys2, peer_u, peer_v,
              norm_ple, w_ple_gate, w_ple_proj, norm_final):
    hp, hs = x_prompt, x_sample
    Bp = x_prompt.shape[0]
    new_p, new_s = [], []
    for l in range(DEPTH):
        lw = {'norm_mix': norm_mix[l], 'w_in': w_in[l], 'mlstm_b_i': mlstm_b_i[l], 'mlstm_b_f': mlstm_b_f[l],
              'fox_b_f': fox_b_f[l], 'w_br_m': w_br_m[l], 'w_br_f': w_br_f[l], 'w_out': w_out[l],
              'norm_ffn': norm_ffn[l], 'peer_w_q': peer_w_q[l], 'peer_keys1': peer_keys1[l],
              'peer_keys2': peer_keys2[l], 'peer_u': peer_u[l], 'peer_v': peer_v[l], 'norm_ple': norm_ple[l],
              'w_ple_gate': w_ple_gate[l], 'w_ple_proj': w_ple_proj[l]}
        m0 = (jnp.zeros((Bp, H_M, DH_M, DH_M), jnp.float32), jnp.zeros((Bp, H_M, DH_M), jnp.float32),
              jnp.zeros((Bp, H_M), jnp.float32))
        hp, sp = trunk_layer(hp, p_prompt[l], lw, m0, None)
        hs, ss = trunk_layer(hs, p_sample[l], lw, (state_mlstm_C[l], state_mlstm_n[l], state_mlstm_m[l]),
                             (cache_fox_k[l], cache_fox_v[l], cache_fox_logf[l]))
        new_p.append(sp)
        new_s.append(ss)
    y_prompt = rmsnorm(hp, norm_final)
    y_sample = rmsnorm(hs, norm_final)
    fox_k_p = jnp.stack([s[0] for s in new_p])
    fox_v_p = jnp.stack([s[1] for s in new_p])
    fox_logf_p = jnp.stack([s[2] for s in new_p])
    mlstm_C_p = jnp.stack([s[3] for s in new_p])
    mlstm_n_p = jnp.stack([s[4] for s in new_p])
    mlstm_m_p = jnp.stack([s[5] for s in new_p])
    fox_k_s = jnp.stack([s[0] for s in new_s])
    fox_v_s = jnp.stack([s[1] for s in new_s])
    fox_logf_s = jnp.stack([s[2] for s in new_s])
    mlstm_C_s = jnp.stack([s[3] for s in new_s])
    mlstm_n_s = jnp.stack([s[4] for s in new_s])
    mlstm_m_s = jnp.stack([s[5] for s in new_s])
    return (y_prompt, y_sample, fox_k_p, fox_v_p, fox_logf_p, mlstm_C_p, mlstm_n_p, mlstm_m_p,
            fox_k_s, fox_v_s, fox_logf_s, mlstm_C_s, mlstm_n_s, mlstm_m_s)


_drawn_inputs = setup_inputs


def setup_inputs(seed=0):
    import zlib

    import numpy as np

    out = dict(_drawn_inputs(seed))
    spreads = {}
    factors = {'cache_fox_logf': 4.277, 'norm_ffn': 2.698, 'norm_ple': 48.406, 'norm_final': 9.698}
    for name, (base, spread) in spreads.items():
        noise = np.random.default_rng([zlib.crc32(name.encode()), seed]).standard_normal(out[name].shape)
        drawn = base * np.exp(spread * noise) if base else spread * noise
        out[name] = __import__('jax').numpy.asarray(drawn.astype(out[name].dtype))
    for name, factor in factors.items():
        out[name] = (out[name] * factor).astype(out[name].dtype)
    return out
```

```python
from contextlib import ExitStack

import concourse.bass as bass
from concourse import mybir

F32 = mybir.dt.float32
U32 = mybir.dt.uint32
ALU = mybir.AluOpType
ACT = mybir.ActivationFunctionType
AX = mybir.AxisListType

P = 128
D = 1024
KD = D // P
SEQ, NSEQ, DSEQ, PAST = 1024, 8, 16, 512
PT = SEQ // P
NT = PT + NSEQ * DSEQ // P
TOK = NT * P
H_M, DM = 4, 256
H_F, DF = 16, 64
W_M, W_F = H_M * DM, H_F * DF
PH, PKEYS, PDQ, TOPK = 8, 128, 256, 16
EPS = 1e-6
NEG = -1e30
C_QM, C_KM, C_VM, C_OM = 0, W_M, 2 * W_M, 3 * W_M
C_IM = 4 * W_M
C_QF = C_IM + 2 * H_M
C_KF, C_VF = C_QF + W_F, C_QF + 2 * W_F
C_FF = C_QF + 3 * W_F
C_GM = C_FF + H_F
C_GF = C_GM + D
IN_COLS = C_GF + D
CHUNKS = 20
CW = IN_COLS // CHUNKS
NG = 2 * H_M + H_F
EXPERTS = PH * TOPK


class Stage:

    FIRST_SEM = 160

    def __init__(self, nc, tag):
        self.nc, self.tag, self.ctx, self.held = nc, tag, ExitStack(), []

    def __enter__(self):
        self.ctx.__enter__()
        return self

    def __exit__(self, *a):
        self.ctx.__exit__(*a)
        if a[0] is None:
            self.nc.all_engine_barrier(sems_to_clear=range(self.FIRST_SEM, self.FIRST_SEM + len(self.held)))
            for s in self.held:
                self.nc.release_semaphore(s)

    def sb(self, name, shape, dt=F32):
        return self.ctx.enter_context(self.nc.sbuf_tensor(f"{self.tag}_{name}", shape, dt))

    def ps(self, name, shape):
        return self.ctx.enter_context(self.nc.psum_tensor(f"{self.tag}_psum_{name}", shape, F32))

    def sem(self, name):
        self.held.append(self.nc.alloc_semaphore(f"{self.tag}_{name}", num=self.FIRST_SEM + len(self.held)))
        return self.held[-1]

    def pool_sem(self, name):
        return self.ctx.enter_context(self.nc.semaphore(f"{self.tag}_{name}"))

    def sems(self, names):
        return [self.sem(n) for n in names.split()]


def hold(eng, sem, value, passed):
    eng.wait_ge(sem, value)
    eng.sem_inc(passed, 1)


def bc(ap, shape):
    return ap.broadcast_to(shape)


def stage_constants(nc, K):
    with Stage(nc, "const") as st:
        filled, shaped, cut, reduced = st.sems("filled shaped cut reduced")
        block = st.ctx.enter_context(nc.Block())

        @block.gpsimd
        def _(pool):
            n = 0
            for t, v in [(K["ident"], 0.0), (K["ones"], 1.0), (K["negones"], -1.0), (K["mask"], 0.0),
                         (K["maskT"], 0.0), (K["tri"], 1.0), (K["bmask"], 0.0), (K["bmaskT"], 0.0),
                         (K["btri"], 1.0), (K["last"], 0.0), (K["blast"], 0.0), (K["pick"], 0.0),
                         (K["inblock"], 1.0), (K["headsel"], 0.0), (K["onesrow"], 1.0)]:
                pool.memset(t[:], v).then_inc(filled, 1)
                n += 1
            pool.wait_ge(filled, n)

            def cut_to(t, view, pattern, base, cm, op, fill, sem):
                v = view(t)
                pool.affine_select(out=v, in_=v, compare_op=op, fill=fill, base=base, pattern=pattern,
                                   channel_multiplier=cm).then_inc(sem, 1)

            flat = lambda t: t[:]
            blocks = lambda t: t[:].rearrange("p (n j) -> p n j", n=NSEQ)
            L = DSEQ
            cut_to(K["ident"], flat, [[-1, P]], 0, 1, ALU.not_equal, 1.0, shaped)
            for a, b in (("mask", "maskT"), ("bmask", "bmaskT")):
                cut_to(K[a], flat, [[-1, P]], 0, 1, ALU.is_ge, NEG, shaped)
                cut_to(K[b], flat, [[1, P]], 0, -1, ALU.is_ge, NEG, shaped)
            for a in ("tri", "btri"):
                cut_to(K[a], flat, [[1, P]], 0, -1, ALU.is_ge, 0.0, shaped)
            cut_to(K["last"], flat, [[0, P]], -(P - 1), 1, ALU.not_equal, 1.0, shaped)
            cut_to(K["blast"], blocks, [[-L, NSEQ], [0, L]], -(L - 1), 1, ALU.not_equal, 1.0, shaped)
            cut_to(K["pick"], flat, [[-L, NSEQ]], -(L - 1), 1, ALU.not_equal, 1.0, shaped)
            cut_to(K["inblock"], flat, [[-L, NSEQ]], 0, 1, ALU.is_ge, 0.0, shaped)
            cut_to(K["headsel"], flat, [[-8, 2], [-1, 8], [0, L]], 0, 1, ALU.not_equal, 1.0, shaped)
            pool.wait_ge(shaped, 12)
            cut_to(K["bmask"], blocks, [[L, NSEQ], [0, L]], L - 1, -1, ALU.is_ge, NEG, cut)
            cut_to(K["bmaskT"], blocks, [[-L, NSEQ], [0, L]], 0, 1, ALU.is_ge, NEG, cut)
            cut_to(K["btri"], blocks, [[-L, NSEQ], [0, L]], 0, 1, ALU.is_ge, 0.0, cut)
            cut_to(K["inblock"], flat, [[L, NSEQ]], L - 1, -1, ALU.is_ge, 0.0, cut)
            pool.wait_ge(cut, 4)

        @block.vector
        def _(dve):
            dve.wait_ge(cut, 4)
            dve.tensor_reduce(K["masknew"][:], K["bmask"][:].rearrange("p (n j) -> p j n", n=NSEQ), AX.X,
                              ALU.max).then_inc(reduced, 1)
            dve.wait_ge(reduced, 1)


def stage_norm(nc, K, x, g_cols, aT):
    with Stage(nc, "norm") as st:
        xt, sq, xn = st.sb("xt", [P, D]), st.sb("sq", [P, D]), st.sb("xn", [P, D])
        gain = st.sb("gain", [P, KD])
        ss, ms, rt, rs = (st.sb(n, [P, 1]) for n in ("ss", "ms", "rt", "rs"))
        tp = st.ps("tp", [P, D])
        gain_in, x_in, squared, meaned, rooted, inverted, normed, turned, stored = st.sems(
            "gain_in x_in squared meaned rooted inverted normed turned stored")
        block = st.ctx.enter_context(nc.Block())

        @block.sync
        def _(sp):
            sp.dma_start(gain[:], g_cols).then_inc(gain_in, 16)
            with sp.Fori(0, NT) as i:
                sp.wait_ge(normed, i)
                sp.dma_start(xt[:], x[bass.ts(i, P), :]).then_inc(x_in, 16)

        @block.scalar
        def _(act):
            with act.Fori(0, NT) as i:
                act.wait_ge(x_in, i * 16 + 16)
                act.activation(sq[:], xt[:], ACT.Square, accum_out=ss[:]).then_inc(squared, 1)
                act.wait_ge(meaned, i + 1)
                act.activation(rt[:], ms[:], ACT.Sqrt).then_inc(rooted, 1)
                act.wait_ge(inverted, i + 1)
                act.wait_ge(turned, i)
                act.activation(xn[:], xt[:], ACT.Copy, scale=rs[:]).then_inc(normed, 1)

        @block.tensor
        def _(pe):
            with pe.Fori(0, NT) as i:
                pe.wait_ge(normed, i + 1)
                pe.wait_ge(stored, i)
                for k in range(KD):
                    mm = pe.transpose(tp[:, k * P:(k + 1) * P], xn[:, k * P:(k + 1) * P], K["ident"][:])
                mm.then_inc(turned, 1)

        @block.vector
        def _(dve):
            dve.wait_ge(gain_in, 16)
            with dve.Fori(0, NT) as i:
                dve.wait_ge(squared, i + 1)
                dve.tensor_scalar(ms[:], ss[:], 1.0 / D, EPS, ALU.mult, ALU.add).then_inc(meaned, 1)
                dve.wait_ge(rooted, i + 1)
                dve.reciprocal(rs[:], rt[:]).then_inc(inverted, 1)
                dve.wait_ge(turned, i + 1)
                dve.tensor_tensor(aT[:, :, bass.ts(i, P)], tp[:].rearrange("p (k t) -> p k t", k=KD),
                                  bc(gain[:], [P, KD, P]), ALU.mult).then_inc(stored, 1)
            dve.wait_ge(stored, NT)


def stage_project(nc, aT, w_in, z):
    with Stage(nc, "proj") as st:
        SLOTS = 6
        PER = 2 * NT
        w = st.sb("w", [P, 2, KD, CW])
        zs = st.sb("zs", [P, SLOTS, CW])
        acc = [st.ps(f"acc{s}", [P, 512]) for s in range(SLOTS)]
        w0_in, w1_in, summed, read_dve, read_act = st.sems("w0_in w1_in summed read_dve read_act")
        out = [st.pool_sem(f"out{s}") for s in range(SLOTS)]
        w_in_v = w_in.rearrange("(k p) n -> p k n", p=P)
        block = st.ctx.enter_context(nc.Block())

        @block.sync
        def _(sp):
            sp.dma_start(w[:, 0], w_in_v[:, :, 0:CW]).then_inc(w0_in, 16)
            with sp.Fori(0, CHUNKS // 2 - 1) as i:
                sp.wait_ge(summed, i * PER)
                sp.dma_start(w[:, 1], w_in_v[:, :, bass.ds(i * (2 * CW) + CW, CW)]).then_inc(w1_in, 16)
                sp.wait_ge(summed, i * PER + NT)
                sp.dma_start(w[:, 0], w_in_v[:, :, bass.ds(i * (2 * CW) + 2 * CW, CW)]).then_inc(w0_in, 16)
            sp.wait_ge(summed, (CHUNKS // 2 - 1) * PER)
            sp.dma_start(w[:, 1], w_in_v[:, :, IN_COLS - CW:IN_COLS]).then_inc(w1_in, 16)

        @block.tensor
        def _(pe):
            with pe.Fori(0, CHUNKS // 2) as i:
                for u in range(2):
                    pe.wait_ge((w0_in, w1_in)[u], i * 16 + 16)
                    for t in range(NT):
                        j = u * NT + t
                        pe.wait_ge((read_dve, read_act)[j % 2], i * (PER // 2) + j // 2 + 1)
                        for k in range(KD):
                            mm = pe.matmul(acc[j % SLOTS][:, 0:CW], aT[:, k, t * P:(t + 1) * P], w[:, u, k, :],
                                           start=(k == 0), stop=(k == KD - 1))
                        mm.then_inc(summed, 1)

        def reader(eng, me, copy, read):
            eng.sem_inc(read, SLOTS // 2)
            with eng.Fori(0, CHUNKS // 2) as i:
                for j in range(me, PER, 2):
                    eng.wait_ge(summed, i * PER + j + 1)
                    eng.wait_ge(out[j % SLOTS], (i * (PER // SLOTS) + j // SLOTS) * 16)
                    copy(zs[:, j % SLOTS, :], acc[j % SLOTS][:, 0:CW]).then_inc(read, 1)

        @block.vector
        def _(dve):
            reader(dve, 0, dve.tensor_copy, read_dve)

        @block.scalar
        def _(act):
            reader(act, 1, act.copy, read_act)

        @block.gpsimd
        def _(pool):
            with pool.Fori(0, CHUNKS // 2) as i:
                for j in range(PER):
                    pool.wait_ge((read_dve, read_act)[j % 2], i * (PER // 2) + j // 2 + 1 + SLOTS // 2)
                    t = j % NT
                    pool.dma_start(z[t * P:(t + 1) * P, bass.ds(i * (2 * CW) + (j // NT) * CW, CW)],
                                   zs[:, j % SLOTS, :]).then_inc(out[j % SLOTS], 16)
            for s in range(SLOTS):
                pool.wait_ge(out[s], CHUNKS // 2 * (PER // SLOTS) * 16)


def stage_gates(nc, K, z, bias, cache_lf, gates, T):
    with Stage(nc, "gate") as st:
        b = st.sb("b", [P, NG])
        e = st.sb("e", [P, NT, NG - H_M])
        lfT = st.sb("lfT", [H_F, TOK])
        ck = st.sb("ck", [H_F, SEQ])
        nck = st.sb("nck", [H_F, SEQ])
        one = st.sb("one", [P, SEQ])
        cs = st.sb("cs", [P, PAST + DSEQ])
        csum = st.sb("csum", [P, PAST + DSEQ])
        ncs = st.sb("ncs", [P, PAST + DSEQ])
        tp = st.ps("tp", [H_F, 2048])
        z_in, cache_in, biased, folded, expd, logd, ready, turned, copied, rows_out, new_in, summed, outs = st.sems(
            "z_in cache_in biased folded expd logd ready turned copied rows_out new_in summed outs")
        zr = z.rearrange("(t p) n -> p t n", p=P)
        f = gates[:, :, H_M:NG]
        block = st.ctx.enter_context(nc.Block())

        @block.sync
        def _(sp):
            sp.dma_start(gates[:, :, 0:2 * H_M], zr[:, :, C_IM:C_QF]).then_inc(z_in, 16)
            sp.dma_start(gates[:, :, 2 * H_M:NG], zr[:, :, C_FF:C_GM]).then_inc(z_in, 16)
            sp.dma_start(b[:], bc(bias, [P, NG])).then_inc(z_in, 16)
            sp.dma_start(cs[:, 0:PAST], cache_lf).then_inc(cache_in, 16)
            sp.dma_start(T["fox_k"], z[:, C_KF:C_VF]).then_inc(outs, 16)
            sp.dma_start(T["fox_v"], z[:, C_VF:C_FF]).then_inc(outs, 16)
            sp.wait_ge(ready, 1)
            sp.dma_start(T["fox_lf"].rearrange("(t p) h -> p t h", p=P), gates[:, :, 2 * H_M:NG]).then_inc(outs, 16)
            sp.wait_ge(copied, 1)
            sp.dma_start(T["lfT"], lfT[:]).then_inc(rows_out, 16)
            sp.wait_ge(rows_out, 16)
            for n in range(NSEQ):
                sp.dma_start(cs[n * H_F:(n + 1) * H_F, PAST:], T["lfT"][:, SEQ + n * DSEQ:SEQ + (n + 1) * DSEQ]
                             ).then_inc(new_in, 16)
            sp.wait_ge(summed, 4)
            sp.dma_start(T["nck"], nck[:]).then_inc(outs, 16)
            sp.dma_start(T["ncs"].rearrange("n h s -> (n h) s"), ncs[:]).then_inc(outs, 16)
            sp.wait_ge(outs, 5 * 16)

        @block.vector
        def _(dve):
            dve.memset(one[:], 1.0).then_inc(biased, 1)
            dve.wait_ge(z_in, 48)
            dve.tensor_tensor(gates[:], gates[:], b[:].unsqueeze(1).to_broadcast([P, NT, NG]), ALU.add
                              ).then_inc(biased, 1)
            dve.wait_ge(biased, 2)
            dve.scalar_tensor_tensor(out=e[:], in0=f, scalar=-1.0, in1=f, op0=ALU.mult, op1=ALU.min).then_inc(folded, 1)
            dve.wait_ge(logd, 1)
            dve.scalar_tensor_tensor(out=f, in0=f, scalar=0.0, in1=e[:], op0=ALU.min, op1=ALU.subtract
                                     ).then_inc(ready, 1)
            dve.wait_ge(turned, 1)
            dve.tensor_copy(lfT[:], tp[:, 0:TOK]).then_inc(copied, 1)
            dve.wait_ge(copied, 1)
            dve.tensor_tensor_scan(ck[:], one[0:H_F, :], lfT[:, 0:SEQ], 0.0, ALU.mult, ALU.add).then_inc(summed, 1)
            dve.wait_ge(cache_in, 16)
            dve.wait_ge(new_in, 16 * NSEQ)
            dve.tensor_tensor_scan(csum[:], one[:, 0:PAST + DSEQ], cs[:], 0.0, ALU.mult, ALU.add).then_inc(summed, 1)
            dve.wait_ge(summed, 2)
            dve.tensor_scalar(nck[:], ck[:], -1.0, None, ALU.mult).then_inc(summed, 1)
            dve.tensor_scalar(ncs[:], csum[:], -1.0, None, ALU.mult).then_inc(summed, 1)

        @block.scalar
        def _(act):
            act.wait_ge(folded, 1)
            act.activation(e[:], e[:], ACT.Exp).then_inc(expd, 1)
            act.wait_ge(expd, 1)
            act.activation(e[:], e[:], ACT.Ln, bias=1.0).then_inc(logd, 1)

        @block.tensor
        def _(pe):
            pe.wait_ge(ready, 1)
            for t in range(NT):
                mm = pe.transpose(tp[:, t * P:(t + 1) * P], gates[:, t, 2 * H_M:NG], K["ident"][:])
            mm.then_inc(turned, 1)


def stage_fox_prompt(nc, K, z, T):
    with Stage(nc, "foxp") as st:
        HP = 2
        NS = HP * PT
        q, k, v = (st.sb(n, [P, PT, P]) for n in "qkv")
        qT, kT = (st.sb(n, [DF + 1, HP, SEQ]) for n in ("qT", "kT"))
        prob = st.sb("prob", [P, 2, SEQ])
        probT = st.sb("probT", [P, SEQ])
        nmax, total, inv = (st.sb(n, [P, 2]) for n in ("nmax", "total", "inv"))
        y = st.sb("y", [P, PT, P])
        s_ps = [st.ps(f"s{n}", [P, SEQ]) for n in range(2)]
        t_ps = st.ps("t", [P, SEQ])
        h_ps = st.ps("h", [P, 512])
        y_ps = st.ps("y", [P, 512])
        ybank = [y_ps, h_ps]
        tbank = [h_ps[0:DF, :], t_ps[0:DF, 0:512], t_ps[0:DF, 512:1024]]
        (ones_set, qk_in, v_in, ck_in, turned, turned_out, scored, maxed, expd, inverted, probs_turned,
         probs_out, mixed, y_ready, y_out) = st.sems(
            "ones_set qk_in v_in ck_in turned turned_out scored maxed expd inverted probs_turned "
            "probs_out mixed y_ready y_out")
        zr = z.rearrange("(t p) n -> p t n", p=P)
        NTR = 8
        block = st.ctx.enter_context(nc.Block())

        @block.sync
        def _(sp):
            with sp.Fori(0, H_F // HP) as i:
                sp.wait_ge(turned, i * NTR)
                for buf, col in ((q, C_QF), (k, C_KF)):
                    sp.dma_start(buf[:], zr[:, 0:PT, bass.ds(i * P + col, P)]).then_inc(qk_in, 16)
                sp.wait_ge(scored, i * NS)
                for e in range(HP):
                    sp.dma_start(kT[DF:DF + 1, e, :], T["nck"][bass.ds(i * HP + e, 1), :]).then_inc(ck_in, 16)
                sp.wait_ge(mixed, i * NS)
                sp.dma_start(v[:], zr[:, 0:PT, bass.ds(i * P + C_VF, P)]).then_inc(v_in, 16)
                if True:
                    sp.wait_ge(y_ready, i * NS + NS)
                    sp.dma_start(T["ycat"].rearrange("(t p) n -> p t n", p=P)[:, 0:PT, bass.ds(i * P + W_M, P)],
                                 y[:]).then_inc(y_out, 16)
            sp.wait_ge(y_out, H_F // HP * 16)

        @block.tensor
        def _(pe):
            def scores(i, s):
                e, b = divmod(s, PT)
                if s >= 2:
                    pe.wait_ge(expd, i * NS + s - 1)
                n = (b + 1) * P
                for c in range(0, n, 512):
                    m = min(512, n - c)
                    last = c + m == n
                    mm = pe.matmul(s_ps[s % 2][:, c:c + m], qT[:, e, b * P:(b + 1) * P], kT[:, e, c:c + m],
                                   start=True, stop=not last)
                mm = pe.matmul(s_ps[s % 2][:, n - P:n], K["ident"][:], K["mask"][:], start=False, stop=True)
                mm.then_inc(scored, 1)

            def turn(i, s):
                b = s % PT
                hold(pe, expd, i * NS + s + 1, K["passed"])
                if s >= 1:
                    hold(pe, probs_out, i * NS + s, K["passed"])
                for c in range(b + 1):
                    mm = pe.transpose(t_ps[:, c * P:(c + 1) * P], prob[:, s % 2, c * P:(c + 1) * P], K["ident"][:])
                mm.then_inc(probs_turned, 1)

            def mix(i, s):
                e, b = divmod(s, PT)
                pe.wait_ge(probs_out, i * NS + s + 1)
                if s >= 2:
                    pe.wait_ge(y_ready, i * NS + s - 1)
                for c in range(b + 1):
                    mm = pe.matmul(ybank[s % 2][:, 0:DF], probT[:, c * P:(c + 1) * P],
                                   v[:, c, e * DF:(e + 1) * DF], start=(c == 0), stop=(c == b))
                mm.then_inc(mixed, 1)

            pe.wait_ge(ones_set, 1)
            with pe.Fori(0, H_F // HP) as i:
                pe.wait_ge(qk_in, i * 32 + 32)
                pe.wait_ge(probs_out, i * NS)
                hold(pe, y_ready, i * NS, K["passed"])
                for g in range(NTR):
                    src, e, half = (q, k)[g // 4], g // 2 % 2, g % 2
                    if g >= 3:
                        hold(pe, turned_out, i * NTR + g - 2, K["passed"])
                    for c in range(4):
                        mm = pe.transpose(tbank[g % 3][:, c * P:(c + 1) * P], src[:, half * 4 + c, e * DF:(e + 1) * DF],
                                          K["ident"][:])
                    mm.then_inc(turned, 1)
                pe.wait_ge(turned_out, i * NTR + NTR)
                pe.wait_ge(ck_in, i * 32 + 32)
                for s in range(NS + 1):
                    if s < NS:
                        scores(i, s)
                    if s == 1:
                        pe.wait_ge(v_in, i * 16 + 16)
                    if s >= 1:
                        turn(i, s - 1)
                        mix(i, s - 1)

        @block.vector
        def _(dve):
            dve.memset(qT[DF:DF + 1, :, :], 1.0).then_inc(ones_set, 1)
            with dve.Fori(0, H_F // HP) as i:
                for g in range(NTR):
                    e, half = g // 2 % 2, g % 2
                    dve.wait_ge(turned, i * NTR + g + 1)
                    cols = slice(half * 512, half * 512 + 512)
                    if g < 4:
                        dve.tensor_scalar(qT[0:DF, e, cols], tbank[g % 3], DF ** -0.5, None, ALU.mult
                                          ).then_inc(turned_out, 1)
                    else:
                        dve.tensor_copy(kT[0:DF, e, cols], tbank[g % 3]).then_inc(turned_out, 1)
                dve.wait_ge(y_out, i * 16)
                for s in range(NS + 1):
                    if s < NS:
                        n = (s % PT + 1) * P
                        dve.wait_ge(scored, i * NS + s + 1)
                        dve.tensor_reduce(nmax[:, s % 2:s % 2 + 1], s_ps[s % 2][:, 0:n], AX.X, ALU.max, negate=True
                                          ).then_inc(maxed, 1)
                    if s >= 1:
                        r = s - 1
                        e, b = divmod(r, PT)
                        dve.wait_ge(expd, i * NS + r + 1)
                        dve.reciprocal(inv[:, r % 2:r % 2 + 1], total[:, r % 2:r % 2 + 1]).then_inc(inverted, 1)
                        dve.wait_ge(inverted, i * NS + r + 1)
                        dve.wait_ge(mixed, i * NS + r + 1)
                        dve.tensor_scalar(y[:, b, e * DF:(e + 1) * DF], ybank[r % 2][:, 0:DF],
                                          inv[:, r % 2:r % 2 + 1], None, ALU.mult).then_inc(y_ready, 1)

        @block.scalar
        def _(act):
            with act.Fori(0, H_F // HP) as i:
                for s in range(NS + 1):
                    if s < NS:
                        n = (s % PT + 1) * P
                        act.wait_ge(maxed, i * NS + s + 1)
                        if s >= 2:
                            act.wait_ge(inverted, i * NS + s - 1)
                            act.wait_ge(probs_turned, i * NS + s - 1)
                        else:
                            act.wait_ge(inverted, i * NS)
                            act.wait_ge(probs_turned, i * NS)
                        act.activation(prob[:, s % 2, 0:n], s_ps[s % 2][:, 0:n], ACT.Exp, bias=nmax[:, s % 2:s % 2 + 1],
                                       accum_out=total[:, s % 2:s % 2 + 1]).then_inc(expd, 1)
                    if s >= 1:
                        n = ((s - 1) % PT + 1) * P
                        act.wait_ge(probs_turned, i * NS + s)
                        act.copy(probT[:, 0:n], t_ps[:, 0:n]).then_inc(probs_out, 1)


def stage_fox_sample(nc, K, z, T):
    with Stage(nc, "foxs") as st:
        S = PAST + DSEQ
        ST = PAST // P
        q, k = st.sb("q", [P, W_F]), st.sb("k", [P, W_F])
        qT, kT = st.sb("qT", [P, KD, P]), st.sb("kT", [P, KD, P])
        kc = st.sb("kc", [P, KD, PAST])
        vc = st.sb("vc", [P, ST, W_F])
        vn = st.sb("vn", [DSEQ, W_F])
        ck = st.sb("ck", [H_F, S])
        kn = st.sb("kn", [P, KD, DSEQ])
        qd = st.sb("qd", [P, 2, 4, P])
        prob = st.sb("prob", [P, 2, S])
        probT = st.sb("probT", [P, 5 * P])
        nmax, total, inv = (st.sb(n, [P, 2]) for n in ("nmax", "total", "inv"))
        y = st.sb("y", [P, 2, 512])
        s_ps = [st.ps(f"s{n}", [P, 1024]) for n in range(2)]
        t_ps = st.ps("t", [P, 1024])
        y_ps = st.ps("y", [P, 1024])
        (zeroed, qk_in, turned, turned_out, kc_in, vc_in, placed, scored, maxed, expd, inverted, probs_turned,
         probs_out, mixed, y_ready) = st.sems(
            "zeroed qk_in turned turned_out kc_in vc_in placed scored maxed expd inverted probs_turned "
            "probs_out mixed y_ready")
        y_out = st.pool_sem("y_out")
        HO = 2 * 8 * 16
        block = st.ctx.enter_context(nc.Block())

        @block.sync
        def _(sp):
            sp.dma_start(q[:], z[SEQ:TOK, C_QF:C_KF]).then_inc(qk_in, 16)
            sp.dma_start(k[:], z[SEQ:TOK, C_KF:C_VF]).then_inc(qk_in, 16)
            with sp.Fori(0, NSEQ) as n:
                sp.wait_ge(scored, n * 2)
                sp.dma_start(kc[:], T["cache_kT"][n].rearrange("(c p) s -> p c s", p=P)).then_inc(kc_in, 16)
                sp.dma_start(ck[:], T["ncs"][n]).then_inc(kc_in, 16)
                sp.wait_ge(mixed, n * 2)
                sp.dma_start(vc[:], T["cache_v"][n].rearrange("(c p) s -> p c s", p=P)).then_inc(vc_in, 16)
                sp.dma_start(vn[:], z[bass.ds(n * DSEQ + SEQ, DSEQ), C_VF:C_FF]).then_inc(vc_in, 16)

        @block.gpsimd
        def _(pool):
            with pool.Fori(0, NSEQ) as n:
                for f in range(2):
                    pool.wait_ge(y_ready, n * 2 + f + 1)
                    for h in range(8):
                        pool.dma_start(T["ycat"][bass.ds(n * DSEQ + SEQ, DSEQ),
                                                 W_M + (8 * f + h) * DF:W_M + (8 * f + h + 1) * DF],
                                       y[h * DSEQ:(h + 1) * DSEQ, f, h * DF:(h + 1) * DF]).then_inc(y_out, 16)
            pool.wait_ge(y_out, NSEQ * HO)

        @block.tensor
        def _(pe):
            pe.wait_ge(qk_in, 32)
            for g, src in enumerate((q, k)):
                for c in range(KD):
                    mm = pe.transpose((s_ps[g])[:, c * P:(c + 1) * P], src[:, c * P:(c + 1) * P], K["ident"][:])
                mm.then_inc(turned, 1)
            pe.wait_ge(turned_out, 2)
            with pe.Fori(0, NSEQ) as n:
                pe.wait_ge(placed, n * 5 + 5)
                pe.wait_ge(kc_in, n * 32 + 32)
                for f in range(2):
                    pe.wait_ge(expd, n * 2)
                    for p in range(4):
                        pe.matmul(s_ps[f][:, 0:PAST], qd[:, f, p, :], kc[:, 4 * f + p, :], start=(p == 0), stop=False)
                    pe.matmul(s_ps[f][:, 0:PAST], K["headsel"][:, f].rearrange("p h q -> p (h q)"), ck[:, 0:PAST],
                              start=False, stop=True)
                    for p in range(4):
                        pe.matmul(s_ps[f][:, PAST:S], qd[:, f, p, :], kn[:, 4 * f + p, :], start=(p == 0), stop=False)
                    pe.matmul(s_ps[f][:, PAST:S], K["headsel"][:, f].rearrange("p h q -> p (h q)"), ck[:, PAST:S],
                              start=False, stop=False)
                    pe.matmul(s_ps[f][:, PAST:S], K["ident"][:], K["masknew"][:], start=False, stop=True
                              ).then_inc(scored, 1)
                pe.wait_ge(vc_in, n * 32 + 32)
                for f in range(2):
                    pe.wait_ge(expd, n * 2 + f + 1)
                    pe.wait_ge(probs_out, n * 2 + f)
                    for c in range(ST):
                        pe.transpose(t_ps[:, c * P:(c + 1) * P], prob[:, f, c * P:(c + 1) * P], K["ident"][:])
                    pe.transpose(t_ps[0:DSEQ, ST * P:(ST + 1) * P], prob[:, f, PAST:S], K["ident"][:]
                                 ).then_inc(probs_turned, 1)
                    pe.wait_ge(probs_out, n * 2 + f + 1)
                    pe.wait_ge(y_ready, n * 2)
                    for c in range(ST):
                        pe.matmul(y_ps[:, f * 512:(f + 1) * 512], probT[:, c * P:(c + 1) * P],
                                  vc[:, c, f * 512:(f + 1) * 512], start=(c == 0), stop=False)
                    pe.matmul(y_ps[:, f * 512:(f + 1) * 512], probT[0:DSEQ, ST * P:(ST + 1) * P],
                              vn[:, f * 512:(f + 1) * 512], start=False, stop=True).then_inc(mixed, 1)

        @block.vector
        def _(dve):
            dve.memset(qd[:], 0.0).then_inc(zeroed, 1)
            dve.wait_ge(turned, 1)
            dve.tensor_scalar(qT[:].rearrange("p c t -> p (c t)"), s_ps[0][:], DF ** -0.5, None, ALU.mult
                              ).then_inc(turned_out, 1)
            dve.wait_ge(turned, 2)
            dve.tensor_copy(kT[:].rearrange("p c t -> p (c t)"), s_ps[1][:]).then_inc(turned_out, 1)
            dve.wait_ge(zeroed, 1)
            dve.wait_ge(turned_out, 2)
            with dve.Fori(0, NSEQ) as n:
                dve.wait_ge(scored, n * 2)
                for f in range(2):
                    for e in range(2):
                        base = qd[e * DF:(e + 1) * DF, f, :, :]
                        flat = base.rearrange("p c m -> p (c m)")
                        first = e * DSEQ
                        dve.tensor_copy(diag4(flat, first), qT[e * DF:(e + 1) * DF, 4 * f:4 * f + 4, bass.ts(n, DSEQ)]
                                        ).then_inc(placed, 1)
                dve.tensor_copy(kn[:], kT[:, :, bass.ts(n, DSEQ)]).then_inc(placed, 1)
                for f in range(2):
                    dve.wait_ge(scored, n * 2 + f + 1)
                    dve.tensor_reduce(nmax[:, f:f + 1], s_ps[f][:, 0:S], AX.X, ALU.max, negate=True).then_inc(maxed, 1)
                for f in range(2):
                    dve.wait_ge(expd, n * 2 + f + 1)
                    dve.reciprocal(inv[:, f:f + 1], total[:, f:f + 1]).then_inc(inverted, 1)
                    dve.wait_ge(inverted, n * 2 + f + 1)
                    dve.wait_ge(mixed, n * 2 + f + 1)
                    dve.wait_ge(y_out, n * HO)
                    dve.tensor_scalar(y[:, f, :], y_ps[:, f * 512:(f + 1) * 512], inv[:, f:f + 1], None, ALU.mult
                                      ).then_inc(y_ready, 1)

        @block.scalar
        def _(act):
            with act.Fori(0, NSEQ) as n:
                for f in range(2):
                    act.wait_ge(maxed, n * 2 + f + 1)
                    act.wait_ge(probs_turned, n * 2)
                    act.wait_ge(inverted, n * 2)
                    act.activation(prob[:, f, :], s_ps[f][:, 0:S], ACT.Exp, bias=nmax[:, f:f + 1],
                                   accum_out=total[:, f:f + 1]).then_inc(expd, 1)
                for f in range(2):
                    act.wait_ge(probs_turned, n * 2 + f + 1)
                    act.wait_ge(mixed, n * 2 + f)
                    act.copy(probT[:, 0:PAST], t_ps[:, 0:PAST])
                    act.copy(probT[0:DSEQ, PAST:PAST + P], t_ps[0:DSEQ, PAST:PAST + P]).then_inc(probs_out, 1)


def diag4(flat, first):
    step = P + 2 * DSEQ
    v = flat[:, first:first + 3 * step + DSEQ]
    return bass.AP(tensor=v.tensor, offset=v.offset, ap=[v.ap[0], [step, 4], [1, DSEQ]])


class Chain:

    def __init__(self, eng, sem, it, per, ready):
        self.ready = ready
        self.eng, self.sem, self.it, self.per, self.n = eng, sem, it, per, 0

    def __call__(self, instruction):
        instruction.then_inc(self.sem, 1)
        self.n += 1
        hold(self.eng, self.sem, self.it * self.per + self.n, self.ready)

    def close(self):
        assert self.n == self.per, (self.n, self.per)


def eye_times(dve, K, out, cols, heads):
    return dve.tensor_tensor(out, K["ident"][:].unsqueeze(1).to_broadcast([P, heads, P]), bc(cols, [P, heads, P]),
                             ALU.mult)


def stage_mlstm_prompt(nc, K, z, gates, T):
    with Stage(nc, "mlp") as st:
        H, DA = H_M, DM + 1
        KS = DM ** -0.5
        q, k, o = st.sb("q", [P, W_M]), st.sb("k", [P, W_M]), st.sb("o", [P, W_M])
        v = st.sb("v", [P, H, DA])
        C = st.sb("C", [P, 2 * H, DA])
        qT, kT = st.sb("qT", [P, 2 * H, P]), st.sb("kT", [P, 2 * H, P])
        g8 = st.sb("g8", [P, 2 * H])
        x, b, rmax, m = (st.sb(n, [P, H]) for n in ("x", "b", "rmax", "m"))
        Mm = st.sb("Mm", [P, 2 * H])
        Ml = st.sb("Ml", [P, 2 * H])
        e1, e2 = st.sb("e1", [P, 2 * H]), st.sb("e2", [P, 2 * H])
        w1, w2 = st.sb("w1", [P, 2 * H]), st.sb("w2", [P, 2 * H])
        dx, dM = st.sb("dx", [P, H, P]), st.sb("dM", [P, H, P])
        wD, A = st.sb("wD", [P, H, P]), st.sb("A", [P, H, P])
        inter, num = st.sb("inter", [P, DA]), st.sb("num", [P, DA])
        kw = st.sb("kw", [P, 2, DM])
        den = st.sb("den", [P, 1])
        inv = st.sb("inv", [P, 1])
        so = st.sb("so", [P, W_M])
        y = st.sb("y", [P, W_M])
        g_ps, e_ps, s_ps, t_ps, n1_ps, n2_ps, c0_ps, c1_ps = (
            st.ps(n, [P, 512]) for n in ("g", "e", "s", "t", "n1", "n2", "c0", "c1"))
        tb = [t_ps, c0_ps, c1_ps, t_ps]
        (set_up, z_in, gates_in, summed, x_set, dx_set, rows_e, chain, m_set, dm_set, rows_m, w1_set, wd_set,
         last_set, e2_set, w2_set, turned, turned_out, scored, mixed, n_ready, inter_set, kw_set, c_summed, c_set,
         y_head, o_set, y_out, outs) = st.sems(
            "set_up z_in gates_in summed x_set dx_set rows_e chain m_set dm_set rows_m w1_set wd_set "
            "last_set e2_set w2_set turned turned_out scored mixed n_ready inter_set kw_set c_summed c_set "
            "y_head o_set y_out outs")
        DVE_STEPS = 2 + 3 + 1 + 4 * H
        block = st.ctx.enter_context(nc.Block())

        @block.sync
        def _(sp):
            sp.wait_ge(set_up, 3)
            with sp.Fori(0, PT) as i:
                rows = bass.ts(i, P)
                sp.wait_ge(c_set, i * 2 * H)
                sp.dma_start(q[:], z[rows, C_QM:C_KM]).then_inc(z_in, 16)
                sp.dma_start(k[:], z[rows, C_KM:C_VM]).then_inc(z_in, 16)
                sp.dma_start(v[:, :, 0:DM], z[rows, C_VM:C_OM].rearrange("t (h e) -> t h e", h=H)).then_inc(z_in, 16)
                sp.wait_ge(o_set, i)
                sp.dma_start(o[:], z[rows, C_OM:C_IM]).then_inc(z_in, 16)
                sp.wait_ge(y_head, i * H + H)
                sp.dma_start(T["ycat"][rows, 0:W_M], y[:]).then_inc(y_out, 16)
            sp.wait_ge(c_set, PT * 2 * H)
            for h in range(H):
                sp.dma_start(T["mC_p"][h].rearrange("(j p) e -> p j e", p=P), C[:, 2 * h:2 * h + 2, 0:DM]
                             ).then_inc(outs, 16)
            with nc.allow_non_contiguous_dma(reason="one column of the state"):
                sp.dma_start(T["mn_p"], C[:, :, DM]).then_inc(outs, 16)
            sp.dma_start(T["mm_p"], m[0:1, :]).then_inc(outs, 16)
            sp.wait_ge(outs, (H + 2) * 16)
            sp.wait_ge(y_out, PT * 16)

        @block.tensor
        def _(pe):
            pe.wait_ge(set_up, 3)
            with pe.Fori(0, PT) as i:
                pe.wait_ge(gates_in, i + 1)
                pe.wait_ge(last_set, i)
                pe.matmul(g_ps[:, 0:H], K["tri"][:], g8[:, H:2 * H], start=True, stop=True).then_inc(summed, 1)
                pe.wait_ge(z_in, i * 64 + 64)
                pe.wait_ge(c_set, i * 2 * H)
                for g in range(4):
                    if g == 3:
                        pe.wait_ge(turned_out, i * 4 + 1)
                    for c in range(4):
                        mm = pe.transpose(tb[g][:, c * P:(c + 1) * P],
                                          (q, k)[g // 2][:, (g % 2 * 4 + c) * P:(g % 2 * 4 + c + 1) * P], K["ident"][:])
                    mm.then_inc(turned, 1)
                pe.wait_ge(dx_set, i + 1)
                pe.wait_ge(wd_set, i)
                pe.matmul(e_ps[:], K["ones"][:], dx[:].rearrange("p h t -> p (h t)"), start=True, stop=False)
                for h in range(H):
                    mm = pe.matmul(e_ps[:, h * P:(h + 1) * P], K["ident"][:], K["mask"][:], start=False,
                                   stop=(h == H - 1))
                mm.then_inc(rows_e, 1)
                pe.wait_ge(turned_out, i * 4 + 4)
                pe.wait_ge(mixed, i)
                for h in range(H):
                    for j in range(2):
                        mm = pe.matmul(s_ps[:, h * P:(h + 1) * P], kT[:, 2 * h + j, :], qT[:, 2 * h + j, :],
                                       start=(j == 0), stop=(j == 1))
                mm.then_inc(scored, 1)
                pe.wait_ge(m_set, i + 1)
                pe.matmul(g_ps[:, 2 * H:4 * H], K["last"][:], Mm[:], start=True, stop=True).then_inc(summed, 1)
                pe.wait_ge(dm_set, i + 1)
                pe.matmul(e_ps[:], K["negones"][:], dM[:].rearrange("p h t -> p (h t)"), start=True, stop=False)
                for h in range(H):
                    mm = pe.matmul(e_ps[:, h * P:(h + 1) * P], K["ident"][:], K["maskT"][:], start=False,
                                   stop=(h == H - 1))
                mm.then_inc(rows_m, 1)
                for h in range(H):
                    pe.wait_ge(mixed, i + 1)
                    pe.wait_ge(y_head, i * H + h)
                    pe.matmul(n1_ps[:, 0:DA], A[:, h, :], v[:, h, :], start=True, stop=True)
                    for j in range(2):
                        mm = pe.matmul(n2_ps[:, 0:DA], qT[:, 2 * h + j, :], C[:, 2 * h + j, :], start=(j == 0),
                                       stop=(j == 1))
                    mm.then_inc(n_ready, 1)
                    pe.wait_ge(kw_set, i * H + h + 1)
                    pe.wait_ge(c_set, i * 2 * H + 2 * h)
                    for j, cb in enumerate((c0_ps, c1_ps)):
                        mm = pe.matmul(cb[:, 0:DA], kw[:, h % 2, j * P:(j + 1) * P], v[:, h, :], start=True, stop=True)
                    mm.then_inc(c_summed, 1)

        @block.vector
        def _(dve):
            dve.memset(C[:], 0.0).then_inc(set_up, 1)
            dve.memset(v[:, :, DM:DA], 1.0).then_inc(set_up, 1)
            dve.memset(m[:], 0.0).then_inc(set_up, 1)
            dve.wait_ge(set_up, 3)
            with dve.Fori(0, PT) as i:
                ch = Chain(dve, chain, i, DVE_STEPS, K["passed"])
                dve.wait_ge(summed, i * 2)
                dve.wait_ge(w2_set, i)
                dve.tensor_copy(g8[:], gates[:, bass.ds(i, 1), 0:2 * H].rearrange("p a g -> p (a g)")
                                ).then_inc(gates_in, 1)
                dve.wait_ge(gates_in, i + 1)
                dve.wait_ge(summed, i * 2 + 1)
                dve.wait_ge(wd_set, i)
                dve.tensor_tensor(x[:], g8[:, 0:H], g_ps[:, 0:H], ALU.subtract).then_inc(x_set, 1)
                ch(dve.tensor_copy(b[:], g_ps[:, 0:H]))
                dve.wait_ge(x_set, i + 1)
                eye_times(dve, K, dx[:], x[:], H).then_inc(dx_set, 1)
                dve.wait_ge(rows_e, i + 1)
                ch(dve.tensor_reduce(rmax[:], e_ps[:].rearrange("p (h t) -> p h t", h=H), AX.X, ALU.max))
                dve.wait_ge(summed, i * 2)
                ch(dve.tensor_tensor(Mm[:, 0:H], rmax[:], m[:], ALU.max))
                dve.tensor_tensor(Mm[:, H:2 * H], b[:], Mm[:, 0:H], ALU.add).then_inc(m_set, 1)
                dve.wait_ge(m_set, i + 1)
                ch(dve.tensor_tensor(e1[:, 0:H], m[:], Mm[:, 0:H], ALU.subtract))
                ch(dve.tensor_scalar(e1[:, H:2 * H], Mm[:, H:2 * H], -1.0, None, ALU.mult))
                eye_times(dve, K, dM[:], Mm[:, 0:H], H).then_inc(dm_set, 1)
                dve.wait_ge(summed, i * 2 + 2)
                dve.tensor_copy(Ml[:], g_ps[:, 2 * H:4 * H]).then_inc(last_set, 1)
                dve.wait_ge(last_set, i + 1)
                ch(dve.tensor_tensor(e2[:, 0:H], m[:], Ml[:, 0:H], ALU.subtract))
                dve.tensor_tensor(e2[:, H:2 * H], x[:], Ml[:, 0:H], ALU.subtract).then_inc(e2_set, 1)
                dve.wait_ge(e2_set, i * 2 + 1)
                dve.tensor_copy(m[:], Ml[:, H:2 * H]).then_inc(e2_set, 1)
                dve.wait_ge(e2_set, i * 2 + 2)
                dve.wait_ge(scored, i + 1)
                dve.wait_ge(wd_set, i + 1)
                dve.wait_ge(n_ready, i * H)
                dve.tensor_tensor(A[:].rearrange("p h t -> p (h t)"), s_ps[:], wD[:].rearrange("p h t -> p (h t)"),
                                  ALU.mult).then_inc(mixed, 1)
                dve.wait_ge(w2_set, i + 1)
                dve.wait_ge(y_out, i * 16)
                dve.wait_ge(o_set, i + 1)
                for h in range(H):
                    if h >= 2:
                        dve.wait_ge(c_summed, i * H + h - 1)
                    else:
                        dve.wait_ge(c_summed, i * H)
                    dve.tensor_scalar(kw[:, h % 2, :], k[:, h * DM:(h + 1) * DM], w2[:, H + h:H + h + 1], KS,
                                      ALU.mult, ALU.mult).then_inc(kw_set, 1)
                    dve.wait_ge(inter_set, i * H + h + 1)
                    ch(dve.tensor_tensor(num[:], n1_ps[:, 0:DA], inter[:], ALU.add))
                    ch(dve.scalar_tensor_tensor(out=den[:], in0=num[:, DM:DA], scalar=-1.0, in1=w1[:, H + h:H + h + 1],
                                                op0=ALU.mult, op1=ALU.max))
                    ch(dve.tensor_tensor(den[:], den[:], num[:, DM:DA], ALU.max))
                    ch(dve.reciprocal(inv[:], den[:]))
                    dve.scalar_tensor_tensor(out=y[:, h * DM:(h + 1) * DM], in0=num[:, 0:DM], scalar=inv[:],
                                             in1=so[:, h * DM:(h + 1) * DM], op0=ALU.mult, op1=ALU.mult
                                             ).then_inc(y_head, 1)
                    dve.wait_ge(y_head, i * H + h + 1)
                    dve.wait_ge(c_summed, i * H + h + 1)
                    for j, cb in enumerate((c0_ps, c1_ps)):
                        dve.scalar_tensor_tensor(out=C[:, 2 * h + j, :], in0=C[:, 2 * h + j, :], scalar=w2[:, h:h + 1],
                                                 in1=cb[:, 0:DA], op0=ALU.mult, op1=ALU.add).then_inc(c_set, 1)
                dve.wait_ge(c_set, i * 2 * H + 2 * H)
                ch.close()

        @block.scalar
        def _(act):
            with act.Fori(0, PT) as i:
                act.wait_ge(scored, i)
                act.wait_ge(n_ready, i * H)
                for g in range(4):
                    act.wait_ge(turned, i * 4 + g + 1)
                    dst = (qT, kT)[g // 2][:, g % 2 * 4:g % 2 * 4 + 4, :].rearrange("p c t -> p (c t)")
                    act.mul(dst, tb[g][:], (1.0, KS)[g // 2]).then_inc(turned_out, 1)
                act.wait_ge(m_set, i + 1)
                act.wait_ge(chain, i * DVE_STEPS + 5)
                act.wait_ge(c_set, i * 2 * H)
                act.activation(w1[:], e1[:], ACT.Exp).then_inc(w1_set, 1)
                act.wait_ge(rows_m, i + 1)
                act.wait_ge(mixed, i)
                for h in range(H):
                    e = act.activation(wD[:, h, :], e_ps[:, h * P:(h + 1) * P], ACT.Exp, bias=x[:, h:h + 1])
                e.then_inc(wd_set, 1)
                act.wait_ge(e2_set, i * 2 + 1)
                act.activation(w2[:], e2[:], ACT.Exp).then_inc(w2_set, 1)
                act.wait_ge(z_in, i * 64 + 64)
                act.wait_ge(y_head, i * H)
                act.activation(so[:], o[:], ACT.Sigmoid).then_inc(o_set, 1)
                act.wait_ge(w1_set, i + 1)
                for h in range(H):
                    act.wait_ge(n_ready, i * H + h + 1)
                    act.wait_ge(y_head, i * H + h)
                    act.activation(inter[:], n2_ps[:, 0:DA], ACT.Copy, scale=w1[:, h:h + 1]).then_inc(inter_set, 1)


def stage_mlstm_sample(nc, K, z, gates, T):
    with Stage(nc, "mls") as st:
        H, DA, N = H_M, DM + 1, NSEQ
        KS = DM ** -0.5
        q, k, o = st.sb("q", [P, DM]), st.sb("k", [P, DM]), st.sb("o", [P, DM])
        v = st.sb("v", [P, DA])
        C = st.sb("C", [P, N, 2, DA])
        n_all = st.sb("n_all", [P, N, H, 2])
        n_new = st.sb("n_new", [P, N, H, 2])
        m_all, m_new = st.sb("m_all", [P, H]), st.sb("m_new", [P, H])
        qT, kT = st.sb("qT", [P, 2, P]), st.sb("kT", [P, 2, P])
        qd = st.sb("qd", [P, 2, N * P])
        g2 = st.sb("g2", [P, 2])
        x, b, rmax, m = (st.sb(n, [P, 1]) for n in ("x", "b", "rmax", "m"))
        Mm, Ml = st.sb("Mm", [P, 2]), st.sb("Ml", [P, 2])
        e1, e2, w1, w2 = (st.sb(n, [P, 2]) for n in ("e1", "e2", "w1", "w2"))
        wp, wc = st.sb("wp", [P, N]), st.sb("wc", [P, N])
        dx, dM = st.sb("dx", [P, 1, P]), st.sb("dM", [P, 1, P])
        wD, A = st.sb("wD", [P, P]), st.sb("A", [P, P])
        inter, num, so, y = st.sb("inter", [P, DA]), st.sb("num", [P, DA]), st.sb("so", [P, DM]), st.sb("y", [P, DM])
        kws = st.sb("kws", [P, DM])
        kw = st.sb("kw", [P, 2, DM])
        den, inv = st.sb("den", [P, 1]), st.sb("inv", [P, 1])
        g_ps, e_ps, s_ps, t_ps, n1_ps, n2_ps, c0_ps, c1_ps = (
            st.ps(n, [P, 512]) for n in ("g", "e", "s", "t", "n1", "n2", "c0", "c1"))
        (set_up, state_in, z_in, c_in, c_cols, gates_in, summed, chain, rows_e, m_set, dm_set, rows_m, w1_set, wd_set,
         last_set, e2_set, w2_set, wp_set, turned, turned_out, placed, scored, mixed, n_ready, inter_set, kw_set,
         c_summed, c_set, y_head, o_set, y_out, c_out, outs, dx_set) = st.sems(
            "set_up state_in z_in c_in c_cols gates_in summed chain rows_e m_set dm_set rows_m w1_set wd_set "
            "last_set e2_set w2_set wp_set turned turned_out placed scored mixed n_ready inter_set kw_set "
            "c_summed c_set y_head o_set y_out c_out outs dx_set")
        DVE_STEPS = 2 + 1 + 1 + 2 + 2 + 1 + 5 + 1 + 1
        rows = slice(SEQ, TOK)
        block = st.ctx.enter_context(nc.Block())

        @block.sync
        def _(sp):
            sp.dma_start(n_all[:].rearrange("p n h j -> p (n h j)"), T["n0"]).then_inc(state_in, 16)
            for n in range(N):
                sp.dma_start(m_all[n * DSEQ:(n + 1) * DSEQ, :], T["m0"][n:n + 1, :].to_broadcast([DSEQ, H])
                             ).then_inc(state_in, 16)
            sp.wait_ge(set_up, 2)
            with sp.Fori(0, H) as h:
                sp.wait_ge(c_set, h * 2 * N)
                sp.wait_ge(y_head, h)
                for buf, col in ((q, C_QM), (k, C_KM), (o, C_OM)):
                    sp.dma_start(buf[:], z[rows, bass.ds(h * DM + col, DM)]).then_inc(z_in, 16)
                sp.dma_start(v[:, 0:DM], z[rows, bass.ds(h * DM + C_VM, DM)]).then_inc(z_in, 16)
                sp.wait_ge(c_out, h * N * 16)
                for n in range(N):
                    sp.dma_start(C[:, n, :, 0:DM], T["C0"][n, bass.ds(h, 1)].rearrange("a (j p) e -> p (a j) e", p=P)
                                 ).then_inc(c_in, 16)
                sp.wait_ge(y_head, h + 1)
                sp.dma_start(T["ycat"][rows, bass.ds(h * DM, DM)], y[:]).then_inc(y_out, 16)
                for n in range(N):
                    sp.wait_ge(c_set, h * 2 * N + 2 * n + 2)
                    sp.dma_start(T["mC_s"][n, bass.ds(h, 1)].rearrange("a (j p) e -> p (a j) e", p=P),
                                 C[:, n, :, 0:DM]).then_inc(c_out, 16)
            sp.wait_ge(c_out, H * N * 16)
            sp.wait_ge(y_out, H * 16)
            sp.wait_ge(c_cols, 2 * H)
            sp.dma_start(T["mn_s"], n_new[:].rearrange("p n h j -> p (n h j)")).then_inc(outs, 16)
            sp.dma_start(T["mm_s"], m_new[0:P:DSEQ, :]).then_inc(outs, 16)
            sp.wait_ge(outs, 32)

        @block.tensor
        def _(pe):
            with pe.Fori(0, H) as i:
                pe.wait_ge(gates_in, i + 1)
                pe.wait_ge(last_set, i * 2)
                pe.matmul(g_ps[:, 0:1], K["btri"][:], g2[:, 1:2], start=True, stop=True).then_inc(summed, 1)
                pe.wait_ge(z_in, i * 64 + 64)
                pe.wait_ge(turned_out, i * 2)
                for c in range(4):
                    mm = pe.transpose(t_ps[:, c * P:(c + 1) * P], (q, k)[c // 2][:, c % 2 * P:(c % 2 + 1) * P],
                                      K["ident"][:])
                mm.then_inc(turned, 1)
                pe.wait_ge(dx_set, i + 1)
                pe.wait_ge(wd_set, i)
                pe.matmul(e_ps[:, 0:P], K["ones"][:], dx[:, 0, :], start=True, stop=False)
                pe.matmul(e_ps[:, 0:P], K["ident"][:], K["bmask"][:], start=False, stop=True).then_inc(rows_e, 1)
                pe.wait_ge(turned_out, i * 2 + 2)
                pe.wait_ge(mixed, i)
                for j in range(2):
                    mm = pe.matmul(s_ps[:, 0:P], kT[:, j, :], qT[:, j, :], start=(j == 0), stop=(j == 1))
                mm.then_inc(scored, 1)
                pe.wait_ge(m_set, i + 1)
                pe.matmul(g_ps[:, 2:4], K["blast"][:], Mm[:], start=True, stop=True).then_inc(summed, 1)
                pe.wait_ge(dm_set, i + 1)
                pe.matmul(e_ps[:, 0:P], K["negones"][:], dM[:, 0, :], start=True, stop=False)
                pe.matmul(e_ps[:, 0:P], K["ident"][:], K["bmaskT"][:], start=False, stop=True).then_inc(rows_m, 1)
                pe.wait_ge(wp_set, i + 1)
                pe.matmul(g_ps[:, 8:8 + N], K["ones"][:], wp[:], start=True, stop=True).then_inc(summed, 1)
                pe.wait_ge(mixed, i + 1)
                pe.wait_ge(y_head, i)
                pe.matmul(n1_ps[:, 0:DA], A[:], v[:], start=True, stop=True)
                pe.wait_ge(placed, i + 1)
                pe.wait_ge(c_in, i * N * 16 + N * 16)
                pe.wait_ge(c_cols, i * 2 + 1)
                for n in range(N):
                    for j in range(2):
                        mm = pe.matmul(n2_ps[:, 0:DA], qd[:, j, n * P:(n + 1) * P], C[:, n, j, :],
                                       start=(n + j == 0), stop=(n == N - 1 and j == 1))
                mm.then_inc(n_ready, 1)
                for n in range(N):
                    pe.wait_ge(kw_set, i * N + n + 1)
                    pe.wait_ge(c_set, i * 2 * N + 2 * n)
                    for j, cb in enumerate((c0_ps, c1_ps)):
                        mm = pe.matmul(cb[:, 0:DA], kw[:, n % 2, j * P:(j + 1) * P], v[:], start=True, stop=True)
                    mm.then_inc(c_summed, 1)

        @block.vector
        def _(dve):
            dve.memset(qd[:], 0.0).then_inc(set_up, 1)
            dve.memset(v[:, DM:DA], 1.0).then_inc(set_up, 1)
            dve.wait_ge(set_up, 2)
            dve.wait_ge(state_in, 16 * (N + 1))
            with dve.Fori(0, H) as i:
                ch = Chain(dve, chain, i, DVE_STEPS, K["passed"])
                dve.wait_ge(w2_set, i)
                dve.wait_ge(wd_set, i)
                ch(dve.tensor_copy(g2[:, 0:1], gates[:, PT, bass.ds(i, 1)]))
                ch(dve.tensor_copy(m[:], m_all[:, bass.ds(i, 1)]))
                dve.wait_ge(summed, i * 3)
                dve.tensor_copy(g2[:, 1:2], gates[:, PT, bass.ds(i + H, 1)]).then_inc(gates_in, 1)
                dve.wait_ge(summed, i * 3 + 1)
                ch(dve.tensor_tensor(x[:], g2[:, 0:1], g_ps[:, 0:1], ALU.subtract))
                ch(dve.tensor_copy(b[:], g_ps[:, 0:1]))
                eye_times(dve, K, dx[:], x[:], 1).then_inc(dx_set, 1)
                dve.wait_ge(rows_e, i + 1)
                ch(dve.tensor_reduce(rmax[:], e_ps[:, 0:P], AX.X, ALU.max))
                ch(dve.tensor_tensor(Mm[:, 0:1], rmax[:], m[:], ALU.max))
                dve.tensor_tensor(Mm[:, 1:2], b[:], Mm[:, 0:1], ALU.add).then_inc(m_set, 1)
                dve.wait_ge(m_set, i + 1)
                ch(dve.tensor_tensor(e1[:, 0:1], m[:], Mm[:, 0:1], ALU.subtract))
                ch(dve.tensor_scalar(e1[:, 1:2], Mm[:, 1:2], -1.0, None, ALU.mult))
                eye_times(dve, K, dM[:], Mm[:, 0:1], 1).then_inc(dm_set, 1)
                dve.wait_ge(summed, i * 3 + 2)
                dve.tensor_copy(Ml[:], g_ps[:, 2:4]).then_inc(last_set, 1)
                dve.wait_ge(last_set, i * 2 + 1)
                ch(dve.tensor_tensor(e2[:, 0:1], m[:], Ml[:, 0:1], ALU.subtract))
                dve.tensor_tensor(e2[:, 1:2], x[:], Ml[:, 0:1], ALU.subtract).then_inc(e2_set, 1)
                ch(dve.tensor_copy(m_new[:, bass.ds(i, 1)], Ml[:, 1:2]))
                dve.wait_ge(w2_set, i + 1)
                dve.tensor_scalar(wp[:], K["pick"][:], w2[:, 0:1], None, ALU.mult).then_inc(wp_set, 1)
                dve.wait_ge(turned_out, i * 2 + 2)
                dve.wait_ge(n_ready, i)
                dve.tensor_copy(diag8(qd), qT[:].rearrange("p j (n t) -> p j n t", n=N)).then_inc(placed, 1)
                dve.wait_ge(c_in, i * N * 16 + N * 16)
                dve.tensor_copy(C[:, :, :, DM], n_all[:, :, bass.ds(i, 1), :].rearrange("p n a j -> p n (a j)")
                                ).then_inc(c_cols, 1)
                dve.wait_ge(scored, i + 1)
                dve.wait_ge(wd_set, i + 1)
                dve.tensor_tensor(A[:], s_ps[:, 0:P], wD[:], ALU.mult).then_inc(mixed, 1)
                dve.wait_ge(summed, i * 3 + 3)
                dve.tensor_copy(wc[:], g_ps[:, 8:8 + N]).then_inc(last_set, 1)
                dve.wait_ge(last_set, i * 2 + 2)
                ch(dve.tensor_scalar(kws[:], k[:], w2[:, 1:2], KS, ALU.mult, ALU.mult))
                dve.wait_ge(inter_set, i + 1)
                ch(dve.tensor_tensor(num[:], n1_ps[:, 0:DA], inter[:], ALU.add))
                ch(dve.scalar_tensor_tensor(out=den[:], in0=num[:, DM:DA], scalar=-1.0, in1=w1[:, 1:2], op0=ALU.mult,
                                            op1=ALU.max))
                ch(dve.tensor_tensor(den[:], den[:], num[:, DM:DA], ALU.max))
                ch(dve.reciprocal(inv[:], den[:]))
                dve.wait_ge(o_set, i + 1)
                dve.wait_ge(y_out, i * 16)
                dve.scalar_tensor_tensor(out=y[:], in0=num[:, 0:DM], scalar=inv[:], in1=so[:], op0=ALU.mult,
                                         op1=ALU.mult).then_inc(y_head, 1)
                ch(dve.tensor_copy(den[:], inv[:]))
                for n in range(N + 1):
                    if n < N:
                        if n >= 2:
                            dve.wait_ge(c_summed, i * N + n - 1)
                        dve.tensor_scalar(kw[:, n % 2, :], kws[:], K["inblock"][:, n:n + 1], None, ALU.mult
                                          ).then_inc(kw_set, 1)
                    if n >= 1:
                        r = n - 1
                        dve.wait_ge(c_summed, i * N + r + 1)
                        for j, cb in enumerate((c0_ps, c1_ps)):
                            dve.scalar_tensor_tensor(out=C[:, r, j, :], in0=C[:, r, j, :], scalar=wc[:, r:r + 1],
                                                     in1=cb[:, 0:DA], op0=ALU.mult, op1=ALU.add).then_inc(c_set, 1)
                dve.wait_ge(c_set, i * 2 * N + 2 * N)
                dve.tensor_copy(n_new[:, :, bass.ds(i, 1), :].rearrange("p n a j -> p n (a j)"), C[:, :, :, DM]
                                ).then_inc(c_cols, 1)
                dve.wait_ge(c_cols, i * 2 + 2)
                ch.close()

        @block.scalar
        def _(act):
            with act.Fori(0, H) as i:
                act.wait_ge(turned, i + 1)
                act.wait_ge(placed, i)
                act.wait_ge(scored, i)
                for g, dst in enumerate((qT, kT)):
                    act.mul(dst[:].rearrange("p c t -> p (c t)"), t_ps[:, g * 2 * P:(g + 1) * 2 * P], (1.0, KS)[g]
                            ).then_inc(turned_out, 1)
                act.wait_ge(chain, i * DVE_STEPS + 8)
                act.activation(w1[:], e1[:], ACT.Exp).then_inc(w1_set, 1)
                act.wait_ge(rows_m, i + 1)
                act.wait_ge(mixed, i)
                act.activation(wD[:], e_ps[:, 0:P], ACT.Exp, bias=x[:]).then_inc(wd_set, 1)
                act.wait_ge(e2_set, i + 1)
                act.activation(w2[:], e2[:], ACT.Exp).then_inc(w2_set, 1)
                act.wait_ge(z_in, i * 64 + 64)
                act.wait_ge(y_head, i)
                act.activation(so[:], o[:], ACT.Sigmoid).then_inc(o_set, 1)
                act.wait_ge(w1_set, i + 1)
                act.wait_ge(n_ready, i + 1)
                act.activation(inter[:], n2_ps[:, 0:DA], ACT.Copy, scale=w1[:, 0:1]).then_inc(inter_set, 1)


def diag8(qd):
    v = qd[:]
    return bass.AP(tensor=v.tensor, offset=v.offset,
                   ap=[v.ap[0], [NSEQ * P, 2], [P + DSEQ, NSEQ], [1, DSEQ]])


def stage_merge(nc, K, x, z, gain_row, w_br_m, w_br_f, w_out, T):
    with Stage(nc, "mrg") as st:
        wm, wf, wo = (st.sb(n, [P, KD, D]) for n in ("wm", "wf", "wo"))
        gb = st.sb("gb", [P, D])
        yc, yT, gz = st.sb("yc", [P, 2 * D]), st.sb("yT", [P, 2 * KD, P]), st.sb("gz", [P, 2 * D])
        mg, mT, xt, h, xp = (st.sb(n, [P, D]) for n in ("mg", "mT", "xt", "h", "xp"))
        ss, ms, rt, rs = (st.sb(n, [P, 1]) for n in ("ss", "ms", "rt", "rs"))
        t_ps = [st.ps(f"t{n}", [P, 512]) for n in range(2)]
        m_ps, f_ps, o_ps = (st.ps(n, [P, D]) for n in ("m", "f", "o"))
        (w_in, y_in, g_in, x_in, turned, turned_out, branched, gated, merged, projected, h_set, squared,
         meaned, rooted, inverted, xp_set) = st.sems(
            "w_in y_in g_in x_in turned turned_out branched gated merged projected h_set squared "
            "meaned rooted inverted xp_set")
        stored = st.pool_sem("stored")
        block = st.ctx.enter_context(nc.Block())

        @block.sync
        def _(sp):
            for t, w in ((wm, w_br_m), (wf, w_br_f), (wo, w_out)):
                sp.dma_start(t[:], w.rearrange("(k p) n -> p k n", p=P)).then_inc(w_in, 16)
            sp.dma_start(gb[:], gain_row.to_broadcast([P, D])).then_inc(w_in, 16)
            with sp.Fori(0, NT) as i:
                rows = bass.ts(i, P)
                sp.wait_ge(turned, i * 6)
                sp.dma_start(yc[:], T["ycat"][rows, :]).then_inc(y_in, 16)
                sp.wait_ge(merged, i * 3)
                sp.dma_start(gz[:], z[rows, C_GM:IN_COLS]).then_inc(g_in, 16)
                sp.wait_ge(h_set, i)
                sp.dma_start(xt[:], x[rows, :]).then_inc(x_in, 16)

        @block.gpsimd
        def _(pool):
            with pool.Fori(0, NT) as i:
                rows = bass.ts(i, P)
                pool.wait_ge(h_set, i + 1)
                pool.dma_start(T["h"][rows, :], h[:]).then_inc(stored, 16)
                hold(pool, xp_set, i + 1, K["passed"])
                pool.dma_start(T["xp"][rows, :], xp[:]).then_inc(stored, 16)
            pool.wait_ge(stored, NT * 32)

        @block.tensor
        def _(pe):
            with pe.Fori(0, NT) as i:
                pe.wait_ge(y_in, i * 16 + 16)
                for g in range(4):
                    pe.wait_ge(turned_out, i * 6 + max(g - 1, 0))
                    for c in range(4):
                        mm = pe.transpose(t_ps[g % 2][:, c * P:(c + 1) * P], yc[:, (4 * g + c) * P:(4 * g + c + 1) * P],
                                          K["ident"][:])
                    mm.then_inc(turned, 1)
                pe.wait_ge(w_in, 64)
                for u, (w, acc) in enumerate(((wm, m_ps), (wf, f_ps))):
                    pe.wait_ge(turned_out, i * 6 + 2 * u + 2)
                    for n in range(2):
                        for k in range(KD):
                            mm = pe.matmul(acc[:, n * 512:(n + 1) * 512], yT[:, u * KD + k, :],
                                           w[:, k, n * 512:(n + 1) * 512], start=(k == 0), stop=(k == KD - 1))
                    mm.then_inc(branched, 1)
                pe.wait_ge(merged, i * 3 + 3)
                for g in range(2):
                    for c in range(4):
                        mm = pe.transpose(t_ps[g][:, c * P:(c + 1) * P], mg[:, (4 * g + c) * P:(4 * g + c + 1) * P],
                                          K["ident"][:])
                    mm.then_inc(turned, 1)
                pe.wait_ge(h_set, i)
                pe.wait_ge(turned_out, i * 6 + 6)
                for n in range(2):
                    for k in range(KD):
                        mm = pe.matmul(o_ps[:, n * 512:(n + 1) * 512], mT[:, k * P:(k + 1) * P],
                                       wo[:, k, n * 512:(n + 1) * 512], start=(k == 0), stop=(k == KD - 1))
                mm.then_inc(projected, 1)

        @block.scalar
        def _(act):
            with act.Fori(0, NT) as i:
                for g in range(4):
                    act.wait_ge(turned, i * 6 + g + 1)
                    act.copy(yT[:, 4 * g:4 * g + 4, :].rearrange("p c t -> p (c t)"), t_ps[g % 2][:]
                             ).then_inc(turned_out, 1)
                act.wait_ge(g_in, i * 16 + 16)
                act.activation(gz[:], gz[:], ACT.Sigmoid).then_inc(gated, 1)
                for g in range(2):
                    act.wait_ge(turned, i * 6 + g + 5)
                    act.wait_ge(projected, i)
                    act.copy(mT[:, g * 512:(g + 1) * 512], t_ps[g][:]).then_inc(turned_out, 1)
                act.wait_ge(h_set, i + 1)
                act.wait_ge(stored, i * 32)
                act.activation(xp[:], h[:], ACT.Square, accum_out=ss[:]).then_inc(squared, 1)
                act.wait_ge(meaned, i + 1)
                act.activation(rt[:], ms[:], ACT.Sqrt).then_inc(rooted, 1)

        @block.vector
        def _(dve):
            dve.wait_ge(w_in, 64)
            with dve.Fori(0, NT) as i:
                dve.wait_ge(gated, i + 1)
                dve.wait_ge(turned, i * 6)
                dve.wait_ge(branched, i * 2 + 1)
                dve.tensor_tensor(mg[:], m_ps[:], gz[:, 0:D], ALU.mult).then_inc(merged, 1)
                dve.wait_ge(branched, i * 2 + 2)
                dve.tensor_tensor(gz[:, D:2 * D], f_ps[:], gz[:, D:2 * D], ALU.mult).then_inc(merged, 1)
                dve.wait_ge(merged, i * 3 + 2)
                dve.tensor_tensor(mg[:], mg[:], gz[:, D:2 * D], ALU.add).then_inc(merged, 1)
                dve.wait_ge(projected, i + 1)
                dve.wait_ge(x_in, i * 16 + 16)
                dve.wait_ge(stored, i * 32)
                dve.tensor_tensor(h[:], o_ps[:], xt[:], ALU.add).then_inc(h_set, 1)
                dve.wait_ge(squared, i + 1)
                dve.tensor_scalar(ms[:], ss[:], 1.0 / D, EPS, ALU.mult, ALU.add).then_inc(meaned, 1)
                dve.wait_ge(rooted, i + 1)
                dve.reciprocal(rs[:], rt[:]).then_inc(inverted, 1)
                dve.wait_ge(inverted, i + 1)
                dve.scalar_tensor_tensor(out=xp[:], in0=h[:], scalar=rs[:], in1=gb[:], op0=ALU.mult, op1=ALU.mult
                                         ).then_inc(xp_set, 1)


def stage_queries(nc, K, w_q, keys, idx, gate, T):
    with Stage(nc, "qry") as st:
        NB = 2 * PH
        w = st.sb("w", [P, KD, PH * PDQ])
        kT = st.sb("kT", [P, NB, PKEYS])
        xp, xT = st.sb("xp", [P, D]), st.sb("xT", [P, KD, P])
        qT = st.sb("qT", [P, NB, P])
        sc = st.sb("sc", [P, NB, PKEYS])
        left = st.sb("left", [P, NB, PKEYS])
        best, where, wheref = st.sb("best", [P, NB, TOPK]), st.sb("where", [P, NB, TOPK], U32), st.sb(
            "wheref", [P, NB, TOPK])
        cand, cleft = st.sb("cand", [P, PH, TOPK, TOPK]), st.sb("cleft", [P, PH, TOPK, TOPK])
        top, pos = st.sb("top", [P, PH, TOPK]), st.sb("pos", [P, PH, TOPK], U32)
        part = st.sb("part", [P, 2, PH, TOPK], U32)
        partf = st.sb("partf", [P, 2, PH, TOPK])
        picked = st.sb("picked", [P, 2, PH, TOPK])
        flat = st.sb("flat", [P, EXPERTS])
        ramp_i, ramp = st.sb("ramp_i", [P, TOPK], mybir.dt.int32), st.sb("ramp", [P, TOPK])
        ex, tot, itot = st.sb("ex", [P, PH, TOPK]), st.sb("tot", [P, PH]), st.sb("itot", [P, PH])
        t_ps = [st.ps(f"t{n}", [P, 512]) for n in range(2)]
        q_ps = [st.ps(f"q{n}", [P, 512]) for n in range(2)]
        s_ps = st.ps("s", [P, NB * PKEYS])
        (w_in, ramp_set, x_in, turned, turned_out, queried, q_out, scored, s_out, chain, shifted, expd) = st.sems(
            "w_in ramp_set x_in turned turned_out queried q_out scored s_out chain shifted expd")
        STEPS = 17
        block = st.ctx.enter_context(nc.Block())

        @block.sync
        def _(sp):
            sp.dma_start(w[:], w_q.rearrange("(k p) n -> p k n", p=P)).then_inc(w_in, 16)
            sp.dma_start(kT[:], keys).then_inc(w_in, 16)
            with sp.Fori(0, NT) as i:
                sp.wait_ge(turned, i * 2)
                sp.dma_start(xp[:], T["xp"][bass.ts(i, P), :]).then_inc(x_in, 16)

        @block.gpsimd
        def _(pool):
            pool.iota(ramp_i[:], pattern=[[1, TOPK]], base=0, channel_multiplier=0).then_inc(ramp_set, 1)

        @block.tensor
        def _(pe):
            pe.wait_ge(w_in, 32)
            with pe.Fori(0, NT) as i:
                pe.wait_ge(x_in, i * 16 + 16)
                pe.wait_ge(turned_out, i * 2)
                for g in range(2):
                    for c in range(4):
                        mm = pe.transpose(t_ps[g][:, c * P:(c + 1) * P], xp[:, (4 * g + c) * P:(4 * g + c + 1) * P],
                                          K["ident"][:])
                    mm.then_inc(turned, 1)
                pe.wait_ge(turned_out, i * 2 + 2)
                for g in range(4):
                    pe.wait_ge(q_out, i * 4 + max(g - 1, 0))
                    for c in range(4):
                        for k in range(KD):
                            mm = pe.matmul(q_ps[g % 2][:, c * P:(c + 1) * P], w[:, k, (4 * g + c) * P:(4 * g + c + 1) * P],
                                           xT[:, k, :], start=(k == 0), stop=(k == KD - 1))
                    mm.then_inc(queried, 1)
                pe.wait_ge(q_out, i * 4 + 4)
                pe.wait_ge(s_out, i)
                for c in range(NB):
                    mm = pe.matmul(s_ps[:, c * PKEYS:(c + 1) * PKEYS], qT[:, c, :], kT[:, c, :], start=True, stop=True)
                mm.then_inc(scored, 1)

        @block.scalar
        def _(act):
            with act.Fori(0, NT) as i:
                for g in range(2):
                    act.wait_ge(turned, i * 2 + g + 1)
                    act.wait_ge(queried, i * 4)
                    act.copy(xT[:, 4 * g:4 * g + 4, :].rearrange("p c t -> p (c t)"), t_ps[g][:]
                             ).then_inc(turned_out, 1)
                for g in range(4):
                    act.wait_ge(queried, i * 4 + g + 1)
                    act.wait_ge(scored, i)
                    act.copy(qT[:, 4 * g:4 * g + 4, :].rearrange("p c t -> p (c t)"), q_ps[g % 2][:]
                             ).then_inc(q_out, 1)
                act.wait_ge(scored, i + 1)
                act.wait_ge(chain, i * STEPS)
                act.copy(sc[:].rearrange("p b k -> p (b k)"), s_ps[:]).then_inc(s_out, 1)
                act.wait_ge(shifted, i + 1)
                act.activation(ex[:], ex[:], ACT.Exp).then_inc(expd, 1)

        @block.vector
        def _(dve):
            dve.wait_ge(ramp_set, 1)
            dve.tensor_copy(ramp[:], ramp_i[:]).then_inc(ramp_set, 1)
            dve.wait_ge(ramp_set, 2)
            with dve.Fori(0, NT) as i:
                ch = Chain(dve, chain, i, STEPS, K["passed"])
                hold(dve, s_out, i + 1, K["passed"])

                def top16(values, rest, out, at, blocks):
                    for c in range(blocks):
                        ins = dve.max(out=out[:, c, 0:8], in_=values(c))
                    ch(ins)
                    for c in range(blocks):
                        dve.max_index(out=at[:, c, 0:8], in_max=out[:, c, 0:8], in_values=values(c))
                        ins = dve.match_replace(out=rest(c), in_to_replace=out[:, c, 0:8], in_values=values(c),
                                                imm_value=-3.0e38)
                    ch(ins)
                    for c in range(blocks):
                        ins = dve.max(out=out[:, c, 8:16], in_=rest(c))
                    ch(ins)
                    for c in range(blocks):
                        ins = dve.max_index(out=at[:, c, 8:16], in_max=out[:, c, 8:16], in_values=rest(c))
                    ch(ins)

                top16(lambda c: sc[:, c, :], lambda c: left[:, c, :], best, where, NB)
                dve.tensor_copy(wheref[:], where[:])
                b4 = best[:].rearrange("p (h s) k -> p h s k", s=2)
                ch(dve.tensor_tensor(cand[:], b4[:, :, 0, :].unsqueeze(3).to_broadcast([P, PH, TOPK, TOPK]),
                                     b4[:, :, 1, :].unsqueeze(2).to_broadcast([P, PH, TOPK, TOPK]), ALU.add))
                as_row = lambda t: (lambda c: t[:, c].rearrange("p a b -> p (a b)"))
                top16(as_row(cand), as_row(cleft), top, pos, PH)
                dve.tensor_tensor(ex[:], top[:], bc(top[:, :, 0], [P, PH, TOPK]), ALU.subtract).then_inc(shifted, 1)
                dve.tensor_scalar(part[:, 0], pos[:], 4, None, ALU.logical_shift_right)
                ch(dve.tensor_scalar(part[:, 1], pos[:], TOPK - 1, None, ALU.bitwise_and))
                ch(dve.tensor_copy(partf[:], part[:]))
                w4 = wheref[:].rearrange("p (h s) k -> p h s k", s=2)
                for s, buf in enumerate((cand, cleft)):
                    dve.tensor_tensor(buf[:].rearrange("p h a b -> p (h a) b"),
                                      ramp[:].unsqueeze(1).to_broadcast([P, EXPERTS, TOPK]),
                                      bc(partf[:, s].rearrange("p h k -> p (h k)"), [P, EXPERTS, TOPK]), ALU.is_equal
                                      ).then_inc(chain, 1)
                ch.n += 2
                dve.wait_ge(chain, i * STEPS + ch.n)
                for s, buf in enumerate((cand, cleft)):
                    ins = dve.tensor_tensor(buf[:], buf[:], w4[:, :, s, :].unsqueeze(2).to_broadcast(
                        [P, PH, TOPK, TOPK]), ALU.mult)
                ch(ins)
                for s, buf in enumerate((cand, cleft)):
                    ins = dve.tensor_reduce(picked[:, s], buf[:], AX.X, ALU.add)
                dve.wait_ge(expd, i + 1)
                ins = dve.tensor_reduce(tot[:], ex[:], AX.X, ALU.add)
                ch(ins)
                dve.scalar_tensor_tensor(out=flat[:], in0=picked[:, 0].rearrange("p h k -> p (h k)"),
                                         scalar=float(PKEYS), in1=picked[:, 1].rearrange("p h k -> p (h k)"),
                                         op0=ALU.mult, op1=ALU.add)
                ch(dve.reciprocal(itot[:], tot[:]))
                dve.tensor_copy(idx[:, bass.ds(i, 1), :].rearrange("p a k -> p (a k)"), flat[:])
                dve.tensor_tensor(gate[:, bass.ds(i, 1), :].rearrange("p a (h k) -> p (a h) k", h=PH), ex[:],
                                  bc(itot[:], [P, PH, TOPK]), ALU.mult).then_inc(chain, 1)
                ch.n += 1
                dve.wait_ge(chain, i * STEPS + ch.n)
                ch.close()


def stage_experts(nc, K, idx, gate, u_tab, v_tab, T):
    with Stage(nc, "exp") as st:
        G = 8
        NGR = EXPERTS // G
        u, v = st.sb("u", [P, G, D]), st.sb("v", [P, G, D])
        xp = st.sb("xp", [P, D])
        acc = st.sb("acc", [P, 2, D])
        here = st.sb("here", [P, 2, G], U32)
        dot, act8, wt = st.sb("dot", [P, 2, G]), st.sb("act8", [P, 2, G]), st.sb("wt", [P, 2, G])
        x_in, a_in, zeroed, indexed, dotted, geluted, weighed, added, joined, stored = st.sems(
            "x_in a_in zeroed indexed dotted geluted weighed added joined stored")
        u_in = [st.pool_sem(f"u_in{j}") for j in range(G)]
        v_in = [st.pool_sem(f"v_in{j}") for j in range(G)]
        block = st.ctx.enter_context(nc.Block())

        @block.sync
        def _(sp):
            with sp.Fori(0, NT) as t:
                rows = bass.ts(t, P)
                sp.wait_ge(dotted, t * EXPERTS + G)
                sp.dma_start(xp[:], T["xp"][rows, :]).then_inc(x_in, 16)
                sp.wait_ge(stored, t * 16)
                sp.dma_start(acc[:, 0, :], T["h"][rows, :]).then_inc(a_in, 16)
                sp.wait_ge(joined, t + 1)
                sp.dma_start(T["h2"][rows, :], acc[:, 0, :]).then_inc(stored, 16)
            sp.wait_ge(stored, NT * 16)

        @block.gpsimd
        def _(pool):
            with pool.Fori(0, NT) as t:
                with pool.Fori(0, NGR // 2) as m:
                    for p in range(2):
                        n = (t * NGR + m * 2 + p) * G
                        pool.wait_ge(added, n)
                        pool.tensor_copy(here[:, p, :], idx[:, bass.ds(t, 1), bass.ds(m * (2 * G) + p * G, G)]
                                         .rearrange("p a k -> p (a k)")).then_inc(indexed, 1)
                        pool.wait_ge(indexed, t * NGR + m * 2 + (p + 1))
                        for j in range(G):
                            hold(pool, dotted, n + (j + 1), K["passed"])
                            pool.indirect_dma_start(u[:, j, :], None, u_tab, bass.IndirectOffsetOnAxis(
                                ap=here[:, p, j:j + 1], axis=0)).then_inc(u_in[j], 16)
                            hold(pool, added, n + (j + 1), K["passed"])
                            pool.indirect_dma_start(v[:, j, :], None, v_tab, bass.IndirectOffsetOnAxis(
                                ap=here[:, p, j:j + 1], axis=0)).then_inc(v_in[j], 16)

        @block.vector
        def _(dve):
            dve.sem_inc(dotted, G)
            dve.sem_inc(added, G)
            with dve.Fori(0, NT) as t:
                dve.wait_ge(joined, t)
                dve.memset(acc[:, 1, :], 0.0).then_inc(zeroed, 1)
                dve.wait_ge(zeroed, t + 1)
                dve.wait_ge(x_in, t * 16 + 16)
                hold(dve, a_in, t * 16 + 16, K["passed"])
                with dve.Fori(0, NGR // 2) as m:
                    for p in range(2):
                        g = t * NGR + m * 2 + p
                        for j in range(G):
                            dve.wait_ge(u_in[j], g * 16 + 16)
                            dve.tensor_tensor_reduce(u[:, j, :], u[:, j, :], xp[:], 1.0, 0.0, ALU.mult, ALU.add,
                                                     dot[:, p, j:j + 1]).then_inc(dotted, 1)
                        dve.wait_ge(geluted, g + 1)
                        dve.tensor_tensor(wt[:, p, :], act8[:, p, :],
                                          gate[:, bass.ds(t, 1), bass.ds(m * (2 * G) + p * G, G)]
                                          .rearrange("p a k -> p (a k)"), ALU.mult).then_inc(weighed, 1)
                        dve.wait_ge(weighed, g + 1)
                        for j in range(G):
                            dve.wait_ge(v_in[j], g * 16 + 16)
                            dve.wait_ge(added, g * G + (j + G - 1))
                            dve.scalar_tensor_tensor(out=acc[:, j % 2, :], in0=v[:, j, :], scalar=wt[:, p, j:j + 1],
                                                     in1=acc[:, j % 2, :], op0=ALU.mult, op1=ALU.add
                                                     ).then_inc(added, 1)
                dve.wait_ge(added, t * EXPERTS + (EXPERTS + G))
                dve.tensor_tensor(acc[:, 0, :], acc[:, 0, :], acc[:, 1, :], ALU.add).then_inc(joined, 1)

        @block.scalar
        def _(act):
            with act.Fori(0, NT) as t:
                with act.Fori(0, NGR // 2) as m:
                    for p in range(2):
                        g = t * NGR + m * 2 + p
                        act.wait_ge(dotted, g * G + 2 * G)
                        act.wait_ge(weighed, g)
                        act.activation(act8[:, p, :], dot[:, p, :], ACT.Gelu).then_inc(geluted, 1)


def stage_ple(nc, K, g_cols, w_gate, w_proj, gain_row, pT, T):
    with Stage(nc, "ple") as st:
        wg, wp = st.sb("wg", [P, KD, D]), st.sb("wp", [P, 2, D])
        gc, gb = st.sb("gc", [P, KD]), st.sb("gb", [P, D])
        h, sq, en, eT, pt = st.sb("h", [P, D]), st.sb("sq", [P, D]), st.sb("en", [P, D]), st.sb(
            "eT", [P, KD, P]), st.sb("pt", [P, 2, P])
        sg, h3, y = st.sb("sg", [P, D]), st.sb("h3", [P, D]), st.sb("y", [P, D])
        ss, ms, rt, rs = (st.sb(n, [P, 2]) for n in ("ss", "ms", "rt", "rs"))
        t_ps, g_ps, p_ps = (st.ps(n, [P, D]) for n in ("t", "g", "p"))
        (w_in, h_in, p_in, squared, meaned, rooted, inverted, normed, turned, turned_out, gated, projected, sig_set,
         scaled, h3_set, y_set) = st.sems(
            "w_in h_in p_in squared meaned rooted inverted normed turned turned_out gated projected sig_set "
            "scaled h3_set y_set")
        stored = st.pool_sem("stored")
        block = st.ctx.enter_context(nc.Block())

        @block.sync
        def _(sp):
            sp.dma_start(gc[:], g_cols).then_inc(w_in, 16)
            sp.dma_start(wg[:], w_gate.rearrange("(k p) n -> p k n", p=P)).then_inc(w_in, 16)
            sp.dma_start(wp[:], w_proj.rearrange("(k p) n -> p k n", p=P)).then_inc(w_in, 16)
            sp.dma_start(gb[:], gain_row.to_broadcast([P, D])).then_inc(w_in, 16)
            with sp.Fori(0, NT) as i:
                sp.wait_ge(h3_set, i)
                sp.dma_start(h[:], T["h2"][bass.ts(i, P), :]).then_inc(h_in, 16)
                hold(sp, projected, i, K["passed"])
                sp.dma_start(pt[:], pT.rearrange("(k p) t -> p k t", p=P)[:, :, bass.ts(i, P)]).then_inc(p_in, 16)

        @block.gpsimd
        def _(pool):
            with pool.Fori(0, NT) as i:
                pool.wait_ge(y_set, i + 1)
                pool.dma_start(T["y"][bass.ts(i, P), :], y[:]).then_inc(stored, 16)
            pool.wait_ge(stored, NT * 16)

        @block.scalar
        def _(act):
            with act.Fori(0, NT) as i:
                act.wait_ge(h_in, i * 16 + 16)
                act.activation(sq[:], h[:], ACT.Square, accum_out=ss[:, 0:1]).then_inc(squared, 1)
                act.wait_ge(meaned, i * 2 + 1)
                act.activation(rt[:, 0:1], ms[:, 0:1], ACT.Sqrt).then_inc(rooted, 1)
                act.wait_ge(inverted, i * 2 + 1)
                act.wait_ge(turned, i)
                act.activation(en[:], h[:], ACT.Copy, scale=rs[:, 0:1]).then_inc(normed, 1)
                act.wait_ge(gated, i + 1)
                act.wait_ge(scaled, i)
                act.activation(sg[:], g_ps[:], ACT.Sigmoid).then_inc(sig_set, 1)
                act.wait_ge(h3_set, i + 1)
                act.activation(sq[:], h3[:], ACT.Square, accum_out=ss[:, 1:2]).then_inc(squared, 1)
                act.wait_ge(meaned, i * 2 + 2)
                act.activation(rt[:, 1:2], ms[:, 1:2], ACT.Sqrt).then_inc(rooted, 1)

        @block.tensor
        def _(pe):
            with pe.Fori(0, NT) as i:
                pe.wait_ge(normed, i + 1)
                pe.wait_ge(turned_out, i)
                for k in range(KD):
                    mm = pe.transpose(t_ps[:, k * P:(k + 1) * P], en[:, k * P:(k + 1) * P], K["ident"][:])
                mm.then_inc(turned, 1)
                pe.wait_ge(w_in, 64)
                pe.wait_ge(p_in, i * 16 + 16)
                pe.wait_ge(scaled, i)
                for n in range(2):
                    for k in range(2):
                        mm = pe.matmul(p_ps[:, n * 512:(n + 1) * 512], pt[:, k, :], wp[:, k, n * 512:(n + 1) * 512],
                                       start=(k == 0), stop=(k == 1))
                mm.then_inc(projected, 1)
                pe.wait_ge(turned_out, i + 1)
                pe.wait_ge(sig_set, i)
                for n in range(2):
                    for k in range(KD):
                        mm = pe.matmul(g_ps[:, n * 512:(n + 1) * 512], eT[:, k, :], wg[:, k, n * 512:(n + 1) * 512],
                                       start=(k == 0), stop=(k == KD - 1))
                mm.then_inc(gated, 1)

        @block.vector
        def _(dve):
            dve.wait_ge(w_in, 64)
            with dve.Fori(0, NT) as i:
                def invert(c):
                    dve.wait_ge(squared, i * 2 + c + 1)
                    dve.tensor_scalar(ms[:, c:c + 1], ss[:, c:c + 1], 1.0 / D, EPS, ALU.mult, ALU.add
                                      ).then_inc(meaned, 1)
                    dve.wait_ge(rooted, i * 2 + c + 1)
                    dve.reciprocal(rs[:, c:c + 1], rt[:, c:c + 1]).then_inc(inverted, 1)

                invert(0)
                dve.wait_ge(turned, i + 1)
                dve.tensor_tensor(eT[:], t_ps[:].rearrange("p (k t) -> p k t", k=KD), bc(gc[:], [P, KD, P]), ALU.mult
                                  ).then_inc(turned_out, 1)
                dve.wait_ge(sig_set, i + 1)
                dve.wait_ge(projected, i + 1)
                dve.tensor_tensor(sg[:], sg[:], p_ps[:], ALU.mult).then_inc(scaled, 1)
                dve.wait_ge(scaled, i + 1)
                dve.tensor_tensor(h3[:], h[:], sg[:], ALU.add).then_inc(h3_set, 1)
                invert(1)
                dve.wait_ge(inverted, i * 2 + 2)
                dve.wait_ge(stored, i * 16)
                dve.scalar_tensor_tensor(out=y[:], in0=h3[:], scalar=rs[:, 1:2], in1=gb[:], op0=ALU.mult, op1=ALU.mult
                                         ).then_inc(y_set, 1)


def trunk_kernel(nc, A, O):
    scratch = lambda name, shape: nc.dram_tensor(f"scratch_{name}", shape, F32, kind="Internal").ap()
    z = scratch("z", (TOK, IN_COLS))
    T = dict(O)
    T.update(
        lfT=scratch("lfT", (H_F, TOK)),
        nck=scratch("nck", (H_F, SEQ)),
        ncs=scratch("ncs", (NSEQ, H_F, PAST + DSEQ)),
        ycat=scratch("ycat", (TOK, W_M + W_F)),
        h=scratch("h", (TOK, D)),
        xp=scratch("xp", (TOK, D)),
        h2=scratch("h2", (TOK, D)),
        cache_kT=A["cache_kT"], cache_v=A["cache_v"], C0=A["C0"], n0=A["n0"], m0=A["m0"],
    )
    with ExitStack() as ctx:
        def sb(name, shape, dt=F32):
            return ctx.enter_context(nc.sbuf_tensor(name, shape, dt))

        K = {n: sb(n, [P, P]) for n in ("ident", "ones", "negones", "mask", "maskT", "tri", "bmask", "bmaskT", "btri",
                                        "last", "blast")}
        K["pick"], K["inblock"] = sb("pick", [P, NSEQ]), sb("inblock", [P, NSEQ])
        K["headsel"] = sb("headsel", [H_F, 2, 8, DSEQ])
        K["masknew"] = sb("masknew", [P, DSEQ])
        K["onesrow"] = sb("onesrow", [1, P])
        gates = sb("gates", [P, NT, NG])
        idx, gate = sb("idx", [P, NT, EXPERTS], U32), sb("gate", [P, NT, EXPERTS])
        K["passed"] = ctx.enter_context(nc.semaphore("passed"))
        stage_constants(nc, K)
        with nc.sbuf_tensor("aT", [P, KD, TOK], F32) as aT:
            stage_norm(nc, K, A["x"], A["norm_mix"], aT)
            stage_project(nc, aT, A["w_in"], z)
        stage_gates(nc, K, z, A["gate_bias"], A["cache_lf"], gates, T)
        stage_fox_prompt(nc, K, z, T)
        stage_fox_sample(nc, K, z, T)
        stage_mlstm_prompt(nc, K, z, gates, T)
        stage_mlstm_sample(nc, K, z, gates, T)
        stage_merge(nc, K, A["x"], z, A["norm_ffn"], A["w_br_m"], A["w_br_f"], A["w_out"], T)
        stage_queries(nc, K, A["w_q"], A["keys"], idx, gate, T)
        stage_experts(nc, K, idx, gate, A["u"], A["v"], T)
        stage_ple(nc, K, A["norm_ple"], A["w_ple_gate"], A["w_ple_proj"], A["norm_final"], A["pT"], T)


_OUTS = dict(y=(TOK, D), fox_k=(TOK, W_F), fox_v=(TOK, W_F), fox_lf=(TOK, H_F),
             mC_p=(H_M, DM, DM), mn_p=(P, 2 * H_M), mm_p=(1, H_M),
             mC_s=(NSEQ, H_M, DM, DM), mn_s=(P, NSEQ * H_M * 2), mm_s=(NSEQ, H_M))


def kernel(**inputs):
    import numpy as np
    import concourse.bacc as bacc
    from concourse.bass_utils import run_bass_kernel_spmd

    I = {k: np.asarray(v) for k, v in inputs.items()}
    c = np.ascontiguousarray
    cols = lambda v: c(v.reshape(KD, P).T)
    laid = dict(
        x=np.concatenate([I["x_prompt"].reshape(SEQ, D), I["x_sample"].reshape(-1, D)]),
        pT=c(np.concatenate([I["p_prompt"].reshape(SEQ, -1), I["p_sample"].reshape(NSEQ * DSEQ, -1)]).T),
        norm_mix=cols(I["norm_mix"]), w_in=I["w_in"][0],
        gate_bias=np.concatenate([I["mlstm_b_i"], I["mlstm_b_f"], I["fox_b_f"]], axis=1),
        cache_lf=c(I["cache_fox_logf"][0].transpose(0, 2, 1).reshape(NSEQ * H_F, PAST)),
        cache_kT=c(I["cache_fox_k"][0].transpose(0, 2, 3, 1).reshape(NSEQ, W_F, PAST)),
        cache_v=I["cache_fox_v"][0].reshape(NSEQ, PAST, W_F),
        C0=I["state_mlstm_C"][0], m0=I["state_mlstm_m"][0],
        n0=c(I["state_mlstm_n"][0].reshape(NSEQ, H_M, 2, P).transpose(3, 0, 1, 2).reshape(P, -1)),
        w_br_m=I["w_br_m"][0], w_br_f=I["w_br_f"][0], w_out=I["w_out"][0],
        norm_ffn=I["norm_ffn"], w_q=I["peer_w_q"][0],
        keys=c(np.stack([I["peer_keys1"][0], I["peer_keys2"][0]], axis=1).reshape(2 * PH, PKEYS, P).transpose(2, 0, 1)),
        u=I["peer_u"][0], v=I["peer_v"][0],
        norm_ple=cols(I["norm_ple"]), w_ple_gate=I["w_ple_gate"][0], w_ple_proj=I["w_ple_proj"][0],
        norm_final=I["norm_final"].reshape(1, D),
    )
    nc = bacc.Bacc("TRN2", target_bir_lowering=False, num_devices=1)
    arrays, A, O = {}, {}, {}
    for name, a in laid.items():
        a = c(a)
        arrays[f"in_{name}"] = a
        A[name] = nc.dram_tensor(f"in_{name}", a.shape, mybir.dt.from_np(a.dtype), kind="ExternalInput").ap()
    for name, shape in _OUTS.items():
        O[name] = nc.dram_tensor(f"out_{name}", shape, F32, kind="ExternalOutput").ap()
    trunk_kernel(nc, A, O)
    r = run_bass_kernel_spmd(nc, [arrays], core_ids=[0])
    g = {name: np.asarray(r.results[0][f"out_{name}"]) for name in _OUTS}

    def both(a, *tail):
        return a[:SEQ].reshape(1, 1, SEQ, *tail), a[SEQ:].reshape(1, NSEQ, DSEQ, *tail)

    y_p, y_s = both(g["y"], D)
    k_p, k_s = both(g["fox_k"], H_F, DF)
    v_p, v_s = both(g["fox_v"], H_F, DF)
    l_p, l_s = both(g["fox_lf"], H_F)
    n_p = c(g["mn_p"].reshape(P, H_M, 2).transpose(1, 2, 0)).reshape(1, 1, H_M, DM)
    n_s = c(g["mn_s"].reshape(P, NSEQ, H_M, 2).transpose(1, 2, 3, 0)).reshape(1, NSEQ, H_M, DM)
    return (y_p[0], y_s[0], k_p, v_p, l_p, g["mC_p"].reshape(1, 1, H_M, DM, DM), n_p, g["mm_p"].reshape(1, 1, H_M),
            k_s, v_s, l_s, g["mC_s"].reshape(1, NSEQ, H_M, DM, DM), n_s, g["mm_s"].reshape(1, NSEQ, H_M))
```

```python
from contextlib import ExitStack

import concourse.bass as bass
from concourse import mybir

F32 = mybir.dt.float32
U32 = mybir.dt.uint32
ALU = mybir.AluOpType
ACT = mybir.ActivationFunctionType
AX = mybir.AxisListType

P = 128
D = 1024
KD = D // P
SEQ, NSEQ, DSEQ, PAST = 1024, 8, 16, 512
PT = SEQ // P
NT = PT + NSEQ * DSEQ // P
TOK = NT * P
H_M, DM = 4, 256
H_F, DF = 16, 64
W_M, W_F = H_M * DM, H_F * DF
PH, PKEYS, PDQ, TOPK = 8, 128, 256, 16
EPS = 1e-6
NEG = -1e30
C_QM, C_KM, C_VM, C_OM = 0, W_M, 2 * W_M, 3 * W_M
C_IM = 4 * W_M
C_QF = C_IM + 2 * H_M
C_KF, C_VF = C_QF + W_F, C_QF + 2 * W_F
C_FF = C_QF + 3 * W_F
C_GM = C_FF + H_F
C_GF = C_GM + D
IN_COLS = C_GF + D
CHUNKS = 24
CW = IN_COLS // CHUNKS
FIRST = 5
NG = 2 * H_M + H_F
EXPERTS = PH * TOPK


class Stage:

    FIRST_SEM = 160

    def __init__(self, nc, tag):
        self.nc, self.tag, self.ctx, self.held = nc, tag, ExitStack(), []

    def __enter__(self):
        self.ctx.__enter__()
        return self

    def __exit__(self, *a):
        self.ctx.__exit__(*a)
        if a[0] is None:
            self.nc.all_engine_barrier(sems_to_clear=range(self.FIRST_SEM, self.FIRST_SEM + len(self.held)))
            for s in self.held:
                self.nc.release_semaphore(s)

    def sb(self, name, shape, dt=F32):
        return self.ctx.enter_context(self.nc.sbuf_tensor(f"{self.tag}_{name}", shape, dt))

    def ps(self, name, shape):
        return self.ctx.enter_context(self.nc.psum_tensor(f"{self.tag}_psum_{name}", shape, F32))

    def sem(self, name):
        self.held.append(self.nc.alloc_semaphore(f"{self.tag}_{name}", num=self.FIRST_SEM + len(self.held)))
        return self.held[-1]

    def pool_sem(self, name):
        return self.ctx.enter_context(self.nc.semaphore(f"{self.tag}_{name}"))

    def sems(self, names):
        return [self.sem(n) for n in names.split()]


def hold(eng, sem, value, passed):
    eng.wait_ge(sem, value)
    eng.sem_inc(passed, 1)


def bc(ap, shape):
    return ap.broadcast_to(shape)


def stage_constants(nc, K):
    with Stage(nc, "const") as st:
        filled, shaped, cut, reduced = st.sems("filled shaped cut reduced")
        block = st.ctx.enter_context(nc.Block())

        @block.gpsimd
        def _(pool):
            n = 0
            for t, v in [(K["ident"], 0.0), (K["ones"], 1.0), (K["negones"], -1.0), (K["mask"], 0.0),
                         (K["maskT"], 0.0), (K["tri"], 1.0), (K["bmask"], 0.0), (K["bmaskT"], 0.0),
                         (K["btri"], 1.0), (K["last"], 0.0), (K["blast"], 0.0), (K["pick"], 0.0),
                         (K["inblock"], 1.0), (K["headsel"], 0.0), (K["onesrow"], 1.0)]:
                pool.memset(t[:], v).then_inc(filled, 1)
                n += 1
            pool.wait_ge(filled, n)

            def cut_to(t, view, pattern, base, cm, op, fill, sem):
                v = view(t)
                pool.affine_select(out=v, in_=v, compare_op=op, fill=fill, base=base, pattern=pattern,
                                   channel_multiplier=cm).then_inc(sem, 1)

            flat = lambda t: t[:]
            blocks = lambda t: t[:].rearrange("p (n j) -> p n j", n=NSEQ)
            L = DSEQ
            cut_to(K["ident"], flat, [[-1, P]], 0, 1, ALU.not_equal, 1.0, shaped)
            for a, b in (("mask", "maskT"), ("bmask", "bmaskT")):
                cut_to(K[a], flat, [[-1, P]], 0, 1, ALU.is_ge, NEG, shaped)
                cut_to(K[b], flat, [[1, P]], 0, -1, ALU.is_ge, NEG, shaped)
            for a in ("tri", "btri"):
                cut_to(K[a], flat, [[1, P]], 0, -1, ALU.is_ge, 0.0, shaped)
            cut_to(K["last"], flat, [[0, P]], -(P - 1), 1, ALU.not_equal, 1.0, shaped)
            cut_to(K["blast"], blocks, [[-L, NSEQ], [0, L]], -(L - 1), 1, ALU.not_equal, 1.0, shaped)
            cut_to(K["pick"], flat, [[-L, NSEQ]], -(L - 1), 1, ALU.not_equal, 1.0, shaped)
            cut_to(K["inblock"], flat, [[-L, NSEQ]], 0, 1, ALU.is_ge, 0.0, shaped)
            cut_to(K["headsel"], flat, [[-8, 2], [-1, 8], [0, L]], 0, 1, ALU.not_equal, 1.0, shaped)
            pool.wait_ge(shaped, 12)
            cut_to(K["bmask"], blocks, [[L, NSEQ], [0, L]], L - 1, -1, ALU.is_ge, NEG, cut)
            cut_to(K["bmaskT"], blocks, [[-L, NSEQ], [0, L]], 0, 1, ALU.is_ge, NEG, cut)
            cut_to(K["btri"], blocks, [[-L, NSEQ], [0, L]], 0, 1, ALU.is_ge, 0.0, cut)
            cut_to(K["inblock"], flat, [[L, NSEQ]], L - 1, -1, ALU.is_ge, 0.0, cut)
            pool.wait_ge(cut, 4)

        @block.vector
        def _(dve):
            dve.wait_ge(cut, 4)
            dve.tensor_reduce(K["masknew"][:], K["bmask"][:].rearrange("p (n j) -> p j n", n=NSEQ), AX.X,
                              ALU.max).then_inc(reduced, 1)
            dve.wait_ge(reduced, 1)


def stage_norm(nc, K, x, g_cols, aT, t0, nt):
    with Stage(nc, f"norm{t0}") as st:
        xt, sq, xn = st.sb("xt", [P, D]), st.sb("sq", [P, D]), st.sb("xn", [P, D])
        gain = st.sb("gain", [P, KD])
        ss, ms, rt, rs = (st.sb(n, [P, 1]) for n in ("ss", "ms", "rt", "rs"))
        tp = st.ps("tp", [P, D])
        gain_in, x_in, squared, meaned, rooted, inverted, normed, turned, stored = st.sems(
            "gain_in x_in squared meaned rooted inverted normed turned stored")
        block = st.ctx.enter_context(nc.Block())

        @block.sync
        def _(sp):
            sp.dma_start(gain[:], g_cols).then_inc(gain_in, 16)
            with sp.Fori(0, nt) as i:
                sp.wait_ge(normed, i)
                sp.dma_start(xt[:], x[bass.ds(i * P + t0 * P, P), :]).then_inc(x_in, 16)

        @block.scalar
        def _(act):
            with act.Fori(0, nt) as i:
                act.wait_ge(x_in, i * 16 + 16)
                act.activation(sq[:], xt[:], ACT.Square, accum_out=ss[:]).then_inc(squared, 1)
                act.wait_ge(meaned, i + 1)
                act.activation(rt[:], ms[:], ACT.Sqrt).then_inc(rooted, 1)
                act.wait_ge(inverted, i + 1)
                act.wait_ge(turned, i)
                act.activation(xn[:], xt[:], ACT.Copy, scale=rs[:]).then_inc(normed, 1)

        @block.tensor
        def _(pe):
            with pe.Fori(0, nt) as i:
                pe.wait_ge(normed, i + 1)
                pe.wait_ge(stored, i)
                for k in range(KD):
                    mm = pe.transpose(tp[:, k * P:(k + 1) * P], xn[:, k * P:(k + 1) * P], K["ident"][:])
                mm.then_inc(turned, 1)

        @block.vector
        def _(dve):
            dve.wait_ge(gain_in, 16)
            with dve.Fori(0, nt) as i:
                dve.wait_ge(squared, i + 1)
                dve.tensor_scalar(ms[:], ss[:], 1.0 / D, EPS, ALU.mult, ALU.add).then_inc(meaned, 1)
                dve.wait_ge(rooted, i + 1)
                dve.reciprocal(rs[:], rt[:]).then_inc(inverted, 1)
                dve.wait_ge(turned, i + 1)
                dve.tensor_tensor(aT[:, :, bass.ts(i, P)], tp[:].rearrange("p (k t) -> p k t", k=KD),
                                  bc(gain[:], [P, KD, P]), ALU.mult).then_inc(stored, 1)
            dve.wait_ge(stored, nt)


def stage_project(nc, aT, w_in, z, t0, nt, ex=None):
    with Stage(nc, f"proj{t0}") as st:
        U = 3
        NI = CHUNKS // U
        PER = U * nt
        SLOTS = 5 if PER % 5 == 0 else 6
        w = st.sb("w", [P, U, KD, CW])
        zs = st.sb("zs", [P, SLOTS, CW])
        acc = [st.ps(f"acc{s}", [P, 512]) for s in range(SLOTS)]
        summed, read = st.sems("summed read")
        w_in_u = [st.sem(f"w_in{u}") for u in range(U)]
        out = [st.sem(f"out{s}") for s in range(SLOTS)]
        w_in_v = w_in.rearrange("(k p) n -> p k n", p=P)
        if ex:
            ex.begin(st, NI)
        block = st.ctx.enter_context(nc.Block())

        @block.sync
        def _(sp):
            for u in range(U):
                sp.dma_start(w[:, u], w_in_v[:, :, u * CW:(u + 1) * CW]).then_inc(w_in_u[u], 16)
            if ex:
                ex.load(sp, 0)

            def store(i, j):
                sp.wait_ge(read, i * PER + j + 1 + SLOTS)
                t = t0 + j % nt
                sp.dma_start(z[t * P:(t + 1) * P, bass.ds(i * (U * CW) + (j // nt) * CW, CW)],
                             zs[:, j % SLOTS, :]).then_inc(out[j % SLOTS], 16)

            with sp.Fori(0, NI - 1) as i:
                for u in range(U):
                    for j in range(u * nt, (u + 1) * nt):
                        store(i, j)
                    sp.dma_start(w[:, u], w_in_v[:, :, bass.ds(i * (U * CW) + (U + u) * CW, CW)]
                                 ).then_inc(w_in_u[u], 16)
            for j in range(PER):
                store(NI - 1, j)
            for s in range(SLOTS):
                sp.wait_ge(out[s], NI * (PER // SLOTS) * 16)
            if ex:
                ex.store(sp, 0)
                ex.stored_all(sp)

        @block.tensor
        def _(pe):
            with pe.Fori(0, NI) as i:
                for j in range(PER):
                    u, t = divmod(j, nt)
                    if t == 0:
                        pe.wait_ge(w_in_u[u], i * 16 + 16)
                    pe.wait_ge(read, i * PER + j + 1)
                    for k in range(KD):
                        mm = pe.matmul(acc[j % SLOTS][:, 0:CW], aT[:, k, t * P:(t + 1) * P], w[:, u, k, :],
                                       start=(k == 0), stop=(k == KD - 1))
                    mm.then_inc(summed, 1)

        @block.scalar
        def _(act):
            act.sem_inc(read, SLOTS)
            if ex:
                ex.act_tile(act, 0)
            with act.Fori(0, NI) as i:
                for j in range(PER):
                    if ex and j % 3 == 0:
                        ex.act_group(act, i, j // 3)
                    act.wait_ge(summed, i * PER + j + 1)
                    act.wait_ge(out[j % SLOTS], (i * (PER // SLOTS) + j // SLOTS) * 16)
                    act.copy(zs[:, j % SLOTS, :], acc[j % SLOTS][:, 0:CW]).then_inc(read, 1)

        if ex:
            @block.gpsimd
            def _(pool):
                ex.pool_all(pool)

            @block.vector
            def _(dve):
                ex.dve_all(dve)


def stage_gates(nc, K, z, bias, cache_lf, gates, ck_last, T, t0, nt):
    with Stage(nc, f"gate{t0}") as st:
        p0 = max(t0, 1)
        NP = (t0 + nt - p0) * P
        c0 = (p0 - 1) * P
        rows = slice(t0 * P, (t0 + nt) * P)
        b = st.sb("b", [P, NG])
        e = st.sb("e", [P, nt, NG - H_M])
        lfT = st.sb("lfT", [H_F, nt * P])
        ck = st.sb("ck", [H_F, NP])
        nck = st.sb("nck", [H_F, NP])
        one = st.sb("one", [P, SEQ])
        cs = st.sb("cs", [P, PAST + DSEQ])
        csum = st.sb("csum", [P, PAST + DSEQ])
        ncs = st.sb("ncs", [P, PAST + DSEQ])
        tp = st.ps("tp", [H_F, 2048])
        z_in, cache_in, biased, folded, expd, logd, ready, turned, copied, rows_out, new_in, summed, outs = st.sems(
            "z_in cache_in biased folded expd logd ready turned copied rows_out new_in summed outs")
        zr = z[rows, :].rearrange("(t p) n -> p t n", p=P)
        tiles = slice(t0, t0 + nt)
        f = gates[:, tiles, H_M:NG]
        block = st.ctx.enter_context(nc.Block())

        @block.sync
        def _(sp):
            sp.dma_start(gates[:, tiles, 0:2 * H_M], zr[:, :, C_IM:C_QF]).then_inc(z_in, 16)
            sp.dma_start(gates[:, tiles, 2 * H_M:NG], zr[:, :, C_FF:C_GM]).then_inc(z_in, 16)
            sp.dma_start(b[:], bc(bias, [P, NG])).then_inc(z_in, 16)
            sp.dma_start(T["fox_k"][rows, :], z[rows, C_KF:C_VF]).then_inc(outs, 16)
            sp.dma_start(T["fox_v"][rows, :], z[rows, C_VF:C_FF]).then_inc(outs, 16)
            sp.wait_ge(ready, 1)
            sp.dma_start(T["fox_lf"][rows, :].rearrange("(t p) h -> p t h", p=P), gates[:, tiles, 2 * H_M:NG]
                         ).then_inc(outs, 16)
            if t0 == 0:
                sp.dma_start(cs[:, 0:PAST], cache_lf).then_inc(cache_in, 16)
                sp.wait_ge(copied, 1)
                sp.dma_start(T["lfT"], lfT[:, 0:P]).then_inc(rows_out, 16)
                sp.wait_ge(rows_out, 16)
                for n in range(NSEQ):
                    sp.dma_start(cs[n * H_F:(n + 1) * H_F, PAST:], T["lfT"][:, n * DSEQ:(n + 1) * DSEQ]
                                 ).then_inc(new_in, 16)
            sp.wait_ge(summed, 2)
            sp.dma_start(T["nck"][:, c0:c0 + NP], nck[:]).then_inc(outs, 16)
            if t0 == 0:
                sp.wait_ge(summed, 5)
                sp.dma_start(T["ncs"].rearrange("n h s -> (n h) s"), ncs[:]).then_inc(outs, 16)
            sp.wait_ge(outs, (5 if t0 == 0 else 4) * 16)

        @block.vector
        def _(dve):
            dve.memset(one[:], 1.0).then_inc(biased, 1)
            dve.wait_ge(z_in, 48)
            dve.tensor_tensor(gates[:, tiles, :], gates[:, tiles, :], b[:].unsqueeze(1).to_broadcast([P, nt, NG]),
                              ALU.add).then_inc(biased, 1)
            dve.wait_ge(biased, 2)
            dve.scalar_tensor_tensor(out=e[:], in0=f, scalar=-1.0, in1=f, op0=ALU.mult, op1=ALU.min).then_inc(folded, 1)
            dve.wait_ge(logd, 1)
            dve.scalar_tensor_tensor(out=f, in0=f, scalar=0.0, in1=e[:], op0=ALU.min, op1=ALU.subtract
                                     ).then_inc(ready, 1)
            dve.wait_ge(turned, 1)
            dve.tensor_copy(lfT[:], tp[:, 0:nt * P]).then_inc(copied, 1)
            dve.wait_ge(copied, 1)
            dve.tensor_tensor_scan(ck[:], one[0:H_F, 0:NP], lfT[:, (p0 - t0) * P:], 0.0 if t0 == 0 else ck_last[:],
                                   ALU.mult, ALU.add).then_inc(summed, 1)
            dve.wait_ge(summed, 1)
            dve.tensor_scalar(nck[:], ck[:], -1.0, None, ALU.mult).then_inc(summed, 1)
            dve.tensor_copy(ck_last[:], ck[:, NP - 1:NP]).then_inc(summed, 1)
            if t0 == 0:
                dve.wait_ge(cache_in, 16)
                dve.wait_ge(new_in, 16 * NSEQ)
                dve.tensor_tensor_scan(csum[:], one[:, 0:PAST + DSEQ], cs[:], 0.0, ALU.mult, ALU.add
                                       ).then_inc(summed, 1)
                dve.wait_ge(summed, 4)
                dve.tensor_scalar(ncs[:], csum[:], -1.0, None, ALU.mult).then_inc(summed, 1)

        @block.scalar
        def _(act):
            act.wait_ge(folded, 1)
            act.activation(e[:], e[:], ACT.Exp).then_inc(expd, 1)
            act.wait_ge(expd, 1)
            act.activation(e[:], e[:], ACT.Ln, bias=1.0).then_inc(logd, 1)

        @block.tensor
        def _(pe):
            pe.wait_ge(ready, 1)
            for t in range(nt):
                mm = pe.transpose(tp[:, t * P:(t + 1) * P], gates[:, t0 + t, 2 * H_M:NG], K["ident"][:])
            mm.then_inc(turned, 1)


def stage_fox_prompt(nc, K, z, T, b0, b1, ex=None):
    with Stage(nc, f"foxp{b0}") as st:
        HP = 2
        NB = b1 - b0
        NS = HP * NB
        NI = H_F // HP
        q, k, v = st.sb("q", [P, NB, P]), st.sb("k", [P, b1, P]), st.sb("v", [P, b1, P])
        qT = st.sb("qT", [DF + 1, HP, NB * P])
        kT = st.sb("kT", [DF + 1, HP, b1 * P])
        prob = st.sb("prob", [P, 2, b1 * P])
        probT = st.sb("probT", [P, b1 * P])
        nmax, total, inv = (st.sb(n, [P, 2]) for n in ("nmax", "total", "inv"))
        y = st.sb("y", [P, NB, P])
        s_ps = [st.ps(f"s{n}", [P, SEQ]) for n in range(2)]
        t_ps = st.ps("t", [P, SEQ])
        h_ps = st.ps("h", [P, 512])
        y_ps = st.ps("y", [P, 512])
        ybank = [y_ps, h_ps]
        tbank = [h_ps[0:DF, :], t_ps[0:DF, 0:512], t_ps[0:DF, 512:1024], y_ps[0:DF, :]]
        (ones_set, qk_in, v_in, ck_in, turned, turned_out, scored, maxed, expd, inverted, probs_turned,
         probs_out, mixed, y_ready, y_out) = st.sems(
            "ones_set qk_in v_in ck_in turned turned_out scored maxed expd inverted probs_turned "
            "probs_out mixed y_ready y_out")
        zr = z[P:TOK, :].rearrange("(t p) n -> p t n", p=P)
        groups = [(q, qT, e, c) for e in range(HP) for c in range(0, NB, 4)]
        groups += [(k, kT, e, c) for e in range(HP) for c in range(0, b1, 4)]
        NTR = len(groups)
        if ex:
            ex.begin(st, NI)
        block = st.ctx.enter_context(nc.Block())

        @block.sync
        def _(sp):
            if ex:
                ex.load(sp, 0)
            with sp.Fori(0, NI) as i:
                sp.wait_ge(turned, i * NTR)
                sp.dma_start(q[:], zr[:, b0:b1, bass.ds(i * P + C_QF, P)]).then_inc(qk_in, 16)
                sp.dma_start(k[:], zr[:, 0:b1, bass.ds(i * P + C_KF, P)]).then_inc(qk_in, 16)
                sp.wait_ge(scored, i * NS)
                for e in range(HP):
                    sp.dma_start(kT[DF:DF + 1, e, :], T["nck"][bass.ds(i * HP + e, 1), 0:b1 * P]).then_inc(ck_in, 16)
                sp.wait_ge(mixed, i * NS)
                sp.dma_start(v[:], zr[:, 0:b1, bass.ds(i * P + C_VF, P)]).then_inc(v_in, 16)
                sp.wait_ge(y_ready, i * NS + NS)
                sp.dma_start(T["ycat"][P:TOK, :].rearrange("(t p) n -> p t n", p=P)[:, b0:b1, bass.ds(i * P + W_M, P)],
                             y[:]).then_inc(y_out, 16)
            sp.wait_ge(y_out, NI * 16)
            if ex:
                ex.store(sp, 0)
                ex.stored_all(sp)

        @block.tensor
        def _(pe):
            def scores(i, s):
                e, b = divmod(s, NB)
                if s >= 2:
                    pe.wait_ge(expd, i * NS + s - 1)
                n = (b0 + b + 1) * P
                for c in range(0, n, 512):
                    m = min(512, n - c)
                    mm = pe.matmul(s_ps[s % 2][:, c:c + m], qT[:, e, b * P:(b + 1) * P], kT[:, e, c:c + m],
                                   start=True, stop=(c + m != n))
                mm = pe.matmul(s_ps[s % 2][:, n - P:n], K["ident"][:], K["mask"][:], start=False, stop=True)
                mm.then_inc(scored, 1)

            def turn(i, s):
                b = b0 + s % NB
                hold(pe, expd, i * NS + s + 1, K["passed"])
                if s >= 1:
                    hold(pe, probs_out, i * NS + s, K["passed"])
                for c in range(b + 1):
                    mm = pe.transpose(t_ps[:, c * P:(c + 1) * P], prob[:, s % 2, c * P:(c + 1) * P], K["ident"][:])
                mm.then_inc(probs_turned, 1)

            def mix(i, s):
                e, b = divmod(s, NB)
                pe.wait_ge(probs_out, i * NS + s + 1)
                if s >= 2:
                    pe.wait_ge(y_ready, i * NS + s - 1)
                for c in range(b0 + b + 1):
                    mm = pe.matmul(ybank[s % 2][:, 0:DF], probT[:, c * P:(c + 1) * P],
                                   v[:, c, e * DF:(e + 1) * DF], start=(c == 0), stop=(c == b0 + b))
                mm.then_inc(mixed, 1)

            pe.wait_ge(ones_set, 1)
            with pe.Fori(0, NI) as i:
                pe.wait_ge(qk_in, i * 32 + 32)
                pe.wait_ge(probs_out, i * NS)
                hold(pe, y_ready, i * NS, K["passed"])
                for g, (src, _, e, c0) in enumerate(groups):
                    if g >= 4:
                        hold(pe, turned_out, i * NTR + g - 3, K["passed"])
                    for c in range(min(4, src.shape[1] - c0)):
                        mm = pe.transpose(tbank[g % 4][:, c * P:(c + 1) * P], src[:, c0 + c, e * DF:(e + 1) * DF],
                                          K["ident"][:])
                    mm.then_inc(turned, 1)
                pe.wait_ge(turned_out, i * NTR + NTR)
                pe.wait_ge(ck_in, i * 32 + 32)
                for s in range(NS + 1):
                    if s < NS:
                        scores(i, s)
                    if s == 1:
                        pe.wait_ge(v_in, i * 16 + 16)
                    if s >= 1:
                        turn(i, s - 1)
                        mix(i, s - 1)

        @block.vector
        def _(dve):
            dve.memset(qT[DF:DF + 1, :, :], 1.0).then_inc(ones_set, 1)
            if ex:
                ex.dve_tile(dve, 0)
            with dve.Fori(0, NI) as i:
                for g, (src, dst, e, c0) in enumerate(groups):
                    if g % 2:
                        continue
                    w = min(4, src.shape[1] - c0) * P
                    dve.wait_ge(turned, i * NTR + g + 1)
                    if g >= 1:
                        dve.wait_ge(turned_out, i * NTR + g)
                    if src is q:
                        dve.tensor_scalar(dst[0:DF, e, c0 * P:c0 * P + w], tbank[g % 4][:, 0:w], DF ** -0.5, None,
                                          ALU.mult).then_inc(turned_out, 1)
                    else:
                        dve.tensor_copy(dst[0:DF, e, c0 * P:c0 * P + w], tbank[g % 4][:, 0:w]
                                        ).then_inc(turned_out, 1)
                dve.wait_ge(y_out, i * 16)
                for s in range(NS + 1):
                    if s < NS:
                        n = (b0 + s % NB + 1) * P
                        dve.wait_ge(scored, i * NS + s + 1)
                        dve.tensor_reduce(nmax[:, s % 2:s % 2 + 1], s_ps[s % 2][:, 0:n], AX.X, ALU.max, negate=True
                                          ).then_inc(maxed, 1)
                        if ex:
                            ex.dve_units(dve, i, s // 2, (0, 2) if s % 2 == 0 else (4, 7))
                    if s >= 1:
                        r = s - 1
                        e, b = divmod(r, NB)
                        dve.wait_ge(expd, i * NS + r + 1)
                        dve.reciprocal(inv[:, r % 2:r % 2 + 1], total[:, r % 2:r % 2 + 1]).then_inc(inverted, 1)
                        dve.wait_ge(inverted, i * NS + r + 1)
                        dve.wait_ge(mixed, i * NS + r + 1)
                        dve.tensor_scalar(y[:, b, e * DF:(e + 1) * DF], ybank[r % 2][:, 0:DF],
                                          inv[:, r % 2:r % 2 + 1], None, ALU.mult).then_inc(y_ready, 1)
                    if ex and s < NS:
                        ex.dve_units(dve, i, s // 2, (2, 4) if s % 2 == 0 else (7, 9))
            if ex:
                ex.dve_end(dve, 0)

        @block.scalar
        def _(act):
            if ex:
                ex.act_tile(act, 0)
            with act.Fori(0, NI) as i:
                for g, (src, dst, e, c0) in enumerate(groups):
                    if g % 2 == 0:
                        continue
                    w = min(4, src.shape[1] - c0) * P
                    act.wait_ge(turned, i * NTR + g + 1)
                    act.wait_ge(turned_out, i * NTR + g)
                    act.mul(dst[0:DF, e, c0 * P:c0 * P + w], tbank[g % 4][:, 0:w], DF ** -0.5 if src is q else 1.0
                            ).then_inc(turned_out, 1)
                for s in range(NS + 1):
                    if s < NS:
                        n = (b0 + s % NB + 1) * P
                        act.wait_ge(maxed, i * NS + s + 1)
                        act.wait_ge(inverted, i * NS + max(s - 1, 0))
                        act.wait_ge(probs_turned, i * NS + max(s - 1, 0))
                        act.activation(prob[:, s % 2, 0:n], s_ps[s % 2][:, 0:n], ACT.Exp, bias=nmax[:, s % 2:s % 2 + 1],
                                       accum_out=total[:, s % 2:s % 2 + 1]).then_inc(expd, 1)
                    if s >= 1:
                        n = (b0 + (s - 1) % NB + 1) * P
                        act.wait_ge(probs_turned, i * NS + s)
                        act.copy(probT[:, 0:n], t_ps[:, 0:n]).then_inc(probs_out, 1)
                    if ex and s < NS and s % 2 == 0:
                        ex.act_group(act, i, s // 2)

        if ex:
            @block.gpsimd
            def _(pool):
                ex.pool_all(pool)


def stage_fox_sample(nc, K, z, T):
    with Stage(nc, "foxs") as st:
        S = PAST + DSEQ
        ST = PAST // P
        q, k = st.sb("q", [P, W_F]), st.sb("k", [P, W_F])
        qT, kT = st.sb("qT", [P, KD, P]), st.sb("kT", [P, KD, P])
        kc = st.sb("kc", [P, KD, PAST])
        vc = st.sb("vc", [P, ST, W_F])
        vn = st.sb("vn", [DSEQ, W_F])
        ck = st.sb("ck", [H_F, S])
        kn = st.sb("kn", [P, KD, DSEQ])
        qd = st.sb("qd", [P, 2, 4, P])
        prob = st.sb("prob", [P, 2, S])
        probT = st.sb("probT", [P, 5 * P])
        nmax, total, inv = (st.sb(n, [P, 2]) for n in ("nmax", "total", "inv"))
        y = st.sb("y", [P, 2, 512])
        s_ps = [st.ps(f"s{n}", [P, 1024]) for n in range(2)]
        t_ps = st.ps("t", [P, 1024])
        y_ps = st.ps("y", [P, 1024])
        (zeroed, qk_in, turned, turned_out, kc_in, vc_in, placed, scored, maxed, expd, inverted, probs_turned,
         probs_out, mixed, y_ready) = st.sems(
            "zeroed qk_in turned turned_out kc_in vc_in placed scored maxed expd inverted probs_turned "
            "probs_out mixed y_ready")
        y_out = st.pool_sem("y_out")
        HO = 2 * 8 * 16
        block = st.ctx.enter_context(nc.Block())

        @block.sync
        def _(sp):
            sp.dma_start(q[:], z[0:P, C_QF:C_KF]).then_inc(qk_in, 16)
            sp.dma_start(k[:], z[0:P, C_KF:C_VF]).then_inc(qk_in, 16)
            with sp.Fori(0, NSEQ) as n:
                sp.wait_ge(scored, n * 2)
                sp.dma_start(kc[:], T["cache_kT"][n].rearrange("(c p) s -> p c s", p=P)).then_inc(kc_in, 16)
                sp.dma_start(ck[:], T["ncs"][n]).then_inc(kc_in, 16)
                sp.wait_ge(mixed, n * 2)
                sp.dma_start(vc[:], T["cache_v"][n].rearrange("(c p) s -> p c s", p=P)).then_inc(vc_in, 16)
                sp.dma_start(vn[:], z[bass.ds(n * DSEQ, DSEQ), C_VF:C_FF]).then_inc(vc_in, 16)

        @block.gpsimd
        def _(pool):
            with pool.Fori(0, NSEQ) as n:
                for f in range(2):
                    pool.wait_ge(y_ready, n * 2 + f + 1)
                    for h in range(8):
                        pool.dma_start(T["ycat"][bass.ds(n * DSEQ, DSEQ),
                                                 W_M + (8 * f + h) * DF:W_M + (8 * f + h + 1) * DF],
                                       y[h * DSEQ:(h + 1) * DSEQ, f, h * DF:(h + 1) * DF]).then_inc(y_out, 16)
            pool.wait_ge(y_out, NSEQ * HO)

        @block.tensor
        def _(pe):
            pe.wait_ge(qk_in, 32)
            for g, src in enumerate((q, k)):
                for c in range(KD):
                    mm = pe.transpose((s_ps[g])[:, c * P:(c + 1) * P], src[:, c * P:(c + 1) * P], K["ident"][:])
                mm.then_inc(turned, 1)
            pe.wait_ge(turned_out, 2)
            with pe.Fori(0, NSEQ) as n:
                pe.wait_ge(placed, n * 5 + 5)
                pe.wait_ge(kc_in, n * 32 + 32)
                for f in range(2):
                    pe.wait_ge(expd, n * 2)
                    for p in range(4):
                        pe.matmul(s_ps[f][:, 0:PAST], qd[:, f, p, :], kc[:, 4 * f + p, :], start=(p == 0), stop=False)
                    pe.matmul(s_ps[f][:, 0:PAST], K["headsel"][:, f].rearrange("p h q -> p (h q)"), ck[:, 0:PAST],
                              start=False, stop=True)
                    for p in range(4):
                        pe.matmul(s_ps[f][:, PAST:S], qd[:, f, p, :], kn[:, 4 * f + p, :], start=(p == 0), stop=False)
                    pe.matmul(s_ps[f][:, PAST:S], K["headsel"][:, f].rearrange("p h q -> p (h q)"), ck[:, PAST:S],
                              start=False, stop=False)
                    pe.matmul(s_ps[f][:, PAST:S], K["ident"][:], K["masknew"][:], start=False, stop=True
                              ).then_inc(scored, 1)
                pe.wait_ge(vc_in, n * 32 + 32)
                for f in range(2):
                    pe.wait_ge(expd, n * 2 + f + 1)
                    pe.wait_ge(probs_out, n * 2 + f)
                    for c in range(ST):
                        pe.transpose(t_ps[:, c * P:(c + 1) * P], prob[:, f, c * P:(c + 1) * P], K["ident"][:])
                    pe.transpose(t_ps[0:DSEQ, ST * P:(ST + 1) * P], prob[:, f, PAST:S], K["ident"][:]
                                 ).then_inc(probs_turned, 1)
                    pe.wait_ge(probs_out, n * 2 + f + 1)
                    pe.wait_ge(y_ready, n * 2)
                    for c in range(ST):
                        pe.matmul(y_ps[:, f * 512:(f + 1) * 512], probT[:, c * P:(c + 1) * P],
                                  vc[:, c, f * 512:(f + 1) * 512], start=(c == 0), stop=False)
                    pe.matmul(y_ps[:, f * 512:(f + 1) * 512], probT[0:DSEQ, ST * P:(ST + 1) * P],
                              vn[:, f * 512:(f + 1) * 512], start=False, stop=True).then_inc(mixed, 1)

        @block.vector
        def _(dve):
            dve.memset(qd[:], 0.0).then_inc(zeroed, 1)
            dve.wait_ge(turned, 1)
            dve.tensor_scalar(qT[:].rearrange("p c t -> p (c t)"), s_ps[0][:], DF ** -0.5, None, ALU.mult
                              ).then_inc(turned_out, 1)
            dve.wait_ge(turned, 2)
            dve.tensor_copy(kT[:].rearrange("p c t -> p (c t)"), s_ps[1][:]).then_inc(turned_out, 1)
            dve.wait_ge(zeroed, 1)
            dve.wait_ge(turned_out, 2)
            with dve.Fori(0, NSEQ) as n:
                dve.wait_ge(scored, n * 2)
                for f in range(2):
                    for e in range(2):
                        base = qd[e * DF:(e + 1) * DF, f, :, :]
                        flat = base.rearrange("p c m -> p (c m)")
                        first = e * DSEQ
                        dve.tensor_copy(diag4(flat, first), qT[e * DF:(e + 1) * DF, 4 * f:4 * f + 4, bass.ts(n, DSEQ)]
                                        ).then_inc(placed, 1)
                dve.tensor_copy(kn[:], kT[:, :, bass.ts(n, DSEQ)]).then_inc(placed, 1)
                for f in range(2):
                    dve.wait_ge(scored, n * 2 + f + 1)
                    dve.tensor_reduce(nmax[:, f:f + 1], s_ps[f][:, 0:S], AX.X, ALU.max, negate=True).then_inc(maxed, 1)
                for f in range(2):
                    dve.wait_ge(expd, n * 2 + f + 1)
                    dve.reciprocal(inv[:, f:f + 1], total[:, f:f + 1]).then_inc(inverted, 1)
                    dve.wait_ge(inverted, n * 2 + f + 1)
                    dve.wait_ge(mixed, n * 2 + f + 1)
                    dve.wait_ge(y_out, n * HO)
                    dve.tensor_scalar(y[:, f, :], y_ps[:, f * 512:(f + 1) * 512], inv[:, f:f + 1], None, ALU.mult
                                      ).then_inc(y_ready, 1)

        @block.scalar
        def _(act):
            with act.Fori(0, NSEQ) as n:
                for f in range(2):
                    act.wait_ge(maxed, n * 2 + f + 1)
                    act.wait_ge(probs_turned, n * 2)
                    act.wait_ge(inverted, n * 2)
                    act.activation(prob[:, f, :], s_ps[f][:, 0:S], ACT.Exp, bias=nmax[:, f:f + 1],
                                   accum_out=total[:, f:f + 1]).then_inc(expd, 1)
                for f in range(2):
                    act.wait_ge(probs_turned, n * 2 + f + 1)
                    act.wait_ge(mixed, n * 2 + f)
                    act.copy(probT[:, 0:PAST], t_ps[:, 0:PAST])
                    act.copy(probT[0:DSEQ, PAST:PAST + P], t_ps[0:DSEQ, PAST:PAST + P]).then_inc(probs_out, 1)


def diag4(flat, first):
    step = P + 2 * DSEQ
    v = flat[:, first:first + 3 * step + DSEQ]
    return bass.AP(tensor=v.tensor, offset=v.offset, ap=[v.ap[0], [step, 4], [1, DSEQ]])


class Chain:

    def __init__(self, eng, sem, it, per, ready):
        self.ready = ready
        self.eng, self.sem, self.it, self.per, self.n = eng, sem, it, per, 0

    def __call__(self, instruction):
        instruction.then_inc(self.sem, 1)
        self.n += 1
        hold(self.eng, self.sem, self.it * self.per + self.n, self.ready)

    def close(self):
        assert self.n == self.per, (self.n, self.per)


def eye_times(dve, K, out, cols, heads):
    return dve.tensor_tensor(out, K["ident"][:].unsqueeze(1).to_broadcast([P, heads, P]), bc(cols, [P, heads, P]),
                             ALU.mult)


def stage_mlstm_prompt(nc, K, z, gates, C, m, T, c0, c1, ex=None):
    with Stage(nc, f"mlp{c0}") as st:
        H, DA = H_M, DM + 1
        NC = c1 - c0
        KS = DM ** -0.5
        q, k, o = st.sb("q", [P, W_M]), st.sb("k", [P, W_M]), st.sb("o", [P, W_M])
        v = st.sb("v", [P, H, DA])
        qT, kT = st.sb("qT", [P, 2 * H, P]), st.sb("kT", [P, 2 * H, P])
        g8 = st.sb("g8", [P, 2 * H])
        x, b, rmax = (st.sb(n, [P, H]) for n in ("x", "b", "rmax"))
        Mm = st.sb("Mm", [P, 2 * H])
        Ml = st.sb("Ml", [P, 2 * H])
        e1, e2 = st.sb("e1", [P, 2 * H]), st.sb("e2", [P, 2 * H])
        w1, w2 = st.sb("w1", [P, 2 * H]), st.sb("w2", [P, 2 * H])
        dx, dM = st.sb("dx", [P, H, P]), st.sb("dM", [P, H, P])
        wD, A = st.sb("wD", [P, H, P]), st.sb("A", [P, H, P])
        inter, num = st.sb("inter", [P, DA]), st.sb("num", [P, DA])
        kw = st.sb("kw", [P, 2, DM])
        den = st.sb("den", [P, 1])
        inv = st.sb("inv", [P, 1])
        so = st.sb("so", [P, W_M])
        y = st.sb("y", [P, W_M])
        g_ps, e_ps, s_ps, t_ps, n1_ps, n2_ps, c0_ps, c1_ps = (
            st.ps(n, [P, 512]) for n in ("g", "e", "s", "t", "n1", "n2", "c0", "c1"))
        tb = [t_ps, c0_ps, c1_ps, t_ps]
        (set_up, z_in, gates_in, summed, x_set, dx_set, rows_e, chain, m_set, dm_set, rows_m, w1_set, wd_set,
         last_set, e2_set, w2_set, turned, turned_out, scored, mixed, n_ready, inter_set, kw_set, c_summed, c_set,
         y_head, o_set, y_out, outs) = st.sems(
            "set_up z_in gates_in summed x_set dx_set rows_e chain m_set dm_set rows_m w1_set wd_set "
            "last_set e2_set w2_set turned turned_out scored mixed n_ready inter_set kw_set c_summed c_set "
            "y_head o_set y_out outs")
        SET_UP = 3 if c0 == 0 else 1
        DVE_STEPS = 2 + 3 + 1 + 4 * H
        if ex:
            ex.begin(st, NC, last=True)
        block = st.ctx.enter_context(nc.Block())

        def ex_dots_and_sums(dve, i, p):
            if ex:
                ex.dve_units(dve, i, p, (0, 2 * ex.G + 1))

        def ex_gelu(act, i, p):
            if ex:
                ex.act_group(act, i, p)

        @block.sync
        def _(sp):
            if ex:
                ex.load(sp, 0)
            sp.wait_ge(set_up, SET_UP)
            with sp.Fori(0, NC) as i:
                rows = bass.ds(i * P + (c0 + 1) * P, P)
                sp.wait_ge(c_set, i * 2 * H)
                sp.dma_start(q[:], z[rows, C_QM:C_KM]).then_inc(z_in, 16)
                sp.dma_start(k[:], z[rows, C_KM:C_VM]).then_inc(z_in, 16)
                sp.dma_start(v[:, :, 0:DM], z[rows, C_VM:C_OM].rearrange("t (h e) -> t h e", h=H)).then_inc(z_in, 16)
                sp.wait_ge(o_set, i)
                sp.dma_start(o[:], z[rows, C_OM:C_IM]).then_inc(z_in, 16)
                sp.wait_ge(y_head, i * H + H)
                sp.dma_start(T["ycat"][rows, 0:W_M], y[:]).then_inc(y_out, 16)
            if c1 == PT:
                sp.wait_ge(c_set, NC * 2 * H)
                for h in range(H):
                    sp.dma_start(T["mC_p"][h].rearrange("(j p) e -> p j e", p=P), C[:, 2 * h:2 * h + 2, 0:DM]
                                 ).then_inc(outs, 16)
                with nc.allow_non_contiguous_dma(reason="one column of the state"):
                    sp.dma_start(T["mn_p"], C[:, :, DM]).then_inc(outs, 16)
                sp.dma_start(T["mm_p"], m[0:1, :]).then_inc(outs, 16)
                sp.wait_ge(outs, (H + 2) * 16)
            sp.wait_ge(y_out, NC * 16)
            if ex:
                ex.store(sp, 0)
                ex.stored_all(sp)

        if ex:
            @block.gpsimd
            def _(pool):
                ex.pool_all(pool)

        @block.tensor
        def _(pe):
            pe.wait_ge(set_up, SET_UP)
            with pe.Fori(0, NC) as i:
                pe.wait_ge(gates_in, i + 1)
                pe.wait_ge(last_set, i)
                pe.matmul(g_ps[:, 0:H], K["tri"][:], g8[:, H:2 * H], start=True, stop=True).then_inc(summed, 1)
                pe.wait_ge(z_in, i * 64 + 64)
                pe.wait_ge(c_set, i * 2 * H)
                for g in range(4):
                    if g == 3:
                        pe.wait_ge(turned_out, i * 4 + 1)
                    for c in range(4):
                        mm = pe.transpose(tb[g][:, c * P:(c + 1) * P],
                                          (q, k)[g // 2][:, (g % 2 * 4 + c) * P:(g % 2 * 4 + c + 1) * P], K["ident"][:])
                    mm.then_inc(turned, 1)
                pe.wait_ge(dx_set, i + 1)
                pe.wait_ge(wd_set, i)
                pe.matmul(e_ps[:], K["ones"][:], dx[:].rearrange("p h t -> p (h t)"), start=True, stop=False)
                for h in range(H):
                    mm = pe.matmul(e_ps[:, h * P:(h + 1) * P], K["ident"][:], K["mask"][:], start=False,
                                   stop=(h == H - 1))
                mm.then_inc(rows_e, 1)
                pe.wait_ge(turned_out, i * 4 + 4)
                pe.wait_ge(mixed, i)
                for h in range(H):
                    for j in range(2):
                        mm = pe.matmul(s_ps[:, h * P:(h + 1) * P], kT[:, 2 * h + j, :], qT[:, 2 * h + j, :],
                                       start=(j == 0), stop=(j == 1))
                mm.then_inc(scored, 1)
                pe.wait_ge(m_set, i + 1)
                pe.matmul(g_ps[:, 2 * H:4 * H], K["last"][:], Mm[:], start=True, stop=True).then_inc(summed, 1)
                pe.wait_ge(dm_set, i + 1)
                pe.matmul(e_ps[:], K["negones"][:], dM[:].rearrange("p h t -> p (h t)"), start=True, stop=False)
                for h in range(H):
                    mm = pe.matmul(e_ps[:, h * P:(h + 1) * P], K["ident"][:], K["maskT"][:], start=False,
                                   stop=(h == H - 1))
                mm.then_inc(rows_m, 1)
                for h in range(H):
                    pe.wait_ge(mixed, i + 1)
                    pe.wait_ge(y_head, i * H + h)
                    pe.matmul(n1_ps[:, 0:DA], A[:, h, :], v[:, h, :], start=True, stop=True)
                    for j in range(2):
                        mm = pe.matmul(n2_ps[:, 0:DA], qT[:, 2 * h + j, :], C[:, 2 * h + j, :], start=(j == 0),
                                       stop=(j == 1))
                    mm.then_inc(n_ready, 1)
                    pe.wait_ge(kw_set, i * H + h + 1)
                    pe.wait_ge(c_set, i * 2 * H + 2 * h)
                    for j, cb in enumerate((c0_ps, c1_ps)):
                        mm = pe.matmul(cb[:, 0:DA], kw[:, h % 2, j * P:(j + 1) * P], v[:, h, :], start=True, stop=True)
                    mm.then_inc(c_summed, 1)

        @block.vector
        def _(dve):
            dve.memset(v[:, :, DM:DA], 1.0).then_inc(set_up, 1)
            if c0 == 0:
                dve.memset(C[:], 0.0).then_inc(set_up, 1)
                dve.memset(m[:], 0.0).then_inc(set_up, 1)
            dve.wait_ge(set_up, SET_UP)
            if ex:
                ex.dve_tile(dve, 0)
            with dve.Fori(0, NC) as i:
                ch = Chain(dve, chain, i, DVE_STEPS, K["passed"])
                ex_dots_and_sums(dve, i, 0)
                dve.wait_ge(summed, i * 2)
                dve.wait_ge(w2_set, i)
                dve.tensor_copy(g8[:], gates[:, bass.ds(i + (c0 + 1), 1), 0:2 * H].rearrange("p a g -> p (a g)")
                                ).then_inc(gates_in, 1)
                dve.wait_ge(gates_in, i + 1)
                dve.wait_ge(summed, i * 2 + 1)
                dve.wait_ge(wd_set, i)
                dve.tensor_tensor(x[:], g8[:, 0:H], g_ps[:, 0:H], ALU.subtract).then_inc(x_set, 1)
                ch(dve.tensor_copy(b[:], g_ps[:, 0:H]))
                dve.wait_ge(x_set, i + 1)
                eye_times(dve, K, dx[:], x[:], H).then_inc(dx_set, 1)
                ex_dots_and_sums(dve, i, 1)
                dve.wait_ge(rows_e, i + 1)
                ch(dve.tensor_reduce(rmax[:], e_ps[:].rearrange("p (h t) -> p h t", h=H), AX.X, ALU.max))
                dve.wait_ge(summed, i * 2)
                ch(dve.tensor_tensor(Mm[:, 0:H], rmax[:], m[:], ALU.max))
                dve.tensor_tensor(Mm[:, H:2 * H], b[:], Mm[:, 0:H], ALU.add).then_inc(m_set, 1)
                dve.wait_ge(m_set, i + 1)
                ch(dve.tensor_tensor(e1[:, 0:H], m[:], Mm[:, 0:H], ALU.subtract))
                ch(dve.tensor_scalar(e1[:, H:2 * H], Mm[:, H:2 * H], -1.0, None, ALU.mult))
                eye_times(dve, K, dM[:], Mm[:, 0:H], H).then_inc(dm_set, 1)
                ex_dots_and_sums(dve, i, 2)
                dve.wait_ge(summed, i * 2 + 2)
                dve.tensor_copy(Ml[:], g_ps[:, 2 * H:4 * H]).then_inc(last_set, 1)
                dve.wait_ge(last_set, i + 1)
                ch(dve.tensor_tensor(e2[:, 0:H], m[:], Ml[:, 0:H], ALU.subtract))
                dve.tensor_tensor(e2[:, H:2 * H], x[:], Ml[:, 0:H], ALU.subtract).then_inc(e2_set, 1)
                dve.wait_ge(e2_set, i * 2 + 1)
                dve.tensor_copy(m[:], Ml[:, H:2 * H]).then_inc(e2_set, 1)
                dve.wait_ge(e2_set, i * 2 + 2)
                ex_dots_and_sums(dve, i, 3)
                dve.wait_ge(scored, i + 1)
                dve.wait_ge(wd_set, i + 1)
                dve.wait_ge(n_ready, i * H)
                dve.tensor_tensor(A[:].rearrange("p h t -> p (h t)"), s_ps[:], wD[:].rearrange("p h t -> p (h t)"),
                                  ALU.mult).then_inc(mixed, 1)
                dve.wait_ge(w2_set, i + 1)
                dve.wait_ge(y_out, i * 16)
                dve.wait_ge(o_set, i + 1)
                for h in range(H):
                    if h >= 2:
                        dve.wait_ge(c_summed, i * H + h - 1)
                    else:
                        dve.wait_ge(c_summed, i * H)
                    dve.tensor_scalar(kw[:, h % 2, :], k[:, h * DM:(h + 1) * DM], w2[:, H + h:H + h + 1], KS,
                                      ALU.mult, ALU.mult).then_inc(kw_set, 1)
                    dve.wait_ge(inter_set, i * H + h + 1)
                    ch(dve.tensor_tensor(num[:], n1_ps[:, 0:DA], inter[:], ALU.add))
                    ch(dve.scalar_tensor_tensor(out=den[:], in0=num[:, DM:DA], scalar=-1.0, in1=w1[:, H + h:H + h + 1],
                                                op0=ALU.mult, op1=ALU.max))
                    ch(dve.tensor_tensor(den[:], den[:], num[:, DM:DA], ALU.max))
                    ch(dve.reciprocal(inv[:], den[:]))
                    dve.scalar_tensor_tensor(out=y[:, h * DM:(h + 1) * DM], in0=num[:, 0:DM], scalar=inv[:],
                                             in1=so[:, h * DM:(h + 1) * DM], op0=ALU.mult, op1=ALU.mult
                                             ).then_inc(y_head, 1)
                    dve.wait_ge(y_head, i * H + h + 1)
                    dve.wait_ge(c_summed, i * H + h + 1)
                    for j, cb in enumerate((c0_ps, c1_ps)):
                        dve.scalar_tensor_tensor(out=C[:, 2 * h + j, :], in0=C[:, 2 * h + j, :], scalar=w2[:, h:h + 1],
                                                 in1=cb[:, 0:DA], op0=ALU.mult, op1=ALU.add).then_inc(c_set, 1)
                    ex_dots_and_sums(dve, i, 4 + h)
                dve.wait_ge(c_set, i * 2 * H + 2 * H)
                ch.close()
            if ex:
                ex.dve_end(dve, 0)

        @block.scalar
        def _(act):
            if ex:
                ex.act_tile(act, 0)
            with act.Fori(0, NC) as i:
                ex_gelu(act, i, 0)
                act.wait_ge(scored, i)
                act.wait_ge(n_ready, i * H)
                for g in range(4):
                    act.wait_ge(turned, i * 4 + g + 1)
                    dst = (qT, kT)[g // 2][:, g % 2 * 4:g % 2 * 4 + 4, :].rearrange("p c t -> p (c t)")
                    act.mul(dst, tb[g][:], (1.0, KS)[g // 2]).then_inc(turned_out, 1)
                ex_gelu(act, i, 1)
                act.wait_ge(m_set, i + 1)
                act.wait_ge(chain, i * DVE_STEPS + 5)
                act.wait_ge(c_set, i * 2 * H)
                act.activation(w1[:], e1[:], ACT.Exp).then_inc(w1_set, 1)
                ex_gelu(act, i, 2)
                act.wait_ge(rows_m, i + 1)
                act.wait_ge(mixed, i)
                for h in range(H):
                    e = act.activation(wD[:, h, :], e_ps[:, h * P:(h + 1) * P], ACT.Exp, bias=x[:, h:h + 1])
                e.then_inc(wd_set, 1)
                act.wait_ge(e2_set, i * 2 + 1)
                act.activation(w2[:], e2[:], ACT.Exp).then_inc(w2_set, 1)
                ex_gelu(act, i, 3)
                act.wait_ge(z_in, i * 64 + 64)
                act.wait_ge(y_head, i * H)
                act.activation(so[:], o[:], ACT.Sigmoid).then_inc(o_set, 1)
                act.wait_ge(w1_set, i + 1)
                for h in range(H):
                    act.wait_ge(n_ready, i * H + h + 1)
                    act.wait_ge(y_head, i * H + h)
                    act.activation(inter[:], n2_ps[:, 0:DA], ACT.Copy, scale=w1[:, h:h + 1]).then_inc(inter_set, 1)
                    ex_gelu(act, i, 4 + h)


def stage_mlstm_sample(nc, K, z, gates, T):
    with Stage(nc, "mls") as st:
        H, DA, N = H_M, DM + 1, NSEQ
        KS = DM ** -0.5
        q, k, o = st.sb("q", [P, DM]), st.sb("k", [P, DM]), st.sb("o", [P, DM])
        v = st.sb("v", [P, DA])
        C = st.sb("C", [P, N, 2, DA])
        n_all = st.sb("n_all", [P, N, H, 2])
        n_new = st.sb("n_new", [P, N, H, 2])
        m_all, m_new = st.sb("m_all", [P, H]), st.sb("m_new", [P, H])
        qT, kT = st.sb("qT", [P, 2, P]), st.sb("kT", [P, 2, P])
        qd = st.sb("qd", [P, 2, N * P])
        g2 = st.sb("g2", [P, 2])
        x, b, rmax, m = (st.sb(n, [P, 1]) for n in ("x", "b", "rmax", "m"))
        Mm, Ml = st.sb("Mm", [P, 2]), st.sb("Ml", [P, 2])
        e1, e2, w1, w2 = (st.sb(n, [P, 2]) for n in ("e1", "e2", "w1", "w2"))
        wp, wc = st.sb("wp", [P, N]), st.sb("wc", [P, N])
        dx, dM = st.sb("dx", [P, 1, P]), st.sb("dM", [P, 1, P])
        wD, A = st.sb("wD", [P, P]), st.sb("A", [P, P])
        inter, num, so, y = st.sb("inter", [P, DA]), st.sb("num", [P, DA]), st.sb("so", [P, DM]), st.sb("y", [P, DM])
        kws = st.sb("kws", [P, DM])
        kw = st.sb("kw", [P, 2, DM])
        den, inv = st.sb("den", [P, 1]), st.sb("inv", [P, 1])
        g_ps, e_ps, s_ps, t_ps, n1_ps, n2_ps, c0_ps, c1_ps = (
            st.ps(n, [P, 512]) for n in ("g", "e", "s", "t", "n1", "n2", "c0", "c1"))
        (set_up, state_in, z_in, c_in, c_cols, gates_in, summed, chain, rows_e, m_set, dm_set, rows_m, w1_set, wd_set,
         last_set, e2_set, w2_set, wp_set, turned, turned_out, placed, scored, mixed, n_ready, inter_set, kw_set,
         c_summed, c_set, y_head, o_set, y_out, c_out, outs, dx_set) = st.sems(
            "set_up state_in z_in c_in c_cols gates_in summed chain rows_e m_set dm_set rows_m w1_set wd_set "
            "last_set e2_set w2_set wp_set turned turned_out placed scored mixed n_ready inter_set kw_set "
            "c_summed c_set y_head o_set y_out c_out outs dx_set")
        DVE_STEPS = 2 + 1 + 1 + 2 + 2 + 1 + 5 + 1 + 1
        rows = slice(0, P)
        block = st.ctx.enter_context(nc.Block())

        @block.sync
        def _(sp):
            sp.dma_start(n_all[:].rearrange("p n h j -> p (n h j)"), T["n0"]).then_inc(state_in, 16)
            for n in range(N):
                sp.dma_start(m_all[n * DSEQ:(n + 1) * DSEQ, :], T["m0"][n:n + 1, :].to_broadcast([DSEQ, H])
                             ).then_inc(state_in, 16)
            sp.wait_ge(set_up, 2)
            with sp.Fori(0, H) as h:
                sp.wait_ge(c_set, h * 2 * N)
                sp.wait_ge(y_head, h)
                for buf, col in ((q, C_QM), (k, C_KM), (o, C_OM)):
                    sp.dma_start(buf[:], z[rows, bass.ds(h * DM + col, DM)]).then_inc(z_in, 16)
                sp.dma_start(v[:, 0:DM], z[rows, bass.ds(h * DM + C_VM, DM)]).then_inc(z_in, 16)
                sp.wait_ge(c_out, h * N * 16)
                for n in range(N):
                    sp.dma_start(C[:, n, :, 0:DM], T["C0"][n, bass.ds(h, 1)].rearrange("a (j p) e -> p (a j) e", p=P)
                                 ).then_inc(c_in, 16)
                sp.wait_ge(y_head, h + 1)
                sp.dma_start(T["ycat"][rows, bass.ds(h * DM, DM)], y[:]).then_inc(y_out, 16)
                for n in range(N):
                    sp.wait_ge(c_set, h * 2 * N + 2 * n + 2)
                    sp.dma_start(T["mC_s"][n, bass.ds(h, 1)].rearrange("a (j p) e -> p (a j) e", p=P),
                                 C[:, n, :, 0:DM]).then_inc(c_out, 16)
            sp.wait_ge(c_out, H * N * 16)
            sp.wait_ge(y_out, H * 16)
            sp.wait_ge(c_cols, 2 * H)
            sp.dma_start(T["mn_s"], n_new[:].rearrange("p n h j -> p (n h j)")).then_inc(outs, 16)
            sp.dma_start(T["mm_s"], m_new[0:P:DSEQ, :]).then_inc(outs, 16)
            sp.wait_ge(outs, 32)

        @block.tensor
        def _(pe):
            with pe.Fori(0, H) as i:
                pe.wait_ge(gates_in, i + 1)
                pe.wait_ge(last_set, i * 2)
                pe.matmul(g_ps[:, 0:1], K["btri"][:], g2[:, 1:2], start=True, stop=True).then_inc(summed, 1)
                pe.wait_ge(z_in, i * 64 + 64)
                pe.wait_ge(turned_out, i * 2)
                for c in range(4):
                    mm = pe.transpose(t_ps[:, c * P:(c + 1) * P], (q, k)[c // 2][:, c % 2 * P:(c % 2 + 1) * P],
                                      K["ident"][:])
                mm.then_inc(turned, 1)
                pe.wait_ge(dx_set, i + 1)
                pe.wait_ge(wd_set, i)
                pe.matmul(e_ps[:, 0:P], K["ones"][:], dx[:, 0, :], start=True, stop=False)
                pe.matmul(e_ps[:, 0:P], K["ident"][:], K["bmask"][:], start=False, stop=True).then_inc(rows_e, 1)
                pe.wait_ge(turned_out, i * 2 + 2)
                pe.wait_ge(mixed, i)
                for j in range(2):
                    mm = pe.matmul(s_ps[:, 0:P], kT[:, j, :], qT[:, j, :], start=(j == 0), stop=(j == 1))
                mm.then_inc(scored, 1)
                pe.wait_ge(m_set, i + 1)
                pe.matmul(g_ps[:, 2:4], K["blast"][:], Mm[:], start=True, stop=True).then_inc(summed, 1)
                pe.wait_ge(dm_set, i + 1)
                pe.matmul(e_ps[:, 0:P], K["negones"][:], dM[:, 0, :], start=True, stop=False)
                pe.matmul(e_ps[:, 0:P], K["ident"][:], K["bmaskT"][:], start=False, stop=True).then_inc(rows_m, 1)
                pe.wait_ge(wp_set, i + 1)
                pe.matmul(g_ps[:, 8:8 + N], K["ones"][:], wp[:], start=True, stop=True).then_inc(summed, 1)
                pe.wait_ge(mixed, i + 1)
                pe.wait_ge(y_head, i)
                pe.matmul(n1_ps[:, 0:DA], A[:], v[:], start=True, stop=True)
                pe.wait_ge(placed, i + 1)
                pe.wait_ge(c_in, i * N * 16 + N * 16)
                pe.wait_ge(c_cols, i * 2 + 1)
                for n in range(N):
                    for j in range(2):
                        mm = pe.matmul(n2_ps[:, 0:DA], qd[:, j, n * P:(n + 1) * P], C[:, n, j, :],
                                       start=(n + j == 0), stop=(n == N - 1 and j == 1))
                mm.then_inc(n_ready, 1)
                for n in range(N):
                    pe.wait_ge(kw_set, i * N + n + 1)
                    pe.wait_ge(c_set, i * 2 * N + 2 * n)
                    for j, cb in enumerate((c0_ps, c1_ps)):
                        mm = pe.matmul(cb[:, 0:DA], kw[:, n % 2, j * P:(j + 1) * P], v[:], start=True, stop=True)
                    mm.then_inc(c_summed, 1)

        @block.vector
        def _(dve):
            dve.memset(qd[:], 0.0).then_inc(set_up, 1)
            dve.memset(v[:, DM:DA], 1.0).then_inc(set_up, 1)
            dve.wait_ge(set_up, 2)
            dve.wait_ge(state_in, 16 * (N + 1))
            with dve.Fori(0, H) as i:
                ch = Chain(dve, chain, i, DVE_STEPS, K["passed"])
                dve.wait_ge(w2_set, i)
                dve.wait_ge(wd_set, i)
                ch(dve.tensor_copy(g2[:, 0:1], gates[:, 0, bass.ds(i, 1)]))
                ch(dve.tensor_copy(m[:], m_all[:, bass.ds(i, 1)]))
                dve.wait_ge(summed, i * 3)
                dve.tensor_copy(g2[:, 1:2], gates[:, 0, bass.ds(i + H, 1)]).then_inc(gates_in, 1)
                dve.wait_ge(summed, i * 3 + 1)
                ch(dve.tensor_tensor(x[:], g2[:, 0:1], g_ps[:, 0:1], ALU.subtract))
                ch(dve.tensor_copy(b[:], g_ps[:, 0:1]))
                eye_times(dve, K, dx[:], x[:], 1).then_inc(dx_set, 1)
                dve.wait_ge(rows_e, i + 1)
                ch(dve.tensor_reduce(rmax[:], e_ps[:, 0:P], AX.X, ALU.max))
                ch(dve.tensor_tensor(Mm[:, 0:1], rmax[:], m[:], ALU.max))
                dve.tensor_tensor(Mm[:, 1:2], b[:], Mm[:, 0:1], ALU.add).then_inc(m_set, 1)
                dve.wait_ge(m_set, i + 1)
                ch(dve.tensor_tensor(e1[:, 0:1], m[:], Mm[:, 0:1], ALU.subtract))
                ch(dve.tensor_scalar(e1[:, 1:2], Mm[:, 1:2], -1.0, None, ALU.mult))
                eye_times(dve, K, dM[:], Mm[:, 0:1], 1).then_inc(dm_set, 1)
                dve.wait_ge(summed, i * 3 + 2)
                dve.tensor_copy(Ml[:], g_ps[:, 2:4]).then_inc(last_set, 1)
                dve.wait_ge(last_set, i * 2 + 1)
                ch(dve.tensor_tensor(e2[:, 0:1], m[:], Ml[:, 0:1], ALU.subtract))
                dve.tensor_tensor(e2[:, 1:2], x[:], Ml[:, 0:1], ALU.subtract).then_inc(e2_set, 1)
                ch(dve.tensor_copy(m_new[:, bass.ds(i, 1)], Ml[:, 1:2]))
                dve.wait_ge(w2_set, i + 1)
                dve.tensor_scalar(wp[:], K["pick"][:], w2[:, 0:1], None, ALU.mult).then_inc(wp_set, 1)
                dve.wait_ge(turned_out, i * 2 + 2)
                dve.wait_ge(n_ready, i)
                dve.tensor_copy(diag8(qd), qT[:].rearrange("p j (n t) -> p j n t", n=N)).then_inc(placed, 1)
                dve.wait_ge(c_in, i * N * 16 + N * 16)
                dve.tensor_copy(C[:, :, :, DM], n_all[:, :, bass.ds(i, 1), :].rearrange("p n a j -> p n (a j)")
                                ).then_inc(c_cols, 1)
                dve.wait_ge(scored, i + 1)
                dve.wait_ge(wd_set, i + 1)
                dve.tensor_tensor(A[:], s_ps[:, 0:P], wD[:], ALU.mult).then_inc(mixed, 1)
                dve.wait_ge(summed, i * 3 + 3)
                dve.tensor_copy(wc[:], g_ps[:, 8:8 + N]).then_inc(last_set, 1)
                dve.wait_ge(last_set, i * 2 + 2)
                ch(dve.tensor_scalar(kws[:], k[:], w2[:, 1:2], KS, ALU.mult, ALU.mult))
                dve.wait_ge(inter_set, i + 1)
                ch(dve.tensor_tensor(num[:], n1_ps[:, 0:DA], inter[:], ALU.add))
                ch(dve.scalar_tensor_tensor(out=den[:], in0=num[:, DM:DA], scalar=-1.0, in1=w1[:, 1:2], op0=ALU.mult,
                                            op1=ALU.max))
                ch(dve.tensor_tensor(den[:], den[:], num[:, DM:DA], ALU.max))
                ch(dve.reciprocal(inv[:], den[:]))
                dve.wait_ge(o_set, i + 1)
                dve.wait_ge(y_out, i * 16)
                dve.scalar_tensor_tensor(out=y[:], in0=num[:, 0:DM], scalar=inv[:], in1=so[:], op0=ALU.mult,
                                         op1=ALU.mult).then_inc(y_head, 1)
                ch(dve.tensor_copy(den[:], inv[:]))
                for n in range(N + 1):
                    if n < N:
                        if n >= 2:
                            dve.wait_ge(c_summed, i * N + n - 1)
                        dve.tensor_scalar(kw[:, n % 2, :], kws[:], K["inblock"][:, n:n + 1], None, ALU.mult
                                          ).then_inc(kw_set, 1)
                    if n >= 1:
                        r = n - 1
                        dve.wait_ge(c_summed, i * N + r + 1)
                        for j, cb in enumerate((c0_ps, c1_ps)):
                            dve.scalar_tensor_tensor(out=C[:, r, j, :], in0=C[:, r, j, :], scalar=wc[:, r:r + 1],
                                                     in1=cb[:, 0:DA], op0=ALU.mult, op1=ALU.add).then_inc(c_set, 1)
                dve.wait_ge(c_set, i * 2 * N + 2 * N)
                dve.tensor_copy(n_new[:, :, bass.ds(i, 1), :].rearrange("p n a j -> p n (a j)"), C[:, :, :, DM]
                                ).then_inc(c_cols, 1)
                dve.wait_ge(c_cols, i * 2 + 2)
                ch.close()

        @block.scalar
        def _(act):
            with act.Fori(0, H) as i:
                act.wait_ge(turned, i + 1)
                act.wait_ge(placed, i)
                act.wait_ge(scored, i)
                for g, dst in enumerate((qT, kT)):
                    act.mul(dst[:].rearrange("p c t -> p (c t)"), t_ps[:, g * 2 * P:(g + 1) * 2 * P], (1.0, KS)[g]
                            ).then_inc(turned_out, 1)
                act.wait_ge(chain, i * DVE_STEPS + 8)
                act.activation(w1[:], e1[:], ACT.Exp).then_inc(w1_set, 1)
                act.wait_ge(rows_m, i + 1)
                act.wait_ge(mixed, i)
                act.activation(wD[:], e_ps[:, 0:P], ACT.Exp, bias=x[:]).then_inc(wd_set, 1)
                act.wait_ge(e2_set, i + 1)
                act.activation(w2[:], e2[:], ACT.Exp).then_inc(w2_set, 1)
                act.wait_ge(z_in, i * 64 + 64)
                act.wait_ge(y_head, i)
                act.activation(so[:], o[:], ACT.Sigmoid).then_inc(o_set, 1)
                act.wait_ge(w1_set, i + 1)
                act.wait_ge(n_ready, i + 1)
                act.activation(inter[:], n2_ps[:, 0:DA], ACT.Copy, scale=w1[:, 0:1]).then_inc(inter_set, 1)


def diag8(qd):
    v = qd[:]
    return bass.AP(tensor=v.tensor, offset=v.offset,
                   ap=[v.ap[0], [NSEQ * P, 2], [P + DSEQ, NSEQ], [1, DSEQ]])


def stage_merge(nc, K, x, z, gain_row, w_br_m, w_br_f, w_out, T, t0, nt):
    with Stage(nc, f"mrg{t0}") as st:
        wm, wf, wo = (st.sb(n, [P, KD, D]) for n in ("wm", "wf", "wo"))
        gb = st.sb("gb", [P, D])
        yc, yT, gz = st.sb("yc", [P, 2 * D]), st.sb("yT", [P, 2 * KD, P]), st.sb("gz", [P, 2 * D])
        mg, mT, xt, h, xp = (st.sb(n, [P, D]) for n in ("mg", "mT", "xt", "h", "xp"))
        ss, ms, rt, rs = (st.sb(n, [P, 1]) for n in ("ss", "ms", "rt", "rs"))
        t_ps = [st.ps(f"t{n}", [P, 512]) for n in range(2)]
        m_ps, f_ps, o_ps = (st.ps(n, [P, D]) for n in ("m", "f", "o"))
        (w_in, y_in, g_in, x_in, turned, turned_out, branched, gated, merged, projected, h_set, squared,
         meaned, rooted, inverted, xp_set) = st.sems(
            "w_in y_in g_in x_in turned turned_out branched gated merged projected h_set squared "
            "meaned rooted inverted xp_set")
        stored = st.pool_sem("stored")
        block = st.ctx.enter_context(nc.Block())

        @block.sync
        def _(sp):
            for t, w in ((wm, w_br_m), (wf, w_br_f), (wo, w_out)):
                sp.dma_start(t[:], w.rearrange("(k p) n -> p k n", p=P)).then_inc(w_in, 16)
            sp.dma_start(gb[:], gain_row.to_broadcast([P, D])).then_inc(w_in, 16)
            with sp.Fori(0, nt) as i:
                rows = bass.ds(i * P + t0 * P, P)
                sp.wait_ge(turned, i * 6)
                sp.dma_start(yc[:], T["ycat"][rows, :]).then_inc(y_in, 16)
                sp.wait_ge(merged, i * 3)
                sp.dma_start(gz[:], z[rows, C_GM:IN_COLS]).then_inc(g_in, 16)
                sp.wait_ge(h_set, i)
                sp.dma_start(xt[:], x[rows, :]).then_inc(x_in, 16)

        @block.gpsimd
        def _(pool):
            with pool.Fori(0, nt) as i:
                rows = bass.ds(i * P + t0 * P, P)
                pool.wait_ge(h_set, i + 1)
                pool.dma_start(T["h"][rows, :], h[:]).then_inc(stored, 16)
                hold(pool, xp_set, i + 1, K["passed"])
                pool.dma_start(T["xp"][rows, :], xp[:]).then_inc(stored, 16)
            pool.wait_ge(stored, nt * 32)

        @block.tensor
        def _(pe):
            with pe.Fori(0, nt) as i:
                pe.wait_ge(y_in, i * 16 + 16)
                for g in range(4):
                    pe.wait_ge(turned_out, i * 6 + max(g - 1, 0))
                    for c in range(4):
                        mm = pe.transpose(t_ps[g % 2][:, c * P:(c + 1) * P], yc[:, (4 * g + c) * P:(4 * g + c + 1) * P],
                                          K["ident"][:])
                    mm.then_inc(turned, 1)
                pe.wait_ge(w_in, 64)
                for u, (w, acc) in enumerate(((wm, m_ps), (wf, f_ps))):
                    pe.wait_ge(turned_out, i * 6 + 2 * u + 2)
                    for n in range(2):
                        for k in range(KD):
                            mm = pe.matmul(acc[:, n * 512:(n + 1) * 512], yT[:, u * KD + k, :],
                                           w[:, k, n * 512:(n + 1) * 512], start=(k == 0), stop=(k == KD - 1))
                    mm.then_inc(branched, 1)
                pe.wait_ge(merged, i * 3 + 3)
                for g in range(2):
                    for c in range(4):
                        mm = pe.transpose(t_ps[g][:, c * P:(c + 1) * P], mg[:, (4 * g + c) * P:(4 * g + c + 1) * P],
                                          K["ident"][:])
                    mm.then_inc(turned, 1)
                pe.wait_ge(h_set, i)
                pe.wait_ge(turned_out, i * 6 + 6)
                for n in range(2):
                    for k in range(KD):
                        mm = pe.matmul(o_ps[:, n * 512:(n + 1) * 512], mT[:, k * P:(k + 1) * P],
                                       wo[:, k, n * 512:(n + 1) * 512], start=(k == 0), stop=(k == KD - 1))
                mm.then_inc(projected, 1)

        @block.scalar
        def _(act):
            with act.Fori(0, nt) as i:
                for g in range(4):
                    act.wait_ge(turned, i * 6 + g + 1)
                    act.copy(yT[:, 4 * g:4 * g + 4, :].rearrange("p c t -> p (c t)"), t_ps[g % 2][:]
                             ).then_inc(turned_out, 1)
                act.wait_ge(g_in, i * 16 + 16)
                act.activation(gz[:], gz[:], ACT.Sigmoid).then_inc(gated, 1)
                for g in range(2):
                    act.wait_ge(turned, i * 6 + g + 5)
                    act.wait_ge(projected, i)
                    act.copy(mT[:, g * 512:(g + 1) * 512], t_ps[g][:]).then_inc(turned_out, 1)
                act.wait_ge(h_set, i + 1)
                act.wait_ge(stored, i * 32)
                act.activation(xp[:], h[:], ACT.Square, accum_out=ss[:]).then_inc(squared, 1)
                act.wait_ge(meaned, i + 1)
                act.activation(rt[:], ms[:], ACT.Sqrt).then_inc(rooted, 1)

        @block.vector
        def _(dve):
            dve.wait_ge(w_in, 64)
            with dve.Fori(0, nt) as i:
                dve.wait_ge(gated, i + 1)
                dve.wait_ge(turned, i * 6)
                dve.wait_ge(branched, i * 2 + 1)
                dve.tensor_tensor(mg[:], m_ps[:], gz[:, 0:D], ALU.mult).then_inc(merged, 1)
                dve.wait_ge(branched, i * 2 + 2)
                dve.tensor_tensor(gz[:, D:2 * D], f_ps[:], gz[:, D:2 * D], ALU.mult).then_inc(merged, 1)
                dve.wait_ge(merged, i * 3 + 2)
                dve.tensor_tensor(mg[:], mg[:], gz[:, D:2 * D], ALU.add).then_inc(merged, 1)
                dve.wait_ge(projected, i + 1)
                dve.wait_ge(x_in, i * 16 + 16)
                dve.wait_ge(stored, i * 32)
                dve.tensor_tensor(h[:], o_ps[:], xt[:], ALU.add).then_inc(h_set, 1)
                dve.wait_ge(squared, i + 1)
                dve.tensor_scalar(ms[:], ss[:], 1.0 / D, EPS, ALU.mult, ALU.add).then_inc(meaned, 1)
                dve.wait_ge(rooted, i + 1)
                dve.reciprocal(rs[:], rt[:]).then_inc(inverted, 1)
                dve.wait_ge(inverted, i + 1)
                dve.scalar_tensor_tensor(out=xp[:], in0=h[:], scalar=rs[:], in1=gb[:], op0=ALU.mult, op1=ALU.mult
                                         ).then_inc(xp_set, 1)


def stage_queries(nc, K, w_q, keys, idx, gate, T, t0, nt):
    with Stage(nc, f"qry{t0}") as st:
        NB = 2 * PH
        w = st.sb("w", [P, KD, PH * PDQ])
        kT = st.sb("kT", [P, NB, PKEYS])
        xp, xT = st.sb("xp", [P, D]), st.sb("xT", [P, KD, P])
        qT = st.sb("qT", [P, NB, P])
        sc = st.sb("sc", [P, NB, PKEYS])
        left = st.sb("left", [P, NB, PKEYS])
        best, where, wheref = st.sb("best", [P, NB, TOPK]), st.sb("where", [P, NB, TOPK], U32), st.sb(
            "wheref", [P, NB, TOPK])
        cand, cleft = st.sb("cand", [P, PH, TOPK, TOPK]), st.sb("cleft", [P, PH, TOPK, TOPK])
        top, pos = st.sb("top", [P, PH, TOPK]), st.sb("pos", [P, PH, TOPK], U32)
        part = st.sb("part", [P, 2, PH, TOPK], U32)
        partf = st.sb("partf", [P, 2, PH, TOPK])
        picked = st.sb("picked", [P, 2, PH, TOPK])
        flat = st.sb("flat", [P, EXPERTS])
        ramp_i, ramp = st.sb("ramp_i", [P, TOPK], mybir.dt.int32), st.sb("ramp", [P, TOPK])
        ex, tot, itot = st.sb("ex", [P, PH, TOPK]), st.sb("tot", [P, PH]), st.sb("itot", [P, PH])
        t_ps = [st.ps(f"t{n}", [P, 512]) for n in range(2)]
        q_ps = [st.ps(f"q{n}", [P, 512]) for n in range(2)]
        s_ps = st.ps("s", [P, NB * PKEYS])
        (w_in, ramp_set, x_in, turned, turned_out, queried, q_out, scored, s_out, chain, shifted, expd) = st.sems(
            "w_in ramp_set x_in turned turned_out queried q_out scored s_out chain shifted expd")
        STEPS = 17
        block = st.ctx.enter_context(nc.Block())

        @block.sync
        def _(sp):
            sp.dma_start(w[:], w_q.rearrange("(k p) n -> p k n", p=P)).then_inc(w_in, 16)
            sp.dma_start(kT[:], keys).then_inc(w_in, 16)
            with sp.Fori(0, nt) as i:
                sp.wait_ge(turned, i * 2)
                sp.dma_start(xp[:], T["xp"][bass.ds(i * P + t0 * P, P), :]).then_inc(x_in, 16)

        @block.gpsimd
        def _(pool):
            pool.iota(ramp_i[:], pattern=[[1, TOPK]], base=0, channel_multiplier=0).then_inc(ramp_set, 1)

        @block.tensor
        def _(pe):
            pe.wait_ge(w_in, 32)
            with pe.Fori(0, nt) as i:
                pe.wait_ge(x_in, i * 16 + 16)
                pe.wait_ge(turned_out, i * 2)
                for g in range(2):
                    for c in range(4):
                        mm = pe.transpose(t_ps[g][:, c * P:(c + 1) * P], xp[:, (4 * g + c) * P:(4 * g + c + 1) * P],
                                          K["ident"][:])
                    mm.then_inc(turned, 1)
                pe.wait_ge(turned_out, i * 2 + 2)
                for g in range(4):
                    pe.wait_ge(q_out, i * 4 + max(g - 1, 0))
                    for c in range(4):
                        for k in range(KD):
                            mm = pe.matmul(q_ps[g % 2][:, c * P:(c + 1) * P], w[:, k, (4 * g + c) * P:(4 * g + c + 1) * P],
                                           xT[:, k, :], start=(k == 0), stop=(k == KD - 1))
                    mm.then_inc(queried, 1)
                pe.wait_ge(q_out, i * 4 + 4)
                pe.wait_ge(s_out, i)
                for c in range(NB):
                    mm = pe.matmul(s_ps[:, c * PKEYS:(c + 1) * PKEYS], qT[:, c, :], kT[:, c, :], start=True, stop=True)
                mm.then_inc(scored, 1)

        @block.scalar
        def _(act):
            def queries(i):
                for g in range(2):
                    act.wait_ge(turned, i * 2 + g + 1)
                    act.wait_ge(queried, i * 4)
                    act.copy(xT[:, 4 * g:4 * g + 4, :].rearrange("p c t -> p (c t)"), t_ps[g][:]
                             ).then_inc(turned_out, 1)
                for g in range(4):
                    act.wait_ge(queried, i * 4 + g + 1)
                    act.wait_ge(scored, i)
                    act.copy(qT[:, 4 * g:4 * g + 4, :].rearrange("p c t -> p (c t)"), q_ps[g % 2][:]
                             ).then_inc(q_out, 1)
                act.wait_ge(scored, i + 1)

            def weights(i):
                act.wait_ge(shifted, i + 1)
                act.activation(ex[:], ex[:], ACT.Exp).then_inc(expd, 1)

            queries(0)
            act.copy(sc[:].rearrange("p b k -> p (b k)"), s_ps[:]).then_inc(s_out, 1)
            with act.Fori(0, nt - 1) as i:
                queries(i + 1)
                weights(i)
                act.wait_ge(chain, i * STEPS + 4)
                act.copy(sc[:].rearrange("p b k -> p (b k)"), s_ps[:]).then_inc(s_out, 1)
            weights(nt - 1)

        @block.vector
        def _(dve):
            dve.wait_ge(ramp_set, 1)
            dve.tensor_copy(ramp[:], ramp_i[:]).then_inc(ramp_set, 1)
            if t0 == 0:
                dve.memset(idx[:, NT * EXPERTS:], 0).then_inc(ramp_set, 1)
            dve.wait_ge(ramp_set, 3 if t0 == 0 else 2)
            with dve.Fori(0, nt) as i:
                ch = Chain(dve, chain, i, STEPS, K["passed"])
                hold(dve, s_out, i + 1, K["passed"])

                def top16(values, rest, out, at, blocks):
                    for c in range(blocks):
                        ins = dve.max(out=out[:, c, 0:8], in_=values(c))
                    ch(ins)
                    for c in range(blocks):
                        dve.max_index(out=at[:, c, 0:8], in_max=out[:, c, 0:8], in_values=values(c))
                        ins = dve.match_replace(out=rest(c), in_to_replace=out[:, c, 0:8], in_values=values(c),
                                                imm_value=-3.0e38)
                    ch(ins)
                    for c in range(blocks):
                        ins = dve.max(out=out[:, c, 8:16], in_=rest(c))
                    ch(ins)
                    for c in range(blocks):
                        ins = dve.max_index(out=at[:, c, 8:16], in_max=out[:, c, 8:16], in_values=rest(c))
                    ch(ins)

                top16(lambda c: sc[:, c, :], lambda c: left[:, c, :], best, where, NB)
                dve.tensor_copy(wheref[:], where[:])
                b4 = best[:].rearrange("p (h s) k -> p h s k", s=2)
                ch(dve.tensor_tensor(cand[:], b4[:, :, 0, :].unsqueeze(3).to_broadcast([P, PH, TOPK, TOPK]),
                                     b4[:, :, 1, :].unsqueeze(2).to_broadcast([P, PH, TOPK, TOPK]), ALU.add))
                as_row = lambda t: (lambda c: t[:, c].rearrange("p a b -> p (a b)"))
                top16(as_row(cand), as_row(cleft), top, pos, PH)
                dve.tensor_tensor(ex[:], top[:], bc(top[:, :, 0], [P, PH, TOPK]), ALU.subtract).then_inc(shifted, 1)
                dve.tensor_scalar(part[:, 0], pos[:], 4, None, ALU.logical_shift_right)
                ch(dve.tensor_scalar(part[:, 1], pos[:], TOPK - 1, None, ALU.bitwise_and))
                ch(dve.tensor_copy(partf[:], part[:]))
                w4 = wheref[:].rearrange("p (h s) k -> p h s k", s=2)
                for s, buf in enumerate((cand, cleft)):
                    dve.tensor_tensor(buf[:].rearrange("p h a b -> p (h a) b"),
                                      ramp[:].unsqueeze(1).to_broadcast([P, EXPERTS, TOPK]),
                                      bc(partf[:, s].rearrange("p h k -> p (h k)"), [P, EXPERTS, TOPK]), ALU.is_equal
                                      ).then_inc(chain, 1)
                ch.n += 2
                dve.wait_ge(chain, i * STEPS + ch.n)
                for s, buf in enumerate((cand, cleft)):
                    ins = dve.tensor_tensor(buf[:], buf[:], w4[:, :, s, :].unsqueeze(2).to_broadcast(
                        [P, PH, TOPK, TOPK]), ALU.mult)
                ch(ins)
                for s, buf in enumerate((cand, cleft)):
                    ins = dve.tensor_reduce(picked[:, s], buf[:], AX.X, ALU.add)
                dve.wait_ge(expd, i + 1)
                ins = dve.tensor_reduce(tot[:], ex[:], AX.X, ALU.add)
                ch(ins)
                dve.scalar_tensor_tensor(out=flat[:], in0=picked[:, 0].rearrange("p h k -> p (h k)"),
                                         scalar=float(PKEYS), in1=picked[:, 1].rearrange("p h k -> p (h k)"),
                                         op0=ALU.mult, op1=ALU.add)
                ch(dve.reciprocal(itot[:], tot[:]))
                dve.tensor_copy(idx[:, bass.ds(i * EXPERTS + t0 * EXPERTS, EXPERTS)], flat[:])
                dve.tensor_tensor(gate[:, bass.ds(i * EXPERTS + t0 * EXPERTS, EXPERTS)].rearrange("p (h k) -> p h k", h=PH), ex[:],
                                  bc(itot[:], [P, PH, TOPK]), ALU.mult).then_inc(chain, 1)
                ch.n += 1
                dve.wait_ge(chain, i * STEPS + ch.n)
                ch.close()


class Experts:

    G = 4
    PER_TILE = EXPERTS // G

    def __init__(self, nc, K, ctx, tile0, idx, gate, u_tab, v_tab, T):
        def sb(name, shape, dt=F32):
            return ctx.enter_context(nc.sbuf_tensor(f"ex{tile0}_{name}", shape, dt))

        G = self.G
        self.K, self.idx, self.gate, self.u_tab, self.v_tab, self.T = K, idx, gate, u_tab, v_tab, T
        self.u, self.v = sb("u", [P, 2 * G, D]), sb("v", [P, G, D])
        self.x_next, self.h_next, self.xp = sb("x_next", [P, D]), sb("h_next", [P, D]), sb("xp", [P, D])
        self.acc, self.sum = sb("acc", [P, 2, D]), sb("sum", [P, D])
        self.here = sb("here", [P, 4, G], U32)
        self.dot, self.act, self.wt = sb("dot", [P, 2, G]), sb("act", [P, 2, G]), sb("wt", [P, 2, G])
        self.u_in = [ctx.enter_context(nc.semaphore(f"ex{tile0}_u_in{j}")) for j in range(2 * G)]
        self.v_in = [ctx.enter_context(nc.semaphore(f"ex{tile0}_v_in{j}")) for j in range(G)]
        self.u_base, self.v_base, self.first, self.tile0, self.nt = 0, 0, tile0, tile0, 0

    def begin(self, st, NI, nt=1, last=False):
        self.u_base += self.nt * self.PER_TILE // 2 * 16
        self.v_base += self.nt * self.PER_TILE * 16
        self.tile0 += self.nt
        self.nt, self.NI, self.GPI, self.last = nt, NI, self.PER_TILE // NI, last
        (self.opened, self.dotted, self.added, self.indexed, self.geluted, self.weighed, self.xp_set, self.acc_set,
         self.zeroed, self.joined, self.x_in, self.h_in, self.stored) = st.sems(
            "ex_opened ex_dotted ex_added ex_indexed ex_geluted ex_weighed ex_xp_set ex_acc_set "
            "ex_zeroed ex_joined ex_x_in ex_h_in ex_stored")

    def group(self, t, i, p):
        return t * self.PER_TILE + i * self.GPI + p


    def fetch_u(self, pool, slot, at, j):
        pool.indirect_dma_start(self.u[:, slot * self.G + j, :], None, self.u_tab, bass.IndirectOffsetOnAxis(
            ap=self.here[:, at, j:j + 1], axis=0)).then_inc(self.u_in[slot * self.G + j], 16)

    def pool_all(self, pool):
        G, passed = self.G, self.K["passed"]
        if self.tile0 == self.first:
            at = self.tile0 * EXPERTS
            pool.tensor_copy(self.here[:, 0, :], self.idx[:, at:at + G]).then_inc(self.opened, 1)
            pool.wait_ge(self.opened, 1)
            for j in range(G):
                self.fetch_u(pool, 0, 0, j)
        with pool.Fori(0, self.nt) as t:
            with pool.Fori(0, self.NI) as i:
                for p in range(self.GPI):
                    n = self.group(t, i, p)
                    pool.tensor_copy(self.here[:, (p + 1) % 4, :],
                                     self.idx[:, bass.ds(n * G + (self.tile0 * EXPERTS + G), G)]
                                     ).then_inc(self.indexed, 1)
                    for j in range(G):
                        hold(pool, self.added, n * G + (j + 1), passed)
                        pool.indirect_dma_start(self.v[:, j, :], None, self.v_tab, bass.IndirectOffsetOnAxis(
                            ap=self.here[:, p % 4, j:j + 1], axis=0)).then_inc(self.v_in[j], 16)
                        if j == 0:
                            hold(pool, self.indexed, n + 1, passed)
                        hold(pool, self.dotted, n * G + (j + 1), passed)
                        self.fetch_u(pool, (p + 1) % 2, (p + 1) % 4, j)
        if self.last:
            for j in range(G):
                pool.wait_ge(self.u_in[j], self.u_base + self.nt * self.PER_TILE // 2 * 16 + 16)


    def dve_tile(self, dve, t):
        if isinstance(t, int):
            dve.sem_inc(self.dotted, self.G)
            dve.sem_inc(self.added, self.G)
        else:
            dve.wait_ge(self.joined, t)
        dve.memset(self.acc[:, 1, :], 0.0).then_inc(self.zeroed, 1)
        hold(dve, self.zeroed, t + 1, self.K["passed"])
        hold(dve, self.xp_set, t + 1, self.K["passed"])
        hold(dve, self.acc_set, t + 1, self.K["passed"])

    def dve_units(self, dve, i, p, units, t=0):
        G = self.G
        n = self.group(t, i, p)
        pair = t * (self.PER_TILE // 2) + i * (self.GPI // 2) + p // 2
        for unit in range(*units):
            if unit < G:
                j = unit
                slot = p % 2 * G + j
                dve.wait_ge(self.u_in[slot], pair * 16 + (16 + self.u_base))
                dve.tensor_tensor_reduce(self.u[:, slot, :], self.u[:, slot, :], self.xp[:], 1.0, 0.0, ALU.mult,
                                         ALU.add, self.dot[:, p % 2, j:j + 1]).then_inc(self.dotted, 1)
            elif unit == G:
                dve.wait_ge(self.geluted, n + 1)
                dve.tensor_tensor(self.wt[:, p % 2, :], self.act[:, p % 2, :],
                                  self.gate[:, bass.ds(n * G + self.tile0 * EXPERTS, G)], ALU.mult
                                  ).then_inc(self.weighed, 1)
            else:
                j = unit - G - 1
                if j == 0:
                    dve.wait_ge(self.weighed, n + 1)
                dve.wait_ge(self.v_in[j], n * 16 + (16 + self.v_base))
                dve.wait_ge(self.added, n * G + (j + G - 1))
                dve.scalar_tensor_tensor(out=self.acc[:, j % 2, :], in0=self.v[:, j, :],
                                         scalar=self.wt[:, p % 2, j:j + 1], in1=self.acc[:, j % 2, :],
                                         op0=ALU.mult, op1=ALU.add).then_inc(self.added, 1)

    def dve_end(self, dve, t):
        dve.wait_ge(self.added, t * EXPERTS + (EXPERTS + self.G))
        if not isinstance(t, int):
            dve.wait_ge(self.stored, t * 16)
        dve.tensor_tensor(self.sum[:], self.acc[:, 0, :], self.acc[:, 1, :], ALU.add).then_inc(self.joined, 1)

    def dve_all(self, dve):
        self.dve_tile(dve, 0)
        with dve.Fori(0, self.NI) as i:
            for p in range(self.GPI):
                self.dve_units(dve, i, p, (0, 2 * self.G + 1))
        self.dve_end(dve, 0)


    def act_tile(self, act, t):
        act.wait_ge(self.x_in, t * 16 + 16)
        act.wait_ge(self.dotted, t * EXPERTS + self.G)
        act.copy(self.xp[:], self.x_next[:]).then_inc(self.xp_set, 1)
        act.wait_ge(self.h_in, t * 16 + 16)
        if not isinstance(t, int):
            act.wait_ge(self.joined, t)
        act.copy(self.acc[:, 0, :], self.h_next[:]).then_inc(self.acc_set, 1)

    def act_group(self, act, i, p, t=0):
        n = self.group(t, i, p)
        act.wait_ge(self.dotted, n * self.G + 2 * self.G)
        act.wait_ge(self.weighed, n)
        act.activation(self.act[:, p % 2, :], self.dot[:, p % 2, :], ACT.Gelu).then_inc(self.geluted, 1)


    def rows(self, t):
        return bass.ds(t * P + self.tile0 * P, P)

    def load(self, sp, t):
        sp.dma_start(self.x_next[:], self.T["xp"][self.rows(t), :]).then_inc(self.x_in, 16)
        sp.dma_start(self.h_next[:], self.T["h"][self.rows(t), :]).then_inc(self.h_in, 16)

    def store(self, sp, t):
        sp.wait_ge(self.joined, t + 1)
        sp.dma_start(self.T["h2"][self.rows(t), :], self.sum[:]).then_inc(self.stored, 16)

    def stored_all(self, sp):
        sp.wait_ge(self.stored, self.nt * 16)


def stage_experts(nc, K, ex, nt):
    with Stage(nc, f"exp{ex.tile0 + ex.nt}") as st:
        NI = 8
        ex.begin(st, NI, nt, last=True)
        block = st.ctx.enter_context(nc.Block())

        @block.sync
        def _(sp):
            ex.load(sp, 0)
            with sp.Fori(0, nt - 1) as t:
                sp.wait_ge(ex.xp_set, t + 1)
                sp.wait_ge(ex.acc_set, t + 1)
                ex.load(sp, t + 1)
                ex.store(sp, t)
            ex.store(sp, nt - 1)
            ex.stored_all(sp)

        @block.gpsimd
        def _(pool):
            ex.pool_all(pool)

        @block.vector
        def _(dve):
            dve.sem_inc(ex.dotted, ex.G)
            dve.sem_inc(ex.added, ex.G)
            with dve.Fori(0, nt) as t:
                ex.dve_tile(dve, t)
                with dve.Fori(0, NI) as i:
                    for p in range(ex.GPI):
                        ex.dve_units(dve, i, p, (0, 2 * ex.G + 1), t)
                ex.dve_end(dve, t)

        @block.scalar
        def _(act):
            with act.Fori(0, nt) as t:
                ex.act_tile(act, t)
                with act.Fori(0, NI) as i:
                    for p in range(ex.GPI):
                        ex.act_group(act, i, p, t)


def stage_ple(nc, K, g_cols, w_gate, w_proj, gain_row, pT, T, t0, nt):
    with Stage(nc, f"ple{t0}") as st:
        wg, wp = st.sb("wg", [P, KD, D]), st.sb("wp", [P, 2, D])
        gc, gb = st.sb("gc", [P, KD]), st.sb("gb", [P, D])
        h, sq, en, eT, pt = st.sb("h", [P, D]), st.sb("sq", [P, D]), st.sb("en", [P, D]), st.sb(
            "eT", [P, KD, P]), st.sb("pt", [P, 2, P])
        sg, h3, y = st.sb("sg", [P, D]), st.sb("h3", [P, D]), st.sb("y", [P, D])
        ss, ms, rt, rs = (st.sb(n, [P, 2]) for n in ("ss", "ms", "rt", "rs"))
        t_ps, g_ps, p_ps = (st.ps(n, [P, D]) for n in ("t", "g", "p"))
        (w_in, h_in, p_in, squared, meaned, rooted, inverted, normed, turned, turned_out, gated, projected, sig_set,
         scaled, h3_set, y_set) = st.sems(
            "w_in h_in p_in squared meaned rooted inverted normed turned turned_out gated projected sig_set "
            "scaled h3_set y_set")
        stored = st.pool_sem("stored")
        block = st.ctx.enter_context(nc.Block())

        @block.sync
        def _(sp):
            sp.dma_start(gc[:], g_cols).then_inc(w_in, 16)
            sp.dma_start(wg[:], w_gate.rearrange("(k p) n -> p k n", p=P)).then_inc(w_in, 16)
            sp.dma_start(wp[:], w_proj.rearrange("(k p) n -> p k n", p=P)).then_inc(w_in, 16)
            sp.dma_start(gb[:], gain_row.to_broadcast([P, D])).then_inc(w_in, 16)
            with sp.Fori(0, nt) as i:
                sp.wait_ge(h3_set, i)
                sp.dma_start(h[:], T["h2"][bass.ds(i * P + t0 * P, P), :]).then_inc(h_in, 16)
                hold(sp, projected, i, K["passed"])
                sp.dma_start(pt[:], pT.rearrange("(k p) t -> p k t", p=P)[:, :, bass.ds(i * P + t0 * P, P)]).then_inc(p_in, 16)

        @block.gpsimd
        def _(pool):
            with pool.Fori(0, nt) as i:
                pool.wait_ge(y_set, i + 1)
                pool.dma_start(T["y"][bass.ds(i * P + t0 * P, P), :], y[:]).then_inc(stored, 16)
            pool.wait_ge(stored, nt * 16)

        @block.scalar
        def _(act):
            with act.Fori(0, nt) as i:
                act.wait_ge(h_in, i * 16 + 16)
                act.activation(sq[:], h[:], ACT.Square, accum_out=ss[:, 0:1]).then_inc(squared, 1)
                act.wait_ge(meaned, i * 2 + 1)
                act.activation(rt[:, 0:1], ms[:, 0:1], ACT.Sqrt).then_inc(rooted, 1)
                act.wait_ge(inverted, i * 2 + 1)
                act.wait_ge(turned, i)
                act.activation(en[:], h[:], ACT.Copy, scale=rs[:, 0:1]).then_inc(normed, 1)
                act.wait_ge(gated, i + 1)
                act.wait_ge(scaled, i)
                act.activation(sg[:], g_ps[:], ACT.Sigmoid).then_inc(sig_set, 1)
                act.wait_ge(h3_set, i + 1)
                act.activation(sq[:], h3[:], ACT.Square, accum_out=ss[:, 1:2]).then_inc(squared, 1)
                act.wait_ge(meaned, i * 2 + 2)
                act.activation(rt[:, 1:2], ms[:, 1:2], ACT.Sqrt).then_inc(rooted, 1)

        @block.tensor
        def _(pe):
            with pe.Fori(0, nt) as i:
                pe.wait_ge(normed, i + 1)
                pe.wait_ge(turned_out, i)
                for k in range(KD):
                    mm = pe.transpose(t_ps[:, k * P:(k + 1) * P], en[:, k * P:(k + 1) * P], K["ident"][:])
                mm.then_inc(turned, 1)
                pe.wait_ge(w_in, 64)
                pe.wait_ge(p_in, i * 16 + 16)
                pe.wait_ge(scaled, i)
                for n in range(2):
                    for k in range(2):
                        mm = pe.matmul(p_ps[:, n * 512:(n + 1) * 512], pt[:, k, :], wp[:, k, n * 512:(n + 1) * 512],
                                       start=(k == 0), stop=(k == 1))
                mm.then_inc(projected, 1)
                pe.wait_ge(turned_out, i + 1)
                pe.wait_ge(sig_set, i)
                for n in range(2):
                    for k in range(KD):
                        mm = pe.matmul(g_ps[:, n * 512:(n + 1) * 512], eT[:, k, :], wg[:, k, n * 512:(n + 1) * 512],
                                       start=(k == 0), stop=(k == KD - 1))
                mm.then_inc(gated, 1)

        @block.vector
        def _(dve):
            dve.wait_ge(w_in, 64)
            with dve.Fori(0, nt) as i:
                def invert(c):
                    dve.wait_ge(squared, i * 2 + c + 1)
                    dve.tensor_scalar(ms[:, c:c + 1], ss[:, c:c + 1], 1.0 / D, EPS, ALU.mult, ALU.add
                                      ).then_inc(meaned, 1)
                    dve.wait_ge(rooted, i * 2 + c + 1)
                    dve.reciprocal(rs[:, c:c + 1], rt[:, c:c + 1]).then_inc(inverted, 1)

                invert(0)
                dve.wait_ge(turned, i + 1)
                dve.tensor_tensor(eT[:], t_ps[:].rearrange("p (k t) -> p k t", k=KD), bc(gc[:], [P, KD, P]), ALU.mult
                                  ).then_inc(turned_out, 1)
                dve.wait_ge(sig_set, i + 1)
                dve.wait_ge(projected, i + 1)
                dve.tensor_tensor(sg[:], sg[:], p_ps[:], ALU.mult).then_inc(scaled, 1)
                dve.wait_ge(scaled, i + 1)
                dve.tensor_tensor(h3[:], h[:], sg[:], ALU.add).then_inc(h3_set, 1)
                invert(1)
                dve.wait_ge(inverted, i * 2 + 2)
                dve.wait_ge(stored, i * 16)
                dve.scalar_tensor_tensor(out=y[:], in0=h3[:], scalar=rs[:, 1:2], in1=gb[:], op0=ALU.mult, op1=ALU.mult
                                         ).then_inc(y_set, 1)


def trunk_kernel(nc, A, O):
    scratch = lambda name, shape: nc.dram_tensor(f"scratch_{name}", shape, F32, kind="Internal").ap()
    z = scratch("z", (TOK, IN_COLS))
    T = dict(O)
    T.update(
        lfT=scratch("lfT", (H_F, P)),
        nck=scratch("nck", (H_F, SEQ)),
        ncs=scratch("ncs", (NSEQ, H_F, PAST + DSEQ)),
        ycat=scratch("ycat", (TOK, W_M + W_F)),
        h=scratch("h", (TOK, D)),
        xp=scratch("xp", (TOK, D)),
        h2=scratch("h2", (TOK, D)),
        cache_kT=A["cache_kT"], cache_v=A["cache_v"], C0=A["C0"], n0=A["n0"], m0=A["m0"],
    )
    with ExitStack() as ctx:
        def sb(name, shape, dt=F32):
            return ctx.enter_context(nc.sbuf_tensor(name, shape, dt))

        K = {n: sb(n, [P, P]) for n in ("ident", "ones", "negones", "mask", "maskT", "tri", "bmask", "bmaskT", "btri",
                                        "last", "blast")}
        K["pick"], K["inblock"] = sb("pick", [P, NSEQ]), sb("inblock", [P, NSEQ])
        K["headsel"] = sb("headsel", [H_F, 2, 8, DSEQ])
        K["masknew"] = sb("masknew", [P, DSEQ])
        K["onesrow"] = sb("onesrow", [1, P])
        K["passed"] = ctx.enter_context(nc.semaphore("passed"))
        gates = sb("gates", [P, NT, NG])
        ck_last = sb("ck_last", [H_F, 1])
        C, m = sb("C", [P, 2 * H_M, DM + 1]), sb("m", [P, H_M])
        idx, gate = sb("idx", [P, NT * EXPERTS + Experts.G], U32), sb("gate", [P, NT * EXPERTS])

        def route(t0, nt):
            stage_merge(nc, K, A["x"], z, A["norm_ffn"], A["w_br_m"], A["w_br_f"], A["w_out"], T, t0, nt)
            stage_queries(nc, K, A["w_q"], A["keys"], idx, gate, T, t0, nt)

        stage_constants(nc, K)
        aT_later = sb("aT_later", [P, KD, (NT - FIRST) * P])
        stage_norm(nc, K, A["x"], A["norm_mix"], aT_later, FIRST, NT - FIRST)
        with nc.sbuf_tensor("aT", [P, KD, FIRST * P], F32) as aT:
            stage_norm(nc, K, A["x"], A["norm_mix"], aT, 0, FIRST)
            stage_project(nc, aT, A["w_in"], z, 0, FIRST)
        stage_gates(nc, K, z, A["gate_bias"], A["cache_lf"], gates, ck_last, T, 0, FIRST)
        stage_fox_prompt(nc, K, z, T, 0, FIRST - 1)
        stage_fox_sample(nc, K, z, T)
        stage_mlstm_prompt(nc, K, z, gates, C, m, T, 0, FIRST - 1)
        stage_mlstm_sample(nc, K, z, gates, T)
        route(0, FIRST)
        with ExitStack() as rings:
            ex = Experts(nc, K, rings, 0, idx, gate, A["u"], A["v"], T)
            stage_project(nc, aT_later, A["w_in"], z, FIRST, NT - FIRST, ex)
            stage_gates(nc, K, z, A["gate_bias"], A["cache_lf"], gates, ck_last, T, FIRST, NT - FIRST)
            stage_fox_prompt(nc, K, z, T, FIRST - 1, PT, ex)
            stage_mlstm_prompt(nc, K, z, gates, C, m, T, FIRST - 1, PT, ex)
        route(FIRST, NT - FIRST)
        with ExitStack() as rings:
            ex = Experts(nc, K, rings, 3, idx, gate, A["u"], A["v"], T)
            stage_experts(nc, K, ex, NT - 3)
        stage_ple(nc, K, A["norm_ple"], A["w_ple_gate"], A["w_ple_proj"], A["norm_final"], A["pT"], T, 0, NT)


_OUTS = dict(y=(TOK, D), fox_k=(TOK, W_F), fox_v=(TOK, W_F), fox_lf=(TOK, H_F),
             mC_p=(H_M, DM, DM), mn_p=(P, 2 * H_M), mm_p=(1, H_M),
             mC_s=(NSEQ, H_M, DM, DM), mn_s=(P, NSEQ * H_M * 2), mm_s=(NSEQ, H_M))


def kernel(**inputs):
    import numpy as np
    import concourse.bacc as bacc
    from concourse.bass_utils import run_bass_kernel_spmd

    I = {k: np.asarray(v) for k, v in inputs.items()}
    c = np.ascontiguousarray
    cols = lambda v: c(v.reshape(KD, P).T)
    laid = dict(
        x=np.concatenate([I["x_sample"].reshape(-1, D), I["x_prompt"].reshape(SEQ, D)]),
        pT=c(np.concatenate([I["p_sample"].reshape(NSEQ * DSEQ, -1), I["p_prompt"].reshape(SEQ, -1)]).T),
        norm_mix=cols(I["norm_mix"]), w_in=I["w_in"][0],
        gate_bias=np.concatenate([I["mlstm_b_i"], I["mlstm_b_f"], I["fox_b_f"]], axis=1),
        cache_lf=c(I["cache_fox_logf"][0].transpose(0, 2, 1).reshape(NSEQ * H_F, PAST)),
        cache_kT=c(I["cache_fox_k"][0].transpose(0, 2, 3, 1).reshape(NSEQ, W_F, PAST)),
        cache_v=I["cache_fox_v"][0].reshape(NSEQ, PAST, W_F),
        C0=I["state_mlstm_C"][0], m0=I["state_mlstm_m"][0],
        n0=c(I["state_mlstm_n"][0].reshape(NSEQ, H_M, 2, P).transpose(3, 0, 1, 2).reshape(P, -1)),
        w_br_m=I["w_br_m"][0], w_br_f=I["w_br_f"][0], w_out=I["w_out"][0],
        norm_ffn=I["norm_ffn"], w_q=I["peer_w_q"][0],
        keys=c(np.stack([I["peer_keys1"][0], I["peer_keys2"][0]], axis=1).reshape(2 * PH, PKEYS, P).transpose(2, 0, 1)),
        u=I["peer_u"][0], v=I["peer_v"][0],
        norm_ple=cols(I["norm_ple"]), w_ple_gate=I["w_ple_gate"][0], w_ple_proj=I["w_ple_proj"][0],
        norm_final=I["norm_final"].reshape(1, D),
    )
    nc = bacc.Bacc("TRN2", target_bir_lowering=False, num_devices=1)
    arrays, A, O = {}, {}, {}
    for name, a in laid.items():
        a = c(a)
        arrays[f"in_{name}"] = a
        A[name] = nc.dram_tensor(f"in_{name}", a.shape, mybir.dt.from_np(a.dtype), kind="ExternalInput").ap()
    for name, shape in _OUTS.items():
        O[name] = nc.dram_tensor(f"out_{name}", shape, F32, kind="ExternalOutput").ap()
    trunk_kernel(nc, A, O)
    r = run_bass_kernel_spmd(nc, [arrays], core_ids=[0])
    g = {name: np.asarray(r.results[0][f"out_{name}"]) for name in _OUTS}

    def both(a, *tail):
        return a[P:].reshape(1, 1, SEQ, *tail), a[:P].reshape(1, NSEQ, DSEQ, *tail)

    y_p, y_s = both(g["y"], D)
    k_p, k_s = both(g["fox_k"], H_F, DF)
    v_p, v_s = both(g["fox_v"], H_F, DF)
    l_p, l_s = both(g["fox_lf"], H_F)
    n_p = c(g["mn_p"].reshape(P, H_M, 2).transpose(1, 2, 0)).reshape(1, 1, H_M, DM)
    n_s = c(g["mn_s"].reshape(P, NSEQ, H_M, 2).transpose(1, 2, 3, 0)).reshape(1, NSEQ, H_M, DM)
    return (y_p[0], y_s[0], k_p, v_p, l_p, g["mC_p"].reshape(1, 1, H_M, DM, DM), n_p, g["mm_p"].reshape(1, 1, H_M),
            k_s, v_s, l_s, g["mC_s"].reshape(1, NSEQ, H_M, DM, DM), n_s, g["mm_s"].reshape(1, NSEQ, H_M))
```
